# Optimizing a Trainium2 kernel written in Bass

```python
import math
import jax, jax.numpy as jnp
from jax import lax
import numpy as np

D_MODEL = 1024
BATCH = 1
SEQ = 512
DEPTH = 2

CHUNK = 64
Q_BLOCK = 128
HEAD_DIM = 64
N_HEADS_TOTAL = D_MODEL // HEAD_DIM
N_HEADS_B = N_HEADS_TOTAL // 4
N_HEADS_A = (N_HEADS_TOTAL - N_HEADS_B) // 2
N_HEADS_C = N_HEADS_TOTAL - N_HEADS_A - N_HEADS_B
DIFF_QK_DIM = HEAD_DIM // 2
DIFF_V_DIM = HEAD_DIM
WIDTH_A = N_HEADS_A * HEAD_DIM
WIDTH_B = N_HEADS_B * DIFF_V_DIM
WIDTH_C = N_HEADS_C * HEAD_DIM
B_QK_WIDTH = N_HEADS_B * 2 * DIFF_QK_DIM
D_MIX = WIDTH_A + WIDTH_B + WIDTH_C
IN_COLS = 3 * WIDTH_A + 2 * B_QK_WIDTH + WIDTH_B + 3 * WIDTH_C
LEFT_CHUNKS = 8
BAND = (LEFT_CHUNKS + 1) * CHUNK
REL_CLIP = 128
D_FF = 2816
NORM_EPS = 1e-6
NEG_INF = -1e30
FFN_RESIDUAL_WEIGHT = 0.5


def rmsnorm(x, g):
    xf = x.astype(jnp.float32)
    y = xf * lax.rsqrt(jnp.mean(xf * xf, axis=-1, keepdims=True) + NORM_EPS)
    return (y * g.astype(jnp.float32)).astype(x.dtype)

def swiglu(x, w_gate, w_up, w_down):
    return (jax.nn.silu(x @ w_gate) * (x @ w_up)) @ w_down

def chunk_band_attention(q, k, v, rel_bias):
    b, s, h, d = q.shape
    nc = s // CHUNK
    qc = q.reshape(b, nc, CHUNK, h, d)
    pad = ((0, 0), (LEFT_CHUNKS, 0), (0, 0), (0, 0), (0, 0))
    kp = jnp.pad(k.reshape(b, nc, CHUNK, h, d), pad)
    vp = jnp.pad(v.reshape(b, nc, CHUNK, h, d), pad)
    kband = jnp.concatenate([kp[:, w:w + nc] for w in range(LEFT_CHUNKS + 1)], axis=2)
    vband = jnp.concatenate([vp[:, w:w + nc] for w in range(LEFT_CHUNKS + 1)], axis=2)
    qi = jnp.arange(CHUNK)
    kk = jnp.arange(BAND)
    rel = jnp.clip(qi[:, None] + LEFT_CHUNKS * CHUNK - kk[None, :], -REL_CLIP, REL_CLIP) + REL_CLIP
    bias = rel_bias[:, rel].astype(jnp.float32)
    valid = (jnp.arange(nc)[:, None] - LEFT_CHUNKS + kk[None, :] // CHUNK) >= 0
    scores = jnp.einsum('bnqhd,bnkhd->bnhqk', qc, kband).astype(jnp.float32) * (d ** -0.5)
    scores = scores + bias[None, None]
    scores = jnp.where(valid[None, :, None, None, :], scores, NEG_INF)
    p = jax.nn.softmax(scores, axis=-1).astype(v.dtype)
    o = jnp.einsum('bnhqk,bnkhd->bnqhd', p, vband)
    return o.reshape(b, s, h, d)

def diff_attention(q, k, v, lam, subln_g, lambda_init):
    b, s, h, _, dq = q.shape
    scale = dq ** -0.5
    slopes = jnp.exp2(-8.0 * jnp.arange(1, h + 1, dtype=jnp.float32) / h)
    outs = []
    for blk in range(s // Q_BLOCK):
        q0 = blk * Q_BLOCK
        kend = q0 + Q_BLOCK
        tpos = q0 + jnp.arange(Q_BLOCK)
        spos = jnp.arange(kend)
        allowed = (spos[None, :] // CHUNK) <= (tpos[:, None] // CHUNK)
        dist = jnp.abs(tpos[:, None] - spos[None, :]).astype(jnp.float32)
        alibi = -slopes[:, None, None] * dist[None]
        sc = jnp.einsum('bqhmd,bkhmd->bhmqk', q[:, q0:kend], k[:, :kend]).astype(jnp.float32) * scale
        sc = sc + alibi[None, :, None]
        sc = jnp.where(allowed[None, None, None], sc, NEG_INF)
        p = jax.nn.softmax(sc, axis=-1)
        w = p[:, :, 0] - lam * p[:, :, 1]
        outs.append(jnp.einsum('bhqk,bkhd->bqhd', w.astype(v.dtype), v[:, :kend]))
    o = jnp.concatenate(outs, axis=1)
    return rmsnorm(o, subln_g) * (1.0 - lambda_init)

def stick_breaking_attention(q, k, v):
    b, s, h, d = q.shape
    scale = d ** -0.5
    outs = []
    for blk in range(s // Q_BLOCK):
        q0 = blk * Q_BLOCK
        kend = q0 + Q_BLOCK
        tpos = q0 + jnp.arange(Q_BLOCK)
        spos = jnp.arange(kend)
        strict = spos[None, :] < tpos[:, None]
        z = jnp.einsum('bqhd,bkhd->bhqk', q[:, q0:kend], k[:, :kend]).astype(jnp.float32) * scale
        log_beta = jax.nn.log_sigmoid(z)
        log_one_minus = jnp.where(strict, jax.nn.log_sigmoid(-z), 0.0)
        suffix = lax.cumsum(log_one_minus, axis=3, reverse=True) - log_one_minus
        a = jnp.where(strict, jnp.exp(log_beta + suffix), 0.0)
        outs.append(jnp.einsum('bhqk,bkhd->bqhd', a.astype(v.dtype), v[:, :kend]))
    return jnp.concatenate(outs, axis=1)

def token_mixing(h, w_in, rel_bias, lq1, lk1, lq2, lk2, subln_g, w_out, lambda_init):
    b, s, _ = h.shape
    proj = h @ w_in
    sizes = [WIDTH_A, WIDTH_A, WIDTH_A, B_QK_WIDTH, B_QK_WIDTH, WIDTH_B, WIDTH_C, WIDTH_C, WIDTH_C]
    qa, ka, va, qb, kb, vb, qc, kc, vc = jnp.split(proj, [int(c) for c in np.cumsum(sizes)[:-1]], axis=-1)
    hd_a = (b, s, N_HEADS_A, HEAD_DIM)
    o_a = chunk_band_attention(qa.reshape(hd_a), ka.reshape(hd_a), va.reshape(hd_a), rel_bias)
    lam = (jnp.exp(jnp.sum(lq1.astype(jnp.float32) * lk1.astype(jnp.float32)))
           - jnp.exp(jnp.sum(lq2.astype(jnp.float32) * lk2.astype(jnp.float32))) + lambda_init)
    hd_bqk = (b, s, N_HEADS_B, 2, DIFF_QK_DIM)
    o_b = diff_attention(qb.reshape(hd_bqk), kb.reshape(hd_bqk), vb.reshape(b, s, N_HEADS_B, DIFF_V_DIM),
                         lam, subln_g, lambda_init)
    hd_c = (b, s, N_HEADS_C, HEAD_DIM)
    o_c = stick_breaking_attention(qc.reshape(hd_c), kc.reshape(hd_c), vc.reshape(hd_c))
    y = jnp.concatenate([o_a.reshape(b, s, WIDTH_A), o_b.reshape(b, s, WIDTH_B),
                         o_c.reshape(b, s, WIDTH_C)], axis=-1)
    return y @ w_out

def first_inputs(seed: int = 0) -> dict:
    key = jax.random.key(seed)
    ks = jax.random.split(key, 32)
    f32 = jnp.float32

    def nrm(k, shape, scale):
        return jax.random.normal(k, shape, f32) * scale

    def gain(k, shape):
        return 1.0 + 0.05 * jax.random.normal(k, shape, f32)

    L = DEPTH
    return {
        "x": jax.random.normal(ks[0], (BATCH, SEQ, D_MODEL), f32),
        "ffn1_pre_g": gain(ks[1], (L, D_MODEL)),
        "ffn1_w_gate": nrm(ks[2], (L, D_MODEL, D_FF), D_MODEL ** -0.5),
        "ffn1_w_up": nrm(ks[3], (L, D_MODEL, D_FF), D_MODEL ** -0.5),
        "ffn1_w_down": nrm(ks[4], (L, D_FF, D_MODEL), D_FF ** -0.5),
        "ffn1_post_g": gain(ks[5], (L, D_MODEL)),
        "mix_pre_g": gain(ks[6], (L, D_MODEL)),
        "w_in": nrm(ks[7], (L, D_MODEL, IN_COLS), D_MODEL ** -0.5),
        "rel_bias": nrm(ks[8], (L, N_HEADS_A, 2 * REL_CLIP + 1), 0.2),
        "diff_lambda_q1": nrm(ks[9], (L, DIFF_QK_DIM), 0.1),
        "diff_lambda_k1": nrm(ks[10], (L, DIFF_QK_DIM), 0.1),
        "diff_lambda_q2": nrm(ks[11], (L, DIFF_QK_DIM), 0.1),
        "diff_lambda_k2": nrm(ks[12], (L, DIFF_QK_DIM), 0.1),
        "diff_subln_g": gain(ks[13], (L, DIFF_V_DIM)),
        "w_out": nrm(ks[14], (L, D_MIX, D_MODEL), D_MIX ** -0.5),
        "mix_post_g": gain(ks[15], (L, D_MODEL)),
        "ffn2_pre_g": gain(ks[16], (L, D_MODEL)),
        "ffn2_w_gate": nrm(ks[17], (L, D_MODEL, D_FF), D_MODEL ** -0.5),
        "ffn2_w_up": nrm(ks[18], (L, D_MODEL, D_FF), D_MODEL ** -0.5),
        "ffn2_w_down": nrm(ks[19], (L, D_FF, D_MODEL), D_FF ** -0.5),
        "ffn2_post_g": gain(ks[20], (L, D_MODEL)),
    }

def first_block(x, ffn1_pre_g, ffn1_w_gate, ffn1_w_up, ffn1_w_down, ffn1_post_g,
              mix_pre_g, w_in, rel_bias, diff_lambda_q1, diff_lambda_k1, diff_lambda_q2,
              diff_lambda_k2, diff_subln_g, w_out, mix_post_g,
              ffn2_pre_g, ffn2_w_gate, ffn2_w_up, ffn2_w_down, ffn2_post_g):
    for l in range(DEPTH):
        lambda_init = 0.8 - 0.6 * math.exp(-0.3 * l)
        f = swiglu(rmsnorm(x, ffn1_pre_g[l]), ffn1_w_gate[l], ffn1_w_up[l], ffn1_w_down[l])
        x = x + FFN_RESIDUAL_WEIGHT * rmsnorm(f, ffn1_post_g[l])
        m = token_mixing(rmsnorm(x, mix_pre_g[l]), w_in[l], rel_bias[l],
                         diff_lambda_q1[l], diff_lambda_k1[l], diff_lambda_q2[l], diff_lambda_k2[l],
                         diff_subln_g[l], w_out[l], lambda_init)
        x = x + rmsnorm(m, mix_post_g[l])
        f = swiglu(rmsnorm(x, ffn2_pre_g[l]), ffn2_w_gate[l], ffn2_w_up[l], ffn2_w_down[l])
        x = x + FFN_RESIDUAL_WEIGHT * rmsnorm(f, ffn2_post_g[l])
    return x


N_META = 16
GROUP_HEAD_DIM = 64
D_MIX_2 = D_MODEL
ATTN_HEADS = 8
ATTN_HEAD_DIM = 64
D_ATTN = ATTN_HEADS * ATTN_HEAD_DIM
D_CONV = D_MIX_2 // 4
D_SC = D_MIX_2 - D_ATTN - D_CONV
CONV_KERNEL = 31
SC_KERNEL = 3
FFN_KERNEL = 3
RMS_EPS = 1e-6
LN_EPS = 1e-5
IN_SPLITS = (D_ATTN, D_ATTN, D_ATTN, ATTN_HEADS,
             D_CONV, D_CONV,
             D_SC, D_SC, D_SC)
D_IN = sum(IN_SPLITS)
NEG_INF_2 = -1e30


def rms_norm(x, g):
    xf = x.astype(jnp.float32)
    y = xf * lax.rsqrt(jnp.mean(xf * xf, axis=-1, keepdims=True) + RMS_EPS)
    return (y * g.astype(jnp.float32)).astype(x.dtype)

def head_rms_norm(y, g):
    b, l, d = y.shape
    yf = y.astype(jnp.float32).reshape(b, l, d // GROUP_HEAD_DIM, GROUP_HEAD_DIM)
    yf = yf * lax.rsqrt(jnp.mean(yf * yf, axis=-1, keepdims=True) + RMS_EPS)
    return (yf.reshape(b, l, d) * g.astype(jnp.float32)).astype(y.dtype)

def layer_norm(x, g, b):
    xf = x.astype(jnp.float32)
    mu = jnp.mean(xf, axis=-1, keepdims=True)
    var = jnp.mean(jnp.square(xf - mu), axis=-1, keepdims=True)
    y = (xf - mu) * lax.rsqrt(var + LN_EPS)
    return (y * g.astype(jnp.float32) + b.astype(jnp.float32)).astype(x.dtype)

def causal_depthwise_conv(x, w):
    k, c = w.shape
    return lax.conv_general_dilated(
        x, w[:, None, :].astype(x.dtype), window_strides=(1,),
        padding=[(k - 1, 0)], dimension_numbers=("NWC", "WIO", "NWC"),
        feature_group_count=c)

def forgetting_attention(q, k, v, log_f):
    L = q.shape[1]
    scale = ATTN_HEAD_DIM ** -0.5
    F = jnp.cumsum(log_f, axis=1).transpose(0, 2, 1)

    def attend(start, end):
        qb = q[:, start:end]
        s = jnp.einsum("bqhd,bkhd->bhqk", qb, k[:, :end],
                       preferred_element_type=jnp.float32) * scale
        s = s + F[:, :, start:end, None] - F[:, :, None, :end]
        mask = jnp.arange(start, end)[:, None] >= jnp.arange(end)[None, :]
        s = jnp.where(mask, s, NEG_INF_2)
        p = jax.nn.softmax(s, axis=-1)
        return jnp.einsum("bhqk,bkhd->bqhd", p.astype(v.dtype), v[:, :end])

    outs = [attend(0, N_META)]
    for i in range((L - N_META) // Q_BLOCK):
        start = N_META + i * Q_BLOCK
        outs.append(attend(start, start + Q_BLOCK))
    return jnp.concatenate(outs, axis=1)

def mixer_sublayer(h, pre_g, post_g, w_in, b_forget, a_dw_w, a_dw_b, a_ln_g,
                   a_ln_b, a_pw_w, sc_conv_w, head_g, w_out):
    bsz, L, _ = h.shape
    u = rms_norm(h, pre_g)
    z = jnp.einsum("bld,de->ble", u, w_in)
    idx = np.cumsum(IN_SPLITS)[:-1].tolist()
    q, k, v, f_logit, a_val, a_gate, sc_b, sc_c, sc_x = jnp.split(z, idx, axis=-1)

    log_f = jax.nn.log_sigmoid((f_logit + b_forget).astype(jnp.float32))
    hs = (bsz, L, ATTN_HEADS, ATTN_HEAD_DIM)
    y_attn = forgetting_attention(q.reshape(hs), k.reshape(hs), v.reshape(hs), log_f)
    y_attn = y_attn.reshape(bsz, L, D_ATTN)

    a = a_val * jax.nn.sigmoid(a_gate)
    a = causal_depthwise_conv(a, a_dw_w) + a_dw_b
    a = jax.nn.silu(layer_norm(a, a_ln_g, a_ln_b))
    y_conv = jnp.einsum("blc,ce->ble", a, a_pw_w)

    y_sc = sc_b * causal_depthwise_conv(sc_c * sc_x, sc_conv_w)

    y = jnp.concatenate([y_attn, y_conv, y_sc], axis=-1)
    y = jnp.einsum("ble,ed->bld", head_rms_norm(y, head_g), w_out)
    return h + rms_norm(y, post_g)

def ffn_sublayer(h, pre_g, post_g, w_up, conv_w, w_down):
    u = rms_norm(h, pre_g)
    z = jnp.einsum("bld,df->blf", u, w_up)
    z = causal_depthwise_conv(z, conv_w)
    g, up = jnp.split(z, 2, axis=-1)
    y = jnp.einsum("blf,fd->bld", jax.nn.silu(g) * up, w_down)
    return h + rms_norm(y, post_g)

def second_inputs(seed: int = 0) -> dict:
    key = jax.random.key(seed)
    ks = jax.random.split(key, 20)
    f32 = jnp.float32

    def nrm(k, shape, scale):
        return jax.random.normal(k, shape, f32) * scale

    def gain(k, shape):
        return 1.0 + 0.05 * jax.random.normal(k, shape, f32)

    x = jax.random.normal(ks[0], (BATCH, SEQ, D_MODEL), f32)
    meta_tokens = nrm(ks[1], (N_META, D_MODEL), 1.0)
    col_scale = np.ones((D_IN,), np.float32)
    f0 = 3 * D_ATTN
    col_scale[f0:f0 + ATTN_HEADS] = 0.1
    w_in = nrm(ks[2], (DEPTH, D_MODEL, D_IN), D_MODEL ** -0.5) * jnp.asarray(col_scale)
    b_forget = jax.random.uniform(ks[3], (DEPTH, ATTN_HEADS), f32, 3.0, 6.0)
    return {
        "x": x,
        "meta_tokens": meta_tokens,
        "mix_pre_g": gain(ks[4], (DEPTH, D_MODEL)),
        "mix_post_g": gain(ks[5], (DEPTH, D_MODEL)),
        "w_in": w_in,
        "b_forget": b_forget,
        "a_dw_w": nrm(ks[6], (DEPTH, CONV_KERNEL, D_CONV), CONV_KERNEL ** -0.5),
        "a_dw_b": nrm(ks[7], (DEPTH, D_CONV), 0.02),
        "a_ln_g": gain(ks[8], (DEPTH, D_CONV)),
        "a_ln_b": nrm(ks[9], (DEPTH, D_CONV), 0.02),
        "a_pw_w": nrm(ks[10], (DEPTH, D_CONV, D_CONV), D_CONV ** -0.5),
        "sc_conv_w": nrm(ks[11], (DEPTH, SC_KERNEL, D_SC), SC_KERNEL ** -0.5),
        "head_g": gain(ks[12], (DEPTH, D_MIX_2)),
        "w_out": nrm(ks[13], (DEPTH, D_MIX_2, D_MODEL), D_MIX_2 ** -0.5),
        "ffn_pre_g": gain(ks[14], (DEPTH, D_MODEL)),
        "ffn_post_g": gain(ks[15], (DEPTH, D_MODEL)),
        "ffn_w_up": nrm(ks[16], (DEPTH, D_MODEL, 2 * D_FF), D_MODEL ** -0.5),
        "ffn_conv_w": nrm(ks[17], (DEPTH, FFN_KERNEL, 2 * D_FF), FFN_KERNEL ** -0.5),
        "ffn_w_down": nrm(ks[18], (DEPTH, D_FF, D_MODEL), D_FF ** -0.5),
    }

def second_block(x, meta_tokens, mix_pre_g, mix_post_g, w_in, b_forget, a_dw_w,
              a_dw_b, a_ln_g, a_ln_b, a_pw_w, sc_conv_w, head_g, w_out,
              ffn_pre_g, ffn_post_g, ffn_w_up, ffn_conv_w, ffn_w_down):
    bsz = x.shape[0]
    meta = jnp.broadcast_to(meta_tokens[None].astype(x.dtype), (bsz, N_META, x.shape[-1]))
    h = jnp.concatenate([meta, x], axis=1)
    for l in range(DEPTH):
        h = mixer_sublayer(h, mix_pre_g[l], mix_post_g[l], w_in[l], b_forget[l],
                           a_dw_w[l], a_dw_b[l], a_ln_g[l], a_ln_b[l], a_pw_w[l],
                           sc_conv_w[l], head_g[l], w_out[l])
        h = ffn_sublayer(h, ffn_pre_g[l], ffn_post_g[l], ffn_w_up[l],
                         ffn_conv_w[l], ffn_w_down[l])
    return h[:, N_META:]


def setup_inputs(seed=0):
    out = dict(first_inputs(seed))
    for name, value in second_inputs(seed + 1).items():
        if name != "x":
            out[name + "_2"] = value
    return out


def reference(
    x, ffn1_pre_g, ffn1_w_gate, ffn1_w_up, ffn1_w_down, ffn1_post_g, mix_pre_g, w_in, rel_bias,
    diff_lambda_q1, diff_lambda_k1, diff_lambda_q2, diff_lambda_k2, diff_subln_g, w_out,
    mix_post_g, ffn2_pre_g, ffn2_w_gate, ffn2_w_up, ffn2_w_down, ffn2_post_g, meta_tokens_2,
    mix_pre_g_2, mix_post_g_2, w_in_2, b_forget_2, a_dw_w_2, a_dw_b_2, a_ln_g_2, a_ln_b_2,
    a_pw_w_2, sc_conv_w_2, head_g_2, w_out_2, ffn_pre_g_2, ffn_post_g_2, ffn_w_up_2,
    ffn_conv_w_2, ffn_w_down_2,
):
    x = first_block(
        x, ffn1_pre_g, ffn1_w_gate, ffn1_w_up, ffn1_w_down, ffn1_post_g, mix_pre_g, w_in,
        rel_bias, diff_lambda_q1, diff_lambda_k1, diff_lambda_q2, diff_lambda_k2, diff_subln_g,
        w_out, mix_post_g, ffn2_pre_g, ffn2_w_gate, ffn2_w_up, ffn2_w_down, ffn2_post_g,
    )
    return second_block(
        x, meta_tokens_2, mix_pre_g_2, mix_post_g_2, w_in_2, b_forget_2, a_dw_w_2, a_dw_b_2,
        a_ln_g_2, a_ln_b_2, a_pw_w_2, sc_conv_w_2, head_g_2, w_out_2, ffn_pre_g_2, ffn_post_g_2,
        ffn_w_up_2, ffn_conv_w_2, ffn_w_down_2,
    )


_drawn_inputs = setup_inputs


def setup_inputs(seed=0):
    import zlib

    import numpy as np

    out = dict(_drawn_inputs(seed))
    spreads = {}
    factors = {'diff_lambda_q1': 2.984,
     'diff_lambda_k1': 7.104,
     'a_dw_b_2': 4.28,
     'a_ln_g_2': 2.871,
     'a_ln_b_2': 8.0}
    for name, (base, spread) in spreads.items():
        noise = np.random.default_rng([zlib.crc32(name.encode()), seed]).standard_normal(out[name].shape)
        drawn = base * np.exp(spread * noise) if base else spread * noise
        out[name] = __import__('jax').numpy.asarray(drawn.astype(out[name].dtype))
    for name, factor in factors.items():
        out[name] = (out[name] * factor).astype(out[name].dtype)
    return out
```

```python
import math
from contextlib import ExitStack

import concourse.bass as bass
from concourse import mybir

F32 = mybir.dt.float32
F32R = mybir.dt.float32r
ALU = mybir.AluOpType
ACT = mybir.ActivationFunctionType
AX = mybir.AxisListType

P = 128
D = 1024
KD = D // P
FF = 2816
KF = FF // P
SEQ = 512
META = 16
LAYERS = 2
PAIR = 2 * P
UP_ITERS = FF // PAIR
UP_GRAN = 4 * UP_ITERS
DOWN_PAIRS = D // PAIR
DOWN_Q = [4, 4, 4, 4, 4, 2]
DOWN_GRAN = DOWN_PAIRS * len(DOWN_Q)
FFN_GRAN = UP_GRAN + DOWN_GRAN
OUT_Q = [4, 4]
OUT_GRAN = DOWN_PAIRS * len(OUT_Q)
EPS = 1e-6
LN_EPS = 1e-5
NEG = -1e30

KINDS = "AAABBCCC"
QKV1 = [(128 * c, 384 + 128 * c, 768 + 128 * c) for c in range(3)]
QKV1 += [(1152 + 128 * c, 1408 + 128 * c, 1664 + 128 * c) for c in range(2)]
QKV1 += [(1920 + 128 * c, 2304 + 128 * c, 2688 + 128 * c) for c in range(3)]
IN1 = 3072
MIX1_GRAN = 24 + OUT_GRAN
UNITS1 = 64
SLOPE = [2.0 ** (-2 * (h + 1)) for h in range(4)]
B_SCALE = 32.0 ** -0.5

IN2 = 2824
F_COL = 1536
ACOL = 1544
COLS2 = [F_COL] + [ACOL + 128 * c for c in (0, 2, 1, 3)]
for _p in range(4):
    COLS2 += [128 * _p, 512 + 128 * _p, 1024 + 128 * _p]
COLS2 += [ACOL + 512 + 128 * c for c in (0, 2, 4, 1, 3, 5)]
MIX2_GRAN = len(COLS2) + 1 + OUT_GRAN
TAPS = 31
QB = 5
UNITS2 = 4 * QB * 2

PAR_FF1PRE, PAR_FF1POST, PAR_MIXPRE, PAR_MIXPOST, PAR_FF2PRE, PAR_FF2POST = (16 * i for i in range(6))
PAR_MIXPRE2, PAR_MIXPOST2, PAR_FFPRE2, PAR_FFPOST2, PAR_HEADG = (96 + 16 * i for i in range(5))
PAR_DWB, PAR_LNG, PAR_LNB, PAR_SUBLN, PAR_SCW = 176, 180, 184, 188, 190
PAR_DW = 202
PAR_FCW = 326
PAR_COLS = PAR_FCW + 3 * 88


class Record:
    pass


class Step:

    def __init__(self):
        self.vt = self.sc = None
        self.tiles, self.tr = [], []
        self.pairs, self.done = [], []


class Stack:

    def __init__(self, n, s, T, off, nh, TW, NT, GL, evf_layer, conv):
        self.n, self.s = n, s
        self.T, self.off = T, off
        self.nh, self.w = nh, T // nh
        self.TW, self.NT = TW, NT
        self.GL = GL
        self.evf_layer = evf_layer
        self.conv = conv


class Ffn:

    def __init__(self, sub, gb, gb2, ev, hb, gate, up, upoff, down):
        self.sub, self.gb, self.gb2, self.ev, self.hb = sub, gb, gb2, ev, hb
        self.gate, self.up, self.upoff, self.down = gate, up, upoff, down


def schedule(pairs, units_per_pair, lag, fill):
    n = pairs * units_per_pair
    steps = []
    for s in range(n + 3):
        steps.append(Step())
        if s < n:
            steps[s].sc = s
            if s % units_per_pair == 0:
                steps[s].vt = s // units_per_pair
    at = 0
    for u in range(n):
        at = max(at, u + lag(u))
        steps[at].tr.append(u)
        if u % units_per_pair == units_per_pair - 1:
            steps[at].pairs.append(u // units_per_pair)
    for p, grans in enumerate(fill):
        tiles = [(g, t) for g in grans for t in range(8)]
        for s in range(units_per_pair):
            a, b = len(tiles) * s // units_per_pair, len(tiles) * (s + 1) // units_per_pair
            st = steps[p * units_per_pair + s]
            st.tiles += tiles[a:b]
            st.done += [g for g, t in tiles[a:b] if t == 7]
    while not steps[-1].tr:
        steps.pop()
    return steps


def t_events(steps):
    order = []
    for st in steps:
        if st.vt is not None:
            order.append(("v", st.vt))
        order += [("p", u) for u in st.tr]
    return {e: n for n, e in enumerate(order)}


STEPS1 = schedule(8, 8, lambda u: 2 if KINDS[u // 8] == "C" else 1,
                  [[3 * p + 3, 3 * p + 4, 3 * p + 5] for p in range(7)])
TEV1 = t_events(STEPS1)
STEPS2 = schedule(4, 2 * QB, lambda u: 1, [[8, 9, 10], [11, 12, 13], [14, 15, 16], list(range(17, 23))])
TEV2 = t_events(STEPS2)
DW_OPS = [(t, c) for t in range(TAPS) for c in range(2)]
DW_PER_STEP = 2


class Chain:

    def __init__(self, eng, sem, per_layer):
        self.eng, self.sem, self.per_layer = eng, sem, per_layer
        self.base, self.n = 0, 0

    def __call__(self, ins):
        ins.then_inc(self.sem, 1)
        self.n += 1
        return ins

    def wait(self):
        self.eng.wait_ge(self.sem, self.base + self.n)


def program(nc, I, out):
    with ExitStack() as ctx:
        def sb(name, shape, dt=F32):
            return ctx.enter_context(nc.sbuf_tensor(name, shape, dt))

        def sem(name):
            return ctx.enter_context(nc.semaphore(name))

        TM = SEQ + META
        x = sb("x", [P, KD, TM])
        y = sb("y", [P, KD, TM])
        xhi, xlo = sb("xhi", [P, KD, TM], F32R), sb("xlo", [P, KD, TM], F32R)
        raw = [sb(f"raw{i}", [P, 1024]) for i in range(2)]
        whi = [sb(f"whi{i}", [P, 1024], F32R) for i in range(2)]
        wlo = [sb(f"wlo{i}", [P, 1024], F32R) for i in range(2)]
        S = [sb(f"S{i}", [P, TM + 2]) for i in range(6)]
        r = sb("r", [P, TM])
        par = sb("par", [P, PAR_COLS])
        ident = sb("ident", [P, P])
        ones = sb("ones", [P, SEQ])
        eps = sb("eps", [P, 1])
        rms = sb("rms", [P, 6])
        rinv = sb("rinv", [P, 6])
        dist = sb("dist", [P, SEQ])
        strict = sb("strict", [P, P])
        negs = sb("negs", [P, P])
        bd = sb("bd", [P, P])
        negc = sb("negc", [P, P])
        bf = sb("bf", [8, LAYERS])
        lneps = sb("lneps", [P, 1])
        nlam = sb("nlam", [P, LAYERS])
        tbias_dram = nc.dram_tensor("tbias_scratch", (LAYERS * 6, P, SEQ), F32).ap()
        rev_dram = nc.dram_tensor("rev_scratch", (LAYERS * 6, 640), F32).ap()
        ps = ctx.enter_context(nc.psum_tensor("ps", [P, 8, 512], F32))
        xin = y[:, :, :].rearrange("p k t -> p (k t)")[:, 0:4 * D].rearrange("p (a d) -> p a d", a=4)

        sq = S[0:2]
        tt = S[2:4]
        acc = S[4]
        diag = S[5]

        area = ExitStack()
        hhi = area.enter_context(nc.sbuf_tensor("hhi", [P, KF, TM], F32R))
        hlo = area.enter_context(nc.sbuf_tensor("hlo", [P, KF, TM], F32R))
        area.close()
        area = ExitStack()

        def ab(name, shape, dt=F32):
            return area.enter_context(nc.sbuf_tensor(name, shape, dt))

        m1 = Record()
        m1.ohi = ab("m1_ohi", [P, KD, SEQ], F32R)
        m1.olo = ab("m1_olo", [P, KD, SEQ], F32R)
        m1.q = [ab(f"m1_q{i}", [P, SEQ]) for i in range(2)]
        m1.k = [ab(f"m1_k{i}", [P, SEQ]) for i in range(2)]
        m1.vt = [ab(f"m1_vt{i}", [P, SEQ]) for i in range(2)]
        m1.v = [ab(f"m1_v{i}", [P, 4, P]) for i in range(2)]
        m1.w = [ab(f"m1_w{i}", [P, 2, SEQ]) for i in range(3)]
        m1.e = [ab(f"m1_e{i}", [P, SEQ]) for i in range(2)]
        m1.sp = ab("m1_sp", [P, SEQ])
        m1.scan = ab("m1_scan", [P, SEQ])
        m1.pt = [ab(f"m1_pt{i}", [P, 4, P]) for i in range(2)]
        m1.ob = ab("m1_ob", [P, 2, SEQ])
        m1.sqb = ab("m1_sqb", [P, 2, SEQ])
        m1.rb = ab("m1_rb", [P, 2, SEQ])
        m1.nmax = [ab(f"m1_nmax{i}", [P, 2]) for i in range(3)]
        m1.sums = [ab(f"m1_sums{i}", [P, 2]) for i in range(3)]
        m1.inv = [ab(f"m1_inv{i}", [P, 2]) for i in range(3)]
        m1.c1 = [ab(f"m1_c1{i}", [P, 1]) for i in range(3)]
        tb = y[:, :, :].rearrange("p k t -> p (k t)")[:, 0:6 * SEQ].rearrange("p (h c) -> p h c", h=6)
        area.close()
        area = ExitStack()
        fb = ab("m2_fb", [P, 8, TM])
        apad = ab("m2_apad", [P, 2, TAPS - 1 + TM])
        aconv = ab("m2_aconv", [P, 2, TM])
        scx, scc, scb = ab("m2_scx", [P, 2 + TM]), ab("m2_scc", [P, TM]), ab("m2_scb", [P, TM])
        area.close()
        area = ExitStack()
        m2 = Record()
        m2.ohi = ab("m2_ohi", [P, KD, TM], F32R)
        m2.olo = ab("m2_olo", [P, KD, TM], F32R)
        m2.q = [ab(f"m2_q{i}", [P, TM]) for i in range(2)]
        m2.k = [ab(f"m2_k{i}", [P, TM]) for i in range(2)]
        m2.vt = [ab(f"m2_vt{i}", [P, TM]) for i in range(2)]
        m2.v = [ab(f"m2_v{i}", [P, QB, P]) for i in range(2)]
        m2.w = [ab(f"m2_w{i}", [P, TM]) for i in range(3)]
        m2.pt = [ab(f"m2_pt{i}", [P, QB, P]) for i in range(2)]
        m2.ahi = ab("m2_ahi", [P, 2, TM], F32R)
        m2.alo = ab("m2_alo", [P, 2, TM], F32R)
        m2.lsq = ab("m2_lsq", [P, 2, TM])
        m2.lrs = ab("m2_lrs", [P, TM])
        m2.u = ab("m2_u", [8, TM])
        m2.lf = ab("m2_lf", [8, TM])
        m2.nf = ab("m2_nf", [8, TM])
        m2.e = ab("m2_e", [8, TM])
        m2.nmax = [ab(f"m2_nmax{i}", [P, 1]) for i in range(3)]
        m2.sums = [ab(f"m2_sums{i}", [P, 1]) for i in range(3)]
        m2.inv = [ab(f"m2_inv{i}", [P, 1]) for i in range(3)]
        area.close()
        area = ExitStack()
        prow = [ab(f"prow{i}", [P, P]) for i in range(6)]
        metain = ab("metain", [META, D])
        relin = ab("relin", [12, 257])
        rev = ab("rev", [12, 640])
        lam_in = ab("lam_in", [P, 4, LAYERS, 32])
        lam_pr = ab("lam_pr", [P, 2, LAYERS, 32])
        lam_s = ab("lam_s", [P, 2, LAYERS])
        lam_e = ab("lam_e", [P, 2, LAYERS])
        area.close()

        def semaphores(b):
            s = Record()
            s.weights_landed = [sem(f"{b}_weights_landed{i}") for i in range(2)]
            s.weights_hi = sem(f"{b}_weights_hi")
            s.weights_split = sem(f"{b}_weights_split")
            s.granules_done = sem(f"{b}_granules_done")
            s.hidden_free = sem(f"{b}_hidden_free")
            s.out_free = sem(f"{b}_out_free")
            s.norm_sums = sem(f"{b}_norm_sums")
            s.norm_rms = sem(f"{b}_norm_rms")
            s.norm_diag = sem(f"{b}_norm_diag")
            s.norm_spread = sem(f"{b}_norm_spread")
            s.norm_r = sem(f"{b}_norm_r")
            s.x_new = sem(f"{b}_x_new")
            s.x_hi = sem(f"{b}_x_hi")
            s.x_lo = sem(f"{b}_x_lo")
            s.x_squared = sem(f"{b}_x_squared")
            s.x_summed = sem(f"{b}_x_summed")
            s.y_squared = sem(f"{b}_y_squared")
            s.y_summed = sem(f"{b}_y_summed")
            s.gate_in = sem(f"{b}_gate_in")
            s.silu_done = sem(f"{b}_silu_done")
            s.hidden_done = sem(f"{b}_hidden_done")
            s.hidden_hi = sem(f"{b}_hidden_hi")
            s.hidden_lo = sem(f"{b}_hidden_lo")
            s.columns_out = sem(f"{b}_columns_out")
            s.scores_done = sem(f"{b}_scores_done")
            s.scores_free = sem(f"{b}_scores_free")
            s.max_done = sem(f"{b}_max_done")
            s.exp_done = sem(f"{b}_exp_done")
            s.probs_done = sem(f"{b}_probs_done")
            s.transposed = sem(f"{b}_transposed")
            s.transposed_out = sem(f"{b}_transposed_out")
            s.pv_done = sem(f"{b}_pv_done")
            s.o_hi_out = sem(f"{b}_o_hi_out")
            return s

        def first_semaphores(b, s):
            s.o_lo_out = sem(f"{b}_o_lo_out")
            s.softplus_steps = sem(f"{b}_softplus_steps")
            s.softplus_read = sem(f"{b}_softplus_read")
            s.stick_logits = sem(f"{b}_stick_logits")
            s.b_act_steps = sem(f"{b}_b_act_steps")
            s.b_sums = sem(f"{b}_b_sums")
            s.b_scaled = sem(f"{b}_b_scaled")
            s.b_hi = sem(f"{b}_b_hi")
            s.b_lo = sem(f"{b}_b_lo")
            s.dve_steps = sem(f"{b}_dve_steps")
            return s

        def second_semaphores(b, s):
            s.up_in = sem(f"{b}_up_in")
            s.last_tap = sem(f"{b}_last_tap")
            s.forget_in = sem(f"{b}_forget_in")
            s.forget_steps = sem(f"{b}_forget_steps")
            s.forget_sums = sem(f"{b}_forget_sums")
            s.forget_spread = sem(f"{b}_forget_spread")
            s.forget_out = sem(f"{b}_forget_out")
            s.a_gate_in = sem(f"{b}_a_gate_in")
            s.a_gate_done = sem(f"{b}_a_gate_done")
            s.dw_taps = sem(f"{b}_dw_taps")
            s.ln_sums = sem(f"{b}_ln_sums")
            s.ln_centered = sem(f"{b}_ln_centered")
            s.ln_squared = sem(f"{b}_ln_squared")
            s.ln_steps = sem(f"{b}_ln_steps")
            s.ln_scaled = sem(f"{b}_ln_scaled")
            s.ln_silu = sem(f"{b}_ln_silu")
            s.a_lo = sem(f"{b}_a_lo")
            s.pw_out = sem(f"{b}_pw_out")
            s.short_done = sem(f"{b}_short_done")
            s.head_squared = sem(f"{b}_head_squared")
            s.head_sums = sem(f"{b}_head_sums")
            s.head_steps = sem(f"{b}_head_steps")
            s.head_scaled = sem(f"{b}_head_scaled")
            s.head_hi = sem(f"{b}_head_hi")
            s.head_lo = sem(f"{b}_head_lo")
            return s

        s_ld = [sem(f"s_ld{i}") for i in range(6)]
        s_ones = sem("s_ones")
        s_const = sem("s_const")
        s_xt, s_xc, s_pt, s_pc = sem("s_xt"), sem("s_xc"), sem("s_ptr"), sem("s_pcopy")
        s_rev, s_revd, s_tbias, s_tb, s_mask = sem("s_rev"), sem("s_revd"), sem("s_tbias"), sem("s_tb"), sem("s_mask")
        s_lam = sem("s_lam")
        s_set, s_dist = sem("s_set"), sem("s_dist")
        s_ot, s_oc, s_out = sem("s_ot"), sem("s_oc"), sem("s_out")
        CR = 2

        b1 = Stack(
            n=1, s=first_semaphores("b1", semaphores("b1")), T=SEQ, off=META, nh=1, TW=128, NT=4, GL=2 * FFN_GRAN + MIX1_GRAN,
            evf_layer=4 * UP_ITERS, conv=False)
        b2 = Stack(
            n=2, s=second_semaphores("b2", semaphores("b2")), T=TM, off=0, nh=2, TW=88, NT=6, GL=FFN_GRAN + MIX2_GRAN,
            evf_layer=2 * UP_ITERS, conv=True)

        def halves(b):
            return [(h * b.w, b.w) for h in range(b.nh)]

        def pview(b, bank, nh=None):
            return ps[:, bank:bank + b.nh, 0:b.w]

        def tview(b, ap):
            return ap.rearrange("p (h w) -> p h w", h=b.nh)

        def xs(b, t, c):
            return t[:, c, b.off:b.off + b.T] if b.n == 1 else t[:, c, 0:b.T]

        def gain(col, l, c):
            return par[:, bass.ds(l * KD + (col + c), 1)]

        def load_raw(sp, b, g, slot, src, shape):
            sp.wait_ge(b.s.weights_split, g + 1)
            k, c = shape
            dst = raw[slot][:, 0:k * c].rearrange("p (k c) -> p k c", k=k)
            sp.dma_start(dst, src.rearrange("(k p) c -> p k c", p=P)).then_inc(b.s.weights_landed[slot], 16)

        def split_hi(act, b, g, g2, slot, n=1024):
            act.wait_ge(b.s.weights_landed[slot], 16 * g2 + 16)
            act.wait_ge(b.s.granules_done, g + 1)
            act.activation(whi[slot][:, 0:n], raw[slot][:, 0:n], ACT.Copy).then_inc(b.s.weights_hi, 1)

        def split_lo(dve, b, g, slot, n=1024):
            dve.wait_ge(b.s.weights_hi, g + 1)
            dve.tensor_tensor(wlo[slot][:, 0:n], raw[slot][:, 0:n], whi[slot][:, 0:n].bitcast(F32),
                              ALU.subtract).then_inc(b.s.weights_split, 1)

        def tile_mm(pe, b, bank, slot, wcol, hi, lo, first, last):
            wh, wl = whi[slot][:, wcol:wcol + P], wlo[slot][:, wcol:wcol + P]
            for n, (t0, w) in enumerate(halves(b)):
                o = ps[:, bank + n, 0:w]
                pe.matmul(o, wh, hi[:, t0:t0 + w], start=first, stop=False)
                pe.matmul(o, wh, lo[:, t0:t0 + w], start=False, stop=False)
                ins = pe.matmul(o, wl, hi[:, t0:t0 + w], start=False, stop=last)
            return ins

        def pe_sum(pe, b, n, bank, srcs):
            for t in range(b.NT):
                for j, sc in enumerate(srcs):
                    ins = pe.matmul(ps[0:b.TW, bank, t:t + 1], sc[:, t * b.TW:(t + 1) * b.TW], ones[:, 0:1],
                                    start=(j == 0), stop=(j == len(srcs) - 1))
            ins.then_inc(b.s.norm_sums, 1)

        def act_rms(act, b, n, bank):
            act.wait_ge(b.s.norm_sums, n + 1)
            act.activation(rms[0:b.TW, 0:b.NT], ps[0:b.TW, bank, 0:b.NT], ACT.Sqrt,
                           bias=eps[0:b.TW, :], scale=1.0 / D).then_inc(b.s.norm_rms, 1)

        def dve_diag(dve, b, n, ch):
            dve.wait_ge(b.s.norm_rms, n + 1)
            ch(dve.reciprocal(rinv[0:b.TW, 0:b.NT], rms[0:b.TW, 0:b.NT]))
            ch.wait()
            dv = diag[0:b.TW, 0:b.T].rearrange("p (t n) -> p t n", t=b.NT)
            dve.tensor_tensor(dv, ident[0:b.TW, 0:b.TW].unsqueeze(1).to_broadcast([b.TW, b.NT, b.TW]),
                              rinv[0:b.TW, 0:b.NT].unsqueeze(2).to_broadcast([b.TW, b.NT, b.TW]),
                              ALU.mult).then_inc(b.s.norm_diag, 1)

        def pe_bc(pe, b, n, bank):
            pe.wait_ge(b.s.norm_diag, n + 1)
            for i, (t0, w) in enumerate(halves(b)):
                ins = pe.matmul(ps[:, bank + i, 0:w], ones[0:b.TW, 0:P], diag[0:b.TW, t0:t0 + w],
                                start=True, stop=True)
            ins.then_inc(b.s.norm_spread, 1)

        def act_r(act, b, n, bank):
            act.wait_ge(b.s.norm_spread, n + 1)
            act.activation(tview(b, r[:, 0:b.T]), pview(b, bank), ACT.Copy).then_inc(b.s.norm_r, 1)

        SUM_PRE, BC_PRE, SUM_POST, BC_POST = 4, 6, 0, 6

        def act_operand(act, b, l, sub, col, c):
            act.wait_ge(b.s.x_new, 8 * sub + c + 1)
            act.activation(xhi[:, c, 0:b.T], xs(b, x, c), ACT.Copy, scale=gain(col, l, c)).then_inc(b.s.x_hi, 1)
            if c == 0:
                act.activation(acc[:, 0:b.T], xs(b, x, c), ACT.Square).then_inc(b.s.x_squared, 1)
            else:
                if c > 2:
                    act.wait_ge(b.s.x_summed, 7 * sub + c - 2)
                act.activation(sq[c % 2][:, 0:b.T], xs(b, x, c), ACT.Square).then_inc(b.s.x_squared, 1)

        def dve_operand_lo(dve, b, l, sub, col, c):
            dve.wait_ge(b.s.x_hi, 8 * sub + c + 1)
            dve.scalar_tensor_tensor(out=xlo[:, c, 0:b.T], in0=xs(b, x, c), scalar=gain(col, l, c),
                                     in1=xhi[:, c, 0:b.T].bitcast(F32), op0=ALU.mult,
                                     op1=ALU.subtract).then_inc(b.s.x_lo, 1)

        def pool_x(pool, b, sub):
            for c in range(1, KD):
                pool.wait_ge(b.s.x_squared, 8 * sub + c + 1)
                if c > 1:
                    pool.wait_ge(b.s.x_summed, 7 * sub + c - 1)
                pool.tensor_tensor(acc[:, 0:b.T], acc[:, 0:b.T], sq[c % 2][:, 0:b.T], ALU.add).then_inc(b.s.x_summed, 1)

        def pool_y(pool, b, sub):
            for c in range(1, KD - 2):
                pool.wait_ge(b.s.y_squared, 8 * sub + c + 1)
                if c > 1:
                    pool.wait_ge(b.s.y_summed, 5 * sub + c - 1)
                pool.tensor_tensor(acc[:, 0:b.T], acc[:, 0:b.T], sq[c % 2][:, 0:b.T], ALU.add).then_inc(b.s.y_summed, 1)

        def act_yevac(act, b, sub, m):
            for o in range(2):
                c = 2 * m + o
                bank = 4 * (m % 2) + 2 * o
                act.activation(tview(b, y[:, c, 0:b.T]), pview(b, bank), ACT.Copy)
                if c > 2:
                    act.wait_ge(b.s.y_summed, 5 * sub + min(c - 2, 5))
                dst = acc if c == 0 else sq[c % 2]
                ins = act.activation(tview(b, dst[:, 0:b.T]), pview(b, bank), ACT.Square)
                ins.then_inc(b.s.y_squared, 1)
            act.wait_ge(b.s.y_squared, 8 * sub + 2 * m + 2)
            act.sem_inc(b.s.out_free, 1)

        def dve_residual(dve, b, l, sub, ch, factor, post, pre):
            dve.wait_ge(b.s.norm_spread, 2 * sub + 2)
            for c in range(KD + 1):
                if c < KD:
                    ch(dve.scalar_tensor_tensor(out=tview(b, tt[c % 2][:, 0:b.T]), in0=tview(b, y[:, c, 0:b.T]),
                                                scalar=factor, in1=pview(b, BC_POST), op0=ALU.mult, op1=ALU.mult))
                    ch.wait()
                    dve.scalar_tensor_tensor(out=xs(b, x, c), in0=tt[c % 2][:, 0:b.T], scalar=gain(post, l, c),
                                             in1=xs(b, x, c), op0=ALU.mult, op1=ALU.add).then_inc(b.s.x_new, 1)
                if c > 0 and pre is not None:
                    dve_operand_lo(dve, b, l, sub + 1, pre, c - 1)

        def sp_ffn(sp, b, l, f):
            with sp.Fori(0, UP_ITERS) as i:
                for q in range(4):
                    W = f.gate if q < 2 else f.up
                    src = W[bass.ds(l * D + (q % 2) * 512, 512), bass.ds(i * PAIR + f.upoff * (q // 2), PAIR)]
                    load_raw(sp, b, f.gb(l) + 4 * i + q, q % 2, src, (4, PAIR))
            for m in range(DOWN_PAIRS):
                for q, k in enumerate(DOWN_Q):
                    src = f.down[bass.ds(l * FF + q * 512, k * P), m * PAIR:(m + 1) * PAIR]
                    load_raw(sp, b, f.gb(l) + UP_GRAN + 6 * m + q, q % 2, src, (k, PAIR))

        def pe_up_granule(pe, b, l, f, i, q, between=None):
            g = f.gb(l) + 4 * i + q
            pe.wait_ge(b.s.weights_split, g + 1 + CR)
            first = q % 2 == 0
            if first:
                pe.wait_ge(b.s.hidden_free, f.ev(l) + 2 * i + q // 2 + 1)
            for o in range(2):
                for kk in range(4):
                    k = 4 * (q % 2) + kk
                    if isinstance(i, int) and i == 0 and q < 2 and o == 0:
                        pe.wait_ge(b.s.x_lo, 8 * f.sub(l) + k + 1)
                    ins = tile_mm(pe, b, 4 * (q // 2) + 2 * o, q % 2, kk * PAIR + o * P,
                                  xhi[:, k, :], xlo[:, k, :], first and kk == 0, not first and kk == 3)
                if o == 0 and between is not None:
                    between()
            ins.then_inc(b.s.granules_done, 1)

        def pe_out(pe, b, l, sub, gb, qs, hi, lo, ready):
            nq = len(qs)

            def pair_of(base, m, mi):
                pe.wait_ge(b.s.out_free, 4 * sub + base + m + 1)
                for q, kn in enumerate(qs):
                    pe.wait_ge(b.s.weights_split, gb + nq * (base + m) + q + 1 + CR)
                    for kk in range(kn):
                        k = 4 * q + kk
                        if ready is not None and mi == 0 and m == 0:
                            ready(k)
                        for o in range(2):
                            ins = tile_mm(pe, b, 4 * m + 2 * o, q % 2, kk * PAIR + o * P, hi[:, k, :], lo[:, k, :],
                                          q == 0 and kk == 0, q == nq - 1 and kk == kn - 1)
                    ins.then_inc(b.s.granules_done, 1)

            for mi in range(2):
                for m in range(2):
                    pair_of(2 * mi, m, mi)

        def pe_post(pe, b, sub):
            pe.wait_ge(b.s.y_squared, 8 * sub + 8)
            pe.wait_ge(b.s.y_summed, 5 * sub + 5)
            pe_sum(pe, b, 2 * sub + 1, SUM_POST, [acc, sq[0], sq[1]])
            pe_bc(pe, b, 2 * sub + 1, BC_POST)

        def pe_pre_sum(pe, b, sub):
            pe.wait_ge(b.s.x_summed, 7 * sub + 7)
            pe_sum(pe, b, 2 * sub, SUM_PRE, [acc])

        def pe_ffn(pe, b, l, f):
            sub = f.sub(l)
            pe.wait_ge(b.s.out_free, 4 * sub + CR)
            pe_up_granule(pe, b, l, f, 0, 0)
            pe_up_granule(pe, b, l, f, 0, 1, lambda: pe_pre_sum(pe, b, sub))
            pe_bc(pe, b, 2 * sub, BC_PRE)
            pe.wait_ge(b.s.norm_r, sub + 1)
            pe_up_granule(pe, b, l, f, 0, 2)
            pe_up_granule(pe, b, l, f, 0, 3)
            with pe.Fori(1, UP_ITERS) as i:
                for q in range(4):
                    pe_up_granule(pe, b, l, f, i, q)
            pe.wait_ge(b.s.hidden_free, f.ev(l) + 2 * UP_ITERS + CR)
            pe_out(pe, b, l, sub, f.gb(l) + UP_GRAN, DOWN_Q, hhi, hlo,
                   lambda k: pe.wait_ge(b.s.hidden_lo, f.hb(l) + k + 1))
            pe_post(pe, b, sub)

        def act_ffn(act, b, l, f, nxt):
            sub, gb = f.sub(l), f.gb(l)

            def hi_split(i, q):
                split_hi(act, b, gb + 4 * i + q, f.gb2(l) + 2 * i + q // 2, q % 2)

            def first_tap(i, up):
                for o in range(2):
                    act.wait_ge(b.s.up_in, 2 * f.hb(l) + 4 * i + 2 * up + o + 1)
                    act.activation(S[2 + 2 * up + o][:, 0:b.T], S[o][:, 2:2 + b.T], ACT.Copy,
                                   scale=tap(l, 2, 2 * i + o, up)).then_inc(b.s.last_tap, 1)

            def silu(i):
                if b.conv:
                    first_tap(i, 0)
                for o in range(2):
                    act.wait_ge(b.s.gate_in, f.hb(l) + 2 * i + o + 1)
                    act.activation(S[2 + o][:, 0:b.T], S[2 + o][:, 0:b.T], ACT.Silu).then_inc(b.s.silu_done, 1)

            def hidden(i):
                if b.conv:
                    first_tap(i, 1)
                for o in range(2):
                    act.wait_ge(b.s.hidden_done, f.hb(l) + 2 * i + o + 1)
                    act.activation(hhi[:, bass.ds(2 * i + o, 1), 0:b.T].rearrange("p a t -> p (a t)"),
                                   S[4 + o][:, 0:b.T], ACT.Copy).then_inc(b.s.hidden_hi, 1)

            hi_split(0, 2)
            act_rms(act, b, 2 * sub, SUM_PRE)
            act_r(act, b, 2 * sub, BC_PRE)
            hi_split(0, 3)
            silu(0)
            hi_split(1, 0)
            hi_split(1, 1)
            hidden(0)
            with act.Fori(1, UP_ITERS) as i:
                hi_split(i, 2)
                hi_split(i, 3)
                silu(i)
                hi_split(i + 1, 0)
                hi_split(i + 1, 1)
                hidden(i)
            act_out(act, b, l, sub, gb + UP_GRAN, f.gb2(l) + UP_GRAN // 2, DOWN_Q)
            act_rms(act, b, 2 * sub + 1, SUM_POST)
            if nxt is not None:
                act_next(act, b, l, sub + 1, *nxt)

        def act_out(act, b, l, sub, gb, gb2, qs):
            nq = len(qs)
            n = DOWN_PAIRS * nq
            for j in range(n):
                if j + 2 < n:
                    split_hi(act, b, gb + j + 2, gb2 + j // 2 + 1, j % 2, qs[(j + 2) % nq] * PAIR)
                if j % nq == nq - 1:
                    act.wait_ge(b.s.granules_done, gb + j + 1 + CR)
                    act_yevac(act, b, sub, j // nq)

        def act_next(act, b, l, sub, col, gb, gb2):
            for j in range(2):
                split_hi(act, b, gb(l) + j, gb2(l), j)
            for c in range(KD):
                act_operand(act, b, l, sub, col, c)

        def dve_ffn(dve, b, l, f, ch, factor, post, nxt):
            sub, gb = f.sub(l), f.gb(l)

            def lo_split(i, q):
                split_lo(dve, b, gb + 4 * i + q, q % 2)

            def conv(i, up):
                for o in range(2):
                    dve.tensor_tensor(tview(b, S[o][:, 2:2 + b.T]), pview(b, 4 * up + 2 * o), tview(b, r[:, 0:b.T]),
                                      ALU.mult).then_inc(b.s.up_in, 1)
                dve.wait_ge(b.s.up_in, 2 * f.hb(l) + 4 * i + 2 * up + 2)
                dve.sem_inc(b.s.hidden_free, 1)
                for k in (1, 0):
                    for o in range(2):
                        c_ = S[2 + 2 * up + o][:, 0:b.T]
                        if k:
                            dve.wait_ge(b.s.last_tap, 2 * f.hb(l) + 4 * i + 2 * up + o + 1)
                        ins = dve.scalar_tensor_tensor(out=c_, in0=S[o][:, k:k + b.T], scalar=tap(l, k, 2 * i + o, up),
                                                       in1=c_, op0=ALU.mult, op1=ALU.add)
                        if k == 0 and not up:
                            ins.then_inc(b.s.gate_in, 1)
                        else:
                            ch(ins)
                    if k or up:
                        ch.wait()

            def gate(i):
                dve.wait_ge(b.s.granules_done, gb + 4 * i + 2 + CR)
                if b.conv:
                    return conv(i, 0)
                for o in range(2):
                    ins = dve.tensor_tensor(tview(b, S[2 + o][:, 0:b.T]), pview(b, 2 * o), tview(b, r[:, 0:b.T]),
                                            ALU.mult).then_inc(b.s.gate_in, 1)
                dve.wait_ge(b.s.gate_in, f.hb(l) + 2 * i + 2)
                dve.sem_inc(b.s.hidden_free, 1)

            def up(i):
                dve.wait_ge(b.s.granules_done, gb + 4 * i + 4 + CR)
                if b.conv:
                    conv(i, 1)
                else:
                    for o in range(2):
                        ch(dve.tensor_tensor(tview(b, S[4 + o][:, 0:b.T]), pview(b, 4 + 2 * o),
                                             tview(b, r[:, 0:b.T]), ALU.mult))
                    ch.wait()
                    dve.sem_inc(b.s.hidden_free, 1)
                for o in range(2):
                    dve.wait_ge(b.s.silu_done, f.hb(l) + 2 * i + o + 1)
                    dve.tensor_tensor(S[4 + o][:, 0:b.T], S[4 + o][:, 0:b.T], S[2 + o][:, 0:b.T],
                                      ALU.mult).then_inc(b.s.hidden_done, 1)
                for o in range(2):
                    dve.wait_ge(b.s.hidden_hi, f.hb(l) + 2 * i + o + 1)
                    h = bass.ds(2 * i + o, 1)
                    dve.tensor_tensor(hlo[:, h, 0:b.T].rearrange("p a t -> p (a t)"), S[4 + o][:, 0:b.T],
                                      hhi[:, h, 0:b.T].rearrange("p a t -> p (a t)").bitcast(F32),
                                      ALU.subtract).then_inc(b.s.hidden_lo, 1)

            lo_split(0, 2)
            dve_diag(dve, b, 2 * sub, ch)
            lo_split(0, 3)
            dve.wait_ge(b.s.norm_r, sub + 1)
            if b.conv:
                for o in range(2):
                    ch(dve.memset(S[o][:, 0:2], 0.0))
            gate(0)
            lo_split(1, 0)
            lo_split(1, 1)
            up(0)
            per = 6 if b.conv else 2
            with dve.Fori(1, UP_ITERS) as i:
                base, n0 = ch.base, ch.n
                ch.base = base + (i - 1) * per
                lo_split(i, 2)
                lo_split(i, 3)
                gate(i)
                lo_split(i + 1, 0)
                lo_split(i + 1, 1)
                up(i)
                assert ch.n == n0 + per, ch.n - n0
            ch.base, ch.n = base, n0 + per * (UP_ITERS - 1)
            dve_out(dve, b, l, sub, gb + UP_GRAN, DOWN_Q, ch, factor, post, nxt)

        def dve_out(dve, b, l, sub, gb, qs, ch, factor, post, nxt):
            nq = len(qs)
            for j in range(DOWN_PAIRS * nq - 2):
                split_lo(dve, b, gb + j + 2, j % 2, qs[(j + 2) % nq] * PAIR)
            dve_diag(dve, b, 2 * sub + 1, ch)
            if nxt is not None:
                for j in range(2):
                    split_lo(dve, b, nxt[1](l) + j, j)
            dve_residual(dve, b, l, sub, ch, factor, post, None if nxt is None else nxt[0])

        def dve_first(dve, b, l, sub, col, gb):
            for j in range(2):
                split_lo(dve, b, gb(l) + j, j)
            for c in range(KD):
                dve_operand_lo(dve, b, l, sub, col, c)

        def tap(l, k, chunk, up):
            return par[:, bass.ds(l * 44 + chunk + (PAR_FCW + 88 * k + 22 * up), 1)]

        def ffn1(which):
            g0 = 0 if which == 0 else FFN_GRAN + MIX1_GRAN
            return Ffn(
                sub=lambda l: l * 3 + 2 * which, gb=lambda l: l * b1.GL + g0, gb2=lambda l: l * (b1.GL // 2) + g0 // 2,
                ev=lambda l: l * b1.evf_layer + 2 * UP_ITERS * which, hb=lambda l: l * 2 * KF + KF * which,
                gate=I[f"ffn{which + 1}_w_gate"].rearrange("l d f -> (l d) f"),
                up=I[f"ffn{which + 1}_w_up"].rearrange("l d f -> (l d) f"), upoff=0,
                down=I[f"ffn{which + 1}_w_down"].rearrange("l f d -> (l f) d"))

        f1, f2 = ffn1(0), ffn1(1)
        mgb = lambda l: l * b1.GL + FFN_GRAN
        mgb2 = lambda l: l * (b1.GL // 2) + FFN_GRAN // 2
        win1 = I["w_in"].rearrange("l d f -> (l d) f")
        wout1 = I["w_out"].rearrange("l d f -> (l d) f")

        def sp_mix1(sp, l):
            b = b1
            for p in range(8):
                for j in range(3):
                    g = 3 * p + j
                    src = win1[bass.ds(l * D, D), QKV1[p][j]:QKV1[p][j] + P]
                    load_raw(sp, b, mgb(l) + g, g % 2, src, (8, P))
                if p == 0:
                    sp.wait_ge(b.s.x_new, 8 * (l * 3 + 1) + 8)
                    sp.wait_ge(s_tbias, 16)
                    sp.dma_start(tb, tbias_dram[bass.ds(l * 6, 6), :, :].rearrange("h p c -> p h c")).then_inc(s_tb, 16)
            sp_wout(sp, b, l, mgb(l) + 24, wout1)

        def sp_wout(sp, b, l, gb, W):
            for m in range(DOWN_PAIRS):
                for q in range(2):
                    src = W[bass.ds(l * D + q * 512, 512), m * PAIR:(m + 1) * PAIR]
                    load_raw(sp, b, gb + 2 * m + q, q, src, (4, PAIR))

        def sbank(u):
            kind = KINDS[u // 8]
            return 4 + 2 * (u % 2) + ((u // 2) % 2 if kind == "C" else 0)

        def unit1(u):
            p, h, j = u // 8, (u // 4) % 2, u % 4
            return p, h, j, KINDS[p], P * (j + 1)

        def pe_mix1(pe, l):
            b, s = b1, b1.s
            sub = l * 3 + 1
            U = l * UNITS1

            def gtile(g, t):
                if t == 0:
                    pe.wait_ge(s.weights_split, mgb(l) + g + 1 + CR)
                    pe.wait_ge(s.columns_out, l * 24 + g + 1)
                if g == 0:
                    pe.wait_ge(s.x_lo, 8 * sub + t + 1)
                ins = tile_mm(pe, b, g % 2, g % 2, t * P, xhi[:, t, :], xlo[:, t, :], t == 0, t == 7)
                if t == 7:
                    ins.then_inc(s.granules_done, 1)

            def scores(u):
                p, h, j, kind, n = unit1(u)
                pe.wait_ge(s.columns_out, l * 24 + 3 * p + 2 + CR)
                back = 4 if kind == "C" and u >= 44 else 2
                pe.wait_ge(s.scores_free, U + u + 1 + CR - back)
                maps = 2 if kind == "B" else 1
                rows = 64 // maps
                for m in range(maps):
                    a = 64 * h + rows * m
                    ins = pe.matmul(ps[:, sbank(u) + m, 0:n], m1.q[p % 2][a:a + rows, P * j:P * j + P],
                                    m1.k[p % 2][a:a + rows, 0:n], start=True, stop=True)
                ins.then_inc(s.scores_done, 1)

            def vtrans(p):
                e = TEV1["v", p]
                pe.wait_ge(s.columns_out, l * 24 + 3 * p + 3 + CR)
                pe.wait_ge(s.transposed_out, l * len(TEV1) + e + 1)
                for t in range(4):
                    ins = pe.transpose(ps[:, 2, P * t:P * t + P], m1.vt[p % 2][:, P * t:P * t + P], ident[:, :])
                ins.then_inc(s.transposed, 1)

            def ptrans(u):
                p, h, j, kind, n = unit1(u)
                pe.wait_ge(s.probs_done, U + u + 1)
                pe.wait_ge(s.transposed_out, l * len(TEV1) + TEV1["p", u] + 1)
                for t in range(j + 1):
                    ins = pe.transpose(ps[:, 2, P * t:P * t + P], m1.w[u % 3][:, 0, P * t:P * t + P], ident[:, :])
                ins.then_inc(s.transposed, 1)

            def pv(u):
                p, h, j, kind, n = unit1(u)
                pe.wait_ge(s.transposed_out, l * len(TEV1) + TEV1["p", u] + 2)
                if u % 8 == 0:
                    pe.wait_ge(s.o_hi_out, l * 8 + p + 1)
                    pe.wait_ge(s.o_lo_out, l * 8 + p + 1)
                for t in range(j + 1):
                    ins = pe.matmul(ps[64 * h:64 * h + 64, 3, P * j:P * j + P], m1.v[p % 2][:, t, 64 * h:64 * h + 64],
                                    m1.pt[u % 2][:, t, :], start=(t == 0), stop=(t == j))
                ins.then_inc(s.pv_done, 1)

            pe.wait_ge(s.out_free, 4 * sub + CR)
            for g in range(3):
                for t in range(8):
                    gtile(g, t)
                if g == 0:
                    pe_pre_sum(pe, b, sub)
                if g == 1:
                    pe_bc(pe, b, 2 * sub, BC_PRE)
            pe.wait_ge(s.norm_r, sub + 1)
            for st in STEPS1:
                if st.vt is not None:
                    vtrans(st.vt)
                if st.sc is not None:
                    scores(st.sc)
                for gt_ in st.tiles[:-1]:
                    gtile(*gt_)
                for u in st.tr:
                    ptrans(u)
                for gt_ in st.tiles[-1:]:
                    gtile(*gt_)
                for u in st.tr:
                    pv(u)
            pe.wait_ge(s.b_act_steps, ACT1[0] + l * ACT1_LAYER)
            for c in range(2):
                ins = pe.matmul(ps[:, 4 + c, 0:SEQ], bd[:, :], m1.sqb[:, c, :], start=True, stop=True)
            ins.then_inc(s.b_sums, 1)
            pe.wait_ge(s.o_lo_out, l * 8 + 9)
            pe.wait_ge(s.o_hi_out, l * 8 + 9)
            pe.wait_ge(s.b_lo, l + 1)
            pe_out(pe, b, l, sub, mgb(l) + 24, OUT_Q, m1.ohi, m1.olo, None)
            pe_post(pe, b, sub)

        ACT1 = [1]
        ACT1_LAYER = 3

        def act_mix1(act, l, nxt):
            b, s = b1, b1.s
            sub = l * 3 + 1
            U = l * UNITS1

            def hi_split(g):
                split_hi(act, b, mgb(l) + g, mgb2(l) + g // 2, g % 2)

            hi_split(2)
            act_rms(act, b, 2 * sub, SUM_PRE)
            act_r(act, b, 2 * sub, BC_PRE)
            hi_split(3)
            hi_split(4)
            for st in STEPS1:
                if st.vt is not None:
                    act.wait_ge(s.transposed, l * len(TEV1) + TEV1["v", st.vt] + 1)
                    act.activation(m1.v[st.vt % 2][:, :, :].rearrange("p a b -> p (a b)"), ps[:, 2, :],
                                   ACT.Copy).then_inc(s.transposed_out, 1)
                u = st.sc
                if u is not None:
                    p, h, j, kind, n = unit1(u)
                    if kind in "AB":
                        act.wait_ge(s.max_done, l * 40 + u + 1)
                        for m in range(2 if kind == "B" else 1):
                            w = m1.w[u % 3][:, m, 0:n]
                            ins = act.activation(w, w, ACT.Exp, bias=m1.nmax[u % 3][:, m:m + 1],
                                                 scale=B_SCALE if kind == "B" else 1.0,
                                                 accum_out=m1.sums[u % 3][:, m:m + 1])
                        ins.then_inc(s.exp_done, 1)
                    else:
                        e = m1.e[u % 2][:, 0:n]
                        c = l * 24 + (u - 40)
                        act.wait_ge(s.scores_done, U + u + 1)
                        if u >= 42:
                            act.wait_ge(s.softplus_read, l * 24 + u - 41)
                        act.activation(e, ps[:, sbank(u), 0:n], ACT.Abs).then_inc(s.softplus_steps, 1)
                        act.wait_ge(s.softplus_steps, 2 * c + 1)
                        act.activation(e, e, ACT.Exp, scale=-1.0).then_inc(s.softplus_steps, 1)
                        act.wait_ge(s.softplus_steps, 2 * c + 2)
                        act.activation(e, e, ACT.Ln, bias=1.0).then_inc(s.exp_done, 1)
                for v in st.tr:
                    act.wait_ge(s.transposed, l * len(TEV1) + TEV1["p", v] + 1)
                    if v >= 2:
                        act.wait_ge(s.pv_done, U + v - 1)
                    nn = unit1(v)[4]
                    act.activation(m1.pt[v % 2][:, :, :].rearrange("p a b -> p (a b)")[:, 0:nn], ps[:, 2, 0:nn],
                                   ACT.Copy).then_inc(s.transposed_out, 1)
                if u is not None and kind == "C":
                    w = m1.w[u % 3][:, 0, 0:n]
                    act.wait_ge(s.stick_logits, l * 24 + (u - 40) + 1)
                    act.activation(w, w, ACT.Exp).then_inc(s.probs_done, 1)
                for p_ in st.pairs:
                    act.wait_ge(s.pv_done, U + 8 * p_ + 8)
                    if KINDS[p_] == "B":
                        act.activation(m1.ob[:, p_ - 3, :], ps[:, 3, :], ACT.Copy).then_inc(s.o_hi_out, 1)
                        if p_ == 4:
                            act.wait_ge(s.o_hi_out, l * 8 + p_ + 2)
                            act.activation(m1.sqb[:, :, :], m1.ob[:, :, :], ACT.Square).then_inc(s.b_act_steps, 1)
                    else:
                        act.activation(m1.ohi[:, p_, :], ps[:, 3, :], ACT.Copy).then_inc(s.o_hi_out, 1)
                for g in st.done:
                    if g + 2 < 24 + 8:
                        hi_split(g + 2)
            act.wait_ge(s.b_sums, l + 1)
            act.activation(m1.rb[:, :, :], ps[:, 4:6, 0:SEQ], ACT.Ln, bias=eps[:, :], scale=1.0 / 64).then_inc(s.b_act_steps, 1)
            act.wait_ge(s.b_act_steps, l * ACT1_LAYER + 2)
            act.activation(m1.rb[:, :, :], m1.rb[:, :, :], ACT.Exp, scale=-0.5).then_inc(s.b_act_steps, 1)
            act.wait_ge(s.b_scaled, l + 1)
            for c in range(2):
                ins = act.activation(m1.ohi[:, 3 + c, :], m1.ob[:, c, :], ACT.Copy,
                                     scale=par[:, bass.ds(l + PAR_SUBLN, 1)])
            ins.then_inc(s.b_hi, 1)
            act_out(act, b, l, sub, mgb(l) + 24, mgb2(l) + 12, OUT_Q)
            act_rms(act, b, 2 * sub + 1, SUM_POST)
            act_next(act, b, l, sub + 1, *nxt)

        def dve_mix1(dve, l, ch, nxt):
            b, s = b1, b1.s
            sub = l * 3 + 1
            U = l * UNITS1

            def lo_split(g):
                split_lo(dve, b, mgb(l) + g, g % 2)

            def evac(g):
                p, j = divmod(g, 3)
                dve.wait_ge(s.granules_done, mgb(l) + g + 1 + CR)
                dst = (m1.q, m1.k, m1.vt)[j][p % 2]
                factor = 0.125 if j == 0 and KINDS[p] != "B" else 1.0
                dve.scalar_tensor_tensor(out=dst[:, :], in0=ps[:, g % 2, :], scalar=factor, in1=r[:, 0:SEQ],
                                         op0=ALU.mult, op1=ALU.mult).then_inc(s.columns_out, 1)

            lo_split(2)
            dve_diag(dve, b, 2 * sub, ch)
            dve.wait_ge(s.norm_r, sub + 1)
            evac(0)
            lo_split(3)
            evac(1)
            lo_split(4)
            evac(2)
            dve.wait_ge(s_tb, 16 * l + 16)
            ch(dve.memset(tb[0:64, :, SEQ - 64:SEQ], NEG))
            ch.wait()
            for st in STEPS1:
                u = st.sc
                if u is not None:
                    p, h, j, kind, n = unit1(u)
                    w3 = m1.w[u % 3]
                    w = w3[:, 0, 0:n]
                    S_ = ps[:, sbank(u), 0:n]
                    dve.wait_ge(s.scores_done, U + u + 1)
                    if u >= 3:
                        dve.wait_ge(s.transposed, l * len(TEV1) + TEV1["p", u - 3] + 1)
                    if kind == "A":
                        head = 2 * p + h
                        ch(dve.tensor_tensor(w, S_, tb[:, head, SEQ - n:SEQ], ALU.add))
                        ch.wait()
                        dve.sem_inc(s.scores_free, 1)
                        dve.tensor_reduce(m1.nmax[u % 3][:, 0:1], w, AX.X, ALU.max, negate=True).then_inc(s.max_done, 1)
                        dve.wait_ge(s.exp_done, U + u + 1)
                        ch(dve.reciprocal(m1.inv[u % 3][:, 0:1], m1.sums[u % 3][:, 0:1]))
                        ch.wait()
                        dve.tensor_scalar(w, w, m1.inv[u % 3][:, 0:1], None, ALU.mult).then_inc(s.probs_done, 1)
                    elif kind == "B":
                        head = 2 * (p - 3) + h
                        for m in range(2):
                            ch(dve.scalar_tensor_tensor(
                                out=w3[:, m, 0:n], in0=dist[:, SEQ - n:SEQ], scalar=-SLOPE[head] / B_SCALE,
                                in1=ps[:, sbank(u) + m, 0:n], op0=ALU.mult, op1=ALU.add))
                        ch.wait()
                        dve.sem_inc(s.scores_free, 1)
                        ch(dve.tensor_reduce(m1.nmax[u % 3][:, 0:2], w3[:, :, 0:n], AX.X, ALU.max, negate=True))
                        ch.wait()
                        dve.tensor_scalar(m1.nmax[u % 3][:, 0:2], m1.nmax[u % 3][:, 0:2], B_SCALE, None,
                                          ALU.mult).then_inc(s.max_done, 1)
                        dve.wait_ge(s.exp_done, U + u + 1)
                        ch(dve.reciprocal(m1.inv[u % 3][:, 0:2], m1.sums[u % 3][:, 0:2]))
                        ch.wait()
                        ch(dve.tensor_tensor(m1.c1[u % 3][:, :], m1.inv[u % 3][:, 1:2],
                                             nlam[:, bass.ds(l, 1)], ALU.mult))
                        ch.wait()
                        ch(dve.tensor_scalar(w3[:, 1, 0:n], w3[:, 1, 0:n], m1.c1[u % 3][:, 0:1], None, ALU.mult))
                        ch.wait()
                        dve.scalar_tensor_tensor(out=w, in0=w, scalar=m1.inv[u % 3][:, 0:1], in1=w3[:, 1, 0:n],
                                                 op0=ALU.mult, op1=ALU.add).then_inc(s.probs_done, 1)
                    else:
                        c = u - 40
                        sp_, sc_ = m1.sp[:, 0:n], m1.scan[:, 0:n]
                        dve.wait_ge(s.exp_done, U + u + 1)
                        ch(dve.scalar_tensor_tensor(out=sp_, in0=S_, scalar=0.0, in1=m1.e[u % 2][:, 0:n],
                                                    op0=ALU.max, op1=ALU.add))
                        ch.wait()
                        dve.sem_inc(s.softplus_read, 1)
                        ch(dve.tensor_tensor(m1.sp[:, n - P:n], m1.sp[:, n - P:n], strict[:, :], ALU.mult))
                        ch.wait()
                        ch(dve.tensor_tensor_scan(sc_[:, ::-1], ones[:, 0:n], sp_[:, ::-1], 0.0, ALU.mult, ALU.add))
                        ch.wait()
                        ch(dve.tensor_tensor(w, S_, sc_, ALU.subtract))
                        ch.wait()
                        dve.sem_inc(s.scores_free, 1)
                        dve.tensor_tensor(m1.w[u % 3][:, 0, n - P:n], m1.w[u % 3][:, 0, n - P:n], negs[:, :],
                                          ALU.add).then_inc(s.stick_logits, 1)
                for g in st.done:
                    if g + 2 < 24 + 8:
                        lo_split(g + 2)
                    evac(g)
                for p_ in st.pairs:
                    if KINDS[p_] == "B":
                        dve.wait_ge(s.o_hi_out, l * 8 + p_ + 2)
                        dve.sem_inc(s.o_lo_out, 1)
                    else:
                        dve.wait_ge(s.o_hi_out, l * 8 + p_ + 2)
                        dve.tensor_tensor(m1.olo[:, p_, :], ps[:, 3, :], m1.ohi[:, p_, :].bitcast(F32),
                                          ALU.subtract).then_inc(s.o_lo_out, 1)
            dve.wait_ge(s.b_act_steps, l * ACT1_LAYER + 3)
            dve.tensor_tensor(m1.ob[:, :, :], m1.ob[:, :, :], m1.rb[:, :, :], ALU.mult).then_inc(s.b_scaled, 1)
            dve.wait_ge(s.b_scaled, l + 1)
            dve.wait_ge(s.b_hi, l + 1)
            dve.scalar_tensor_tensor(out=m1.olo[:, 3:5, :], in0=m1.ob[:, :, :],
                                     scalar=par[:, bass.ds(l + PAR_SUBLN, 1)],
                                     in1=m1.ohi[:, 3:5, :].bitcast(F32), op0=ALU.mult,
                                     op1=ALU.subtract).then_inc(s.b_lo, 1)
            dve_out(dve, b, l, sub, mgb(l) + 24, OUT_Q, ch, 1.0, PAR_MIXPOST, nxt)


        fg = Ffn(
            sub=lambda l: l * 2 + 1, gb=lambda l: l * b2.GL + MIX2_GRAN, gb2=lambda l: l * (b2.GL // 2) + MIX2_GRAN // 2,
            ev=lambda l: l * b2.evf_layer, hb=lambda l: l * KF,
            gate=I["ffn_w_up_2"].rearrange("l d f -> (l d) f"), up=I["ffn_w_up_2"].rearrange("l d f -> (l d) f"),
            upoff=FF, down=I["ffn_w_down_2"].rearrange("l f d -> (l f) d"))
        g2b = lambda l: l * b2.GL
        g2b2 = lambda l: l * (b2.GL // 2)
        win2 = I["w_in_2"].rearrange("l d f -> (l d) f")
        wout2 = I["w_out_2"].rearrange("l d f -> (l d) f")
        pw2 = I["a_pw_w_2"].rearrange("l d f -> (l d) f")
        NCOL = len(COLS2)

        def sp_mix2(sp, l):
            for g, c0 in enumerate(COLS2):
                row = l * D if c0 else l * KD * P
                load_raw(sp, b2, g2b(l) + g, g % 2, win2[bass.ds(row, D), c0:c0 + P], (8, P))
            load_raw(sp, b2, g2b(l) + NCOL, NCOL % 2, pw2[bass.ds(l * 2 * P, 2 * P), :], (2, PAIR))
            sp_wout(sp, b2, l, g2b(l) + NCOL + 1, wout2)

        def n_of(g):
            return 512 if g == NCOL else 1024

        def unit2(u):
            p, qb, h = u // (2 * QB), (u // 2) % QB, u % 2
            return p, qb, h, (0 if qb == 0 else META + P * (qb - 1)), (META if qb == 0 else P), META + P * qb

        def s2(u, n):
            bank = 4 + 2 * (u % 2)
            return ps[:, bank:bank + 2, :].rearrange("p a b -> p (a b)")[:, SEQ - META:SEQ - META + n]

        HEADS_ORDER = [0, 1, 2, 3, 6, 7, 4, 5]

        def pe_mix2(pe, l):
            b, s = b2, b2.s
            sub = l * 2
            U = l * UNITS2
            TE = l * len(TEV2)

            def gtile(g, t):
                if t == 0:
                    pe.wait_ge(s.weights_split, g2b(l) + g + 1 + CR)
                    if g >= 2:
                        pe.wait_ge(s.columns_out, l * NCOL + g + CR)
                if g == 0:
                    pe.wait_ge(s.x_lo, 8 * sub + t + 1)
                ins = tile_mm(pe, b, 2 if g == 0 else 0, g % 2, t * P, xhi[:, t, :], xlo[:, t, :], t == 0, t == 7)
                if t == 7:
                    ins.then_inc(s.granules_done, 1)

            def scores(u):
                p, qb, h, t0, nq, n = unit2(u)
                pe.wait_ge(s.columns_out, l * NCOL + 3 * p + 7 + CR)
                pe.wait_ge(s.scores_free, U + u + 1)
                bank = 4 + 2 * (u % 2)
                a = 64 * h
                if u % (2 * QB) == 1:
                    pe.wait_ge(s.transposed_out, TE + TEV2["v", p] + 2)
                lhs = m2.q[p % 2][a:a + 64, t0:t0 + P]
                ins = pe.matmul(ps[:, bank, SEQ - META:SEQ], lhs, m2.k[p % 2][a:a + 64, 0:META], start=True, stop=True)
                if qb:
                    ins = pe.matmul(ps[0:nq, bank + 1, 0:P * qb], lhs, m2.k[p % 2][a:a + 64, META:n],
                                    start=True, stop=True)
                ins.then_inc(s.scores_done, 1)

            def vtrans(p):
                pe.wait_ge(s.columns_out, l * NCOL + 3 * p + 8 + CR)
                pe.wait_ge(s.transposed_out, TE + TEV2["v", p] + 1)
                pe.wait_ge(s.scores_free, U + 2 * QB * p + CR)
                pe.transpose(ps[0:META, 6, 0:P], m2.vt[p % 2][:, 0:META], ident[:, :])
                for t in range(4):
                    t0 = META + P * t
                    ins = pe.transpose(ps[:, 2, P * t:P * t + P], m2.vt[p % 2][:, t0:t0 + P], ident[:, :])
                ins.then_inc(s.transposed, 1)

            def ptrans(u):
                p, qb, h, t0, nq, n = unit2(u)
                pe.wait_ge(s.probs_done, U + u + 1)
                pe.wait_ge(s.transposed_out, TE + TEV2["p", u] + 1)
                ins = pe.transpose(ps[0:META, 4 + 2 * (u % 2), 0:P], m2.w[u % 3][:, 0:META], ident[:, :])
                for t in range(qb):
                    ins = pe.transpose(ps[:, 2, P * t:P * t + P], m2.w[u % 3][:, META + P * t:META + P * t + P], ident[:, :])
                ins.then_inc(s.transposed, 1)

            def pv(u):
                p, qb, h, t0, nq, n = unit2(u)
                pe.wait_ge(s.transposed_out, TE + TEV2["p", u] + 2)
                if h == 0 and qb < 2:
                    pe.wait_ge(s.o_hi_out, l * 8 + 2 * p + qb + 1)
                c0 = P * max(qb - 1, 0)
                o = ps[64 * h:64 * h + 64, 3, c0:c0 + nq]
                ins = pe.matmul(o, m2.v[p % 2][0:META, 0, 64 * h:64 * h + 64], m2.pt[u % 2][0:META, 0, 0:nq],
                                start=True, stop=(qb == 0))
                for t in range(qb):
                    ins = pe.matmul(o, m2.v[p % 2][:, 1 + t, 64 * h:64 * h + 64], m2.pt[u % 2][:, 1 + t, :],
                                    start=False, stop=(t == qb - 1))
                ins.then_inc(s.pv_done, 1)

            def forget(h):
                pe.wait_ge(s.forget_sums, l + 1)
                if h >= 2:
                    pe.wait_ge(s.forget_out, l * 8 + h - 1)
                for i, (t0, w) in enumerate(halves(b)):
                    ins = pe.matmul(ps[:, 4 + 2 * (h % 2) + i, 0:w], ident[0:8, h:h + 1].to_broadcast([8, P]), m2.nf[:, t0:t0 + w], start=True, stop=True)
                ins.then_inc(s.forget_spread, 1)

            pe.wait_ge(s.out_free, 4 * sub + CR)
            for g in range(8):
                for t in range(8):
                    gtile(g, t)
                if g == 0:
                    pe_pre_sum(pe, b, sub)
                if g == 1:
                    pe_bc(pe, b, 2 * sub, BC_PRE)
                    pe.wait_ge(s.norm_r, sub + 1)
                if g >= 4:
                    forget(2 * g - 8)
                    forget(2 * g - 7)
            pe.wait_ge(s.forget_out, l * 8 + 8)
            for st in STEPS2:
                if st.vt is not None:
                    vtrans(st.vt)
                if st.sc is not None:
                    scores(st.sc)
                for gt_ in st.tiles[:-1]:
                    gtile(*gt_)
                for u in st.tr:
                    ptrans(u)
                for gt_ in st.tiles[-1:]:
                    gtile(*gt_)
                for u in st.tr:
                    pv(u)
            for j in range(2):
                if j == 0:
                    pe.wait_ge(s.dw_taps, l * len(DW_OPS) + len(DW_OPS))
                else:
                    pe.wait_ge(s.ln_squared, l + 1)
                src = aconv if j == 0 else m2.lsq
                for i, (t0, w) in enumerate(halves(b)):
                    for c in range(2):
                        ins = pe.matmul(ps[:, 4 + 2 * j + i, 0:w], ones[:, 0:P], src[:, c, t0:t0 + w],
                                        start=(c == 0), stop=(c == 1))
                ins.then_inc(s.ln_sums, 1)
            for i, c in enumerate(HEADS_ORDER):
                if i == 6:
                    pe.wait_ge(s.weights_split, g2b(l) + NCOL + 1 + CR)
                    pe.wait_ge(s.a_lo, l + 1)
                    pe.wait_ge(s.o_hi_out, l * 8 + 9)
                    for o in range(2):
                        for k in range(2):
                            ins = tile_mm(pe, b, 2 * o, NCOL % 2, k * PAIR + o * P, m2.ahi[:, k, :], m2.alo[:, k, :],
                                          k == 0, k == 1)
                    ins.then_inc(s.granules_done, 1)
                pe.wait_ge(s.head_squared, l * 8 + i + 1)
                if i >= 2:
                    pe.wait_ge(s.head_steps, 2 * (l * 8 + i - 2) + 1)
                if i == 0:
                    pe.wait_ge(s.ln_centered, l + 1)
                if i == 1:
                    pe.wait_ge(s.ln_steps, l * 2 + 1)
                for j, (t0, w) in enumerate(halves(b)):
                    ins = pe.matmul(ps[:, 4 + 2 * (i % 2) + j, 0:w], bd[:, :], S[i % 2][:, t0:t0 + w], start=True, stop=True)
                ins.then_inc(s.head_sums, 1)
            pe.wait_ge(s.pw_out, l + 1)
            pe.wait_ge(s.head_steps, 2 * (l * 8 + 7) + 1)
            pe_out(pe, b, l, sub, g2b(l) + NCOL + 1, OUT_Q, m2.ohi, m2.olo,
                   lambda k: pe.wait_ge(s.head_lo, l * 8 + HEADS_ORDER.index(k) + 1))
            pe_post(pe, b, sub)

        def act_mix2(act, l, nxt):
            b, s = b2, b2.s
            sub = l * 2
            U = l * UNITS2
            TE = l * len(TEV2)

            def hi_split(g):
                split_hi(act, b, g2b(l) + g, g2b2(l) + g // 2, g % 2, n_of(g))

            def forget(h):
                act.wait_ge(s.forget_spread, l * 8 + h + 1)
                act.activation(tview(b, fb[:, h, :]), pview(b, 4 + 2 * (h % 2)), ACT.Copy).then_inc(s.forget_out, 1)

            hi_split(2)
            act_rms(act, b, 2 * sub, SUM_PRE)
            act_r(act, b, 2 * sub, BC_PRE)
            hi_split(3)
            act.wait_ge(s.forget_in, l + 1)
            act.activation(m2.e[:, :], m2.u[:, :], ACT.Abs).then_inc(s.forget_steps, 1)
            act.wait_ge(s.forget_steps, l * 3 + 1)
            act.activation(m2.e[:, :], m2.e[:, :], ACT.Exp, scale=-1.0).then_inc(s.forget_steps, 1)
            act.wait_ge(s.forget_steps, l * 3 + 2)
            act.activation(m2.e[:, :], m2.e[:, :], ACT.Ln, bias=1.0).then_inc(s.forget_steps, 1)
            for g in range(2, 8):
                hi_split(g + 2)
                if g == 4:
                    act.wait_ge(s.a_gate_in, l + 1)
                    act.activation(aconv[:, :, :], aconv[:, :, :], ACT.Sigmoid).then_inc(s.a_gate_done, 1)
                if g >= 4:
                    forget(2 * g - 8)
                    forget(2 * g - 7)
            for st in STEPS2:
                if st.vt is not None:
                    act.wait_ge(s.transposed, TE + TEV2["v", st.vt] + 1)
                    act.activation(m2.v[st.vt % 2][0:META, 0, :], ps[0:META, 6, 0:P], ACT.Copy)
                    act.activation(m2.v[st.vt % 2][:, 1:QB, :].rearrange("p a b -> p (a b)"), ps[:, 2, :],
                                   ACT.Copy).then_inc(s.transposed_out, 1)
                u = st.sc
                if u is not None:
                    p, qb, h, t0, nq, n = unit2(u)
                    act.wait_ge(s.max_done, U + u + 1)
                    w = m2.w[u % 3][:, 0:n]
                    act.activation(w, w, ACT.Exp, bias=m2.nmax[u % 3][:, :], scale=1.0,
                                   accum_out=m2.sums[u % 3][:, :]).then_inc(s.exp_done, 1)
                for v in st.tr:
                    p, qb, h, t0, nq, n = unit2(v)
                    act.wait_ge(s.transposed, TE + TEV2["p", v] + 1)
                    if v >= 2:
                        act.wait_ge(s.pv_done, U + v - 1)
                    ins = act.activation(m2.pt[v % 2][0:META, 0, :], ps[0:META, 4 + 2 * (v % 2), 0:P], ACT.Copy)
                    if qb:
                        ins = act.activation(m2.pt[v % 2][:, 1:1 + qb, :].rearrange("p a b -> p (a b)"),
                                             ps[:, 2, 0:P * qb], ACT.Copy)
                    ins.then_inc(s.transposed_out, 1)
                    if h == 1 and qb == 0:
                        act.wait_ge(s.pv_done, U + v + 1)
                        act.activation(y[:, p, 0:META], ps[:, 3, 0:META], ACT.Copy).then_inc(s.o_hi_out, 1)
                for p_ in st.pairs:
                    act.wait_ge(s.pv_done, U + 2 * QB * (p_ + 1))
                    act.activation(y[:, p_, META:TM], ps[:, 3, :], ACT.Copy).then_inc(s.o_hi_out, 1)
                for g in st.done:
                    hi_split(g + 2)
            act_heads(act, l)
            act_out(act, b, l, sub, g2b(l) + NCOL + 1, g2b2(l) + (NCOL + 1) // 2, OUT_Q)
            act_rms(act, b, 2 * sub + 1, SUM_POST)
            act_next(act, b, l, sub + 1, *nxt)

        def act_heads(act, l):
            b, s = b2, b2.s

            def square(i):
                c = HEADS_ORDER[i]
                if c < 4:
                    act.wait_ge(s.o_hi_out, l * 8 + 2 * c + 3)
                elif c >= 6:
                    act.wait_ge(s.short_done, l * 2 + c - 5)
                else:
                    act.wait_ge(s.pw_out, l + 1)
                if i >= 2:
                    act.wait_ge(s.head_sums, l * 8 + i - 1)
                act.activation(S[i % 2][:, 0:TM], y[:, c, :], ACT.Square).then_inc(s.head_squared, 1)

            def inverse(i):
                act.wait_ge(s.head_sums, l * 8 + i + 1)
                if i >= 2:
                    act.wait_ge(s.head_scaled, l * 8 + i - 1)
                t = tview(b, S[2 + i % 2][:, 0:TM])
                act.activation(t, pview(b, 4 + 2 * (i % 2)), ACT.Ln, bias=eps[:, :], scale=1.0 / 64).then_inc(s.head_steps, 1)
                act.wait_ge(s.head_steps, 2 * (l * 8 + i) + 1)
                act.activation(t, t, ACT.Exp, scale=-0.5).then_inc(s.head_steps, 1)

            def hi(i):
                c = HEADS_ORDER[i]
                act.wait_ge(s.head_scaled, l * 8 + i + 1)
                act.activation(m2.ohi[:, c, :], y[:, c, :], ACT.Copy, scale=gain(PAR_HEADG, l, c)).then_inc(s.head_hi, 1)

            square(0)
            square(1)
            act.wait_ge(s.ln_centered, l + 1)
            act.activation(m2.lsq[:, :, :], aconv[:, :, :], ACT.Square).then_inc(s.ln_squared, 1)
            act.wait_ge(s.ln_sums, l * 2 + 2)
            t = tview(b, m2.lrs[:, :])
            act.activation(t, pview(b, 6), ACT.Ln, bias=lneps[:, :], scale=1.0 / 256).then_inc(s.ln_steps, 1)
            act.wait_ge(s.ln_steps, l * 2 + 1)
            act.activation(t, t, ACT.Exp, scale=-0.5).then_inc(s.ln_steps, 1)
            inverse(0)
            inverse(1)
            square(2)
            square(3)
            inverse(2)
            inverse(3)
            square(4)
            square(5)
            inverse(4)
            inverse(5)
            act.wait_ge(s.ln_scaled, l + 1)
            for c in range(2):
                ins = act.activation(aconv[:, c, :], aconv[:, c, :], ACT.Silu,
                                     bias=par[:, bass.ds(l * 2 + (PAR_LNB + c), 1)],
                                     scale=par[:, bass.ds(l * 2 + (PAR_LNG + c), 1)])
            ins.then_inc(s.ln_silu, 1)
            act.wait_ge(s.ln_silu, 2 * l + 1)
            act.activation(m2.ahi[:, :, :], aconv[:, :, :], ACT.Copy).then_inc(s.ln_silu, 1)
            for i in range(6):
                if i == 0:
                    act.wait_ge(s.a_lo, l + 1)
                hi(i)
            act.wait_ge(s.granules_done, g2b(l) + NCOL + 1 + CR)
            for o in range(2):
                ins = act.activation(tview(b, y[:, 4 + o, :]), pview(b, 2 * o), ACT.Copy)
            ins.then_inc(s.pw_out, 1)
            split_hi(act, b, g2b(l) + NCOL + 2, g2b2(l) + (NCOL + 1) // 2, (NCOL + 2) % 2)
            for i in (6, 7):
                square(i)
            for i in (6, 7):
                inverse(i)
            for i in (6, 7):
                hi(i)

        def dve_mix2(dve, l, ch, nxt):
            b, s = b2, b2.s
            sub = l * 2
            U = l * UNITS2
            TE = l * len(TEV2)

            def lo_split(g):
                split_lo(dve, b, g2b(l) + g, g % 2, n_of(g))

            def scaled(dst, g, rows=P, factor=None):
                src = ps[0:rows, 2:4, 0:b.w] if g == 0 else ps[0:rows, 0:2, 0:b.w]
                rr = tview(b, r[0:rows, 0:TM])
                if factor is None:
                    return dve.tensor_tensor(tview(b, dst), src, rr, ALU.mult)
                return dve.scalar_tensor_tensor(out=tview(b, dst), in0=src, scalar=factor, in1=rr,
                                                op0=ALU.mult, op1=ALU.mult)

            def evac(g):
                dve.wait_ge(s.granules_done, g2b(l) + g + 1 + CR)
                if g == 0:
                    dst = m2.u[:, :]
                elif g < 5:
                    c = (g - 1) // 2
                    dst = aconv[:, c, :] if g % 2 == 0 else apad[:, c, TAPS - 1:]
                elif g < 17:
                    p, j = divmod(g - 5, 3)
                    dst = (m2.q, m2.k, m2.vt)[j][p % 2][:, :]
                else:
                    dst = (scb[:, :], scc[:, :], scx[:, 2:])[(g - 17) % 3]
                scaled(dst, g, 8 if g == 0 else P, 0.125 if 5 <= g < 17 and (g - 5) % 3 == 0 else None).then_inc(s.columns_out, 1)

            def short_conv(c):
                dve.wait_ge(s.columns_out, l * NCOL + 17 + 3 * c + 3 + CR)
                ch(dve.tensor_tensor(scx[:, 2:], scx[:, 2:], scc[:, :], ALU.mult))
                ch.wait()
                for k in (2, 1, 0):
                    w = par[:, bass.ds(l * 6 + (PAR_SCW + 2 * k + c), 1)]
                    if k == 2:
                        ch(dve.tensor_scalar(scc[:, :], scx[:, 2:2 + TM], w, None, ALU.mult))
                    else:
                        ch(dve.scalar_tensor_tensor(out=scc[:, :], in0=scx[:, k:k + TM], scalar=w, in1=scc[:, :],
                                                    op0=ALU.mult, op1=ALU.add))
                    ch.wait()
                dve.tensor_tensor(y[:, 6 + c, :], scb[:, :], scc[:, :], ALU.mult).then_inc(s.short_done, 1)

            dw_at = [0]

            def depthwise(n):
                for t, c in DW_OPS[dw_at[0]:dw_at[0] + n]:
                    w = par[:, bass.ds(l * 2 * TAPS + (PAR_DW + 2 * t + c), 1)]
                    src, dst = apad[:, c, t:t + TM], aconv[:, c, :]
                    if t == 0:
                        dve.tensor_scalar(dst, src, w, par[:, bass.ds(l * 2 + (PAR_DWB + c), 1)], ALU.mult,
                                          ALU.add).then_inc(s.dw_taps, 1)
                    else:
                        dve.wait_ge(s.dw_taps, l * len(DW_OPS) + 2 * (t - 1) + c + 1)
                        dve.scalar_tensor_tensor(out=dst, in0=src, scalar=w, in1=dst, op0=ALU.mult,
                                                 op1=ALU.add).then_inc(s.dw_taps, 1)
                dw_at[0] += n

            lo_split(2)
            dve_diag(dve, b, 2 * sub, ch)
            ch(dve.memset(apad[:, :, 0:TAPS - 1], 0.0))
            ch(dve.memset(scx[:, 0:2], 0.0))
            dve.wait_ge(s.norm_r, sub + 1)
            evac(0)
            dve.wait_ge(s.columns_out, l * NCOL + 1 + CR)
            dve.tensor_scalar(m2.u[:, :], m2.u[:, :], bf[:, bass.ds(l, 1)], None, ALU.add).then_inc(s.forget_in, 1)
            evac(1)
            lo_split(3)
            dve.wait_ge(s.forget_steps, l * 3 + 3)
            ch(dve.scalar_tensor_tensor(out=m2.lf[:, :], in0=m2.u[:, :], scalar=0.0, in1=m2.e[:, :], op0=ALU.min,
                                        op1=ALU.subtract))
            ch.wait()
            for a, n in ((0, SEQ), (SEQ, META)):
                ch(dve.tensor_tensor_scan(m2.nf[:, a:a + n], ones[0:8, 0:n], m2.lf[:, a:a + n],
                                          0.0 if a == 0 else m2.nf[:, a - 1:a], ALU.mult, ALU.subtract))
                ch.wait()
            dve.sem_inc(s.forget_sums, 1)
            for g in range(2, 8):
                evac(g)
                lo_split(g + 2)
                if g == 4:
                    dve.wait_ge(s.columns_out, l * NCOL + 5 + CR)
                    dve.sem_inc(s.a_gate_in, 1)
                if g == 5:
                    dve.wait_ge(s.a_gate_done, l + 1)
                    ch(dve.tensor_tensor(apad[:, :, TAPS - 1:], apad[:, :, TAPS - 1:], aconv[:, :, :], ALU.mult))
                    ch.wait()
            dve.wait_ge(s.forget_out, l * 8 + 8)
            for n_step, st in enumerate(STEPS2):
                u = st.sc
                if u is not None:
                    p, qb, h, t0, nq, n = unit2(u)
                    w = m2.w[u % 3]
                    dve.wait_ge(s.scores_done, U + u + 1)
                    if u >= 3:
                        dve.wait_ge(s.transposed, TE + TEV2["p", u - 3] + 1)
                    ch(dve.tensor_tensor(w[:, 0:n], s2(u, n)[:, :], fb[:, 2 * p + h, 0:n], ALU.add))
                    ch.wait()
                    dve.sem_inc(s.scores_free, 1)
                    ch(dve.tensor_tensor(w[:, n - nq:n], w[:, n - nq:n], negc[:, 0:nq], ALU.add))
                    ch.wait()
                    dve.tensor_reduce(m2.nmax[u % 3][:, :], w[:, 0:n], AX.X, ALU.max, negate=True).then_inc(s.max_done, 1)
                depthwise(DW_PER_STEP)
                if u is not None:
                    dve.wait_ge(s.exp_done, U + u + 1)
                    ch(dve.reciprocal(m2.inv[u % 3][:, :], m2.sums[u % 3][:, :]))
                    ch.wait()
                    dve.tensor_scalar(w[:, 0:n], w[:, 0:n], m2.inv[u % 3][:, :], None,
                                      ALU.mult).then_inc(s.probs_done, 1)
                for g in st.done:
                    evac(g)
                    lo_split(g + 2)
                    if g in (19, 22):
                        short_conv((g - 17) // 3)
            assert dw_at[0] >= len(DW_OPS)
            dve.wait_ge(s.ln_sums, l * 2 + 1)
            for c in range(2):
                ch(dve.scalar_tensor_tensor(out=tview(b, aconv[:, c, :]), in0=pview(b, 4), scalar=-1.0 / 256,
                                            in1=tview(b, aconv[:, c, :]), op0=ALU.mult, op1=ALU.add))
            ch.wait()
            dve.sem_inc(s.ln_centered, 1)
            dve.wait_ge(s.ln_steps, l * 2 + 2)
            dve.tensor_tensor(aconv[:, :, :], aconv[:, :, :], m2.lrs[:, :].unsqueeze(1).to_broadcast([P, 2, TM]),
                              ALU.mult).then_inc(s.ln_scaled, 1)

            def mul(i):
                c = HEADS_ORDER[i]
                dve.wait_ge(s.head_steps, 2 * (l * 8 + i) + 2)
                dve.tensor_tensor(y[:, c, :], y[:, c, :], S[2 + i % 2][:, 0:TM], ALU.mult).then_inc(s.head_scaled, 1)

            def lo(i):
                c = HEADS_ORDER[i]
                dve.wait_ge(s.head_hi, l * 8 + i + 1)
                dve.scalar_tensor_tensor(out=m2.olo[:, c, :], in0=y[:, c, :], scalar=gain(PAR_HEADG, l, c),
                                         in1=m2.ohi[:, c, :].bitcast(F32), op0=ALU.mult,
                                         op1=ALU.subtract).then_inc(s.head_lo, 1)

            for i in range(6):
                mul(i)
            dve.wait_ge(s.ln_silu, 2 * l + 2)
            dve.tensor_tensor(m2.alo[:, :, :], aconv[:, :, :], m2.ahi[:, :, :].bitcast(F32),
                              ALU.subtract).then_inc(s.a_lo, 1)
            for i in range(6):
                lo(i)
            lo_split(NCOL + 2)
            mul(6)
            mul(7)
            lo(6)
            lo(7)
            dve_out(dve, b, l, sub, g2b(l) + NCOL + 1, OUT_Q, ch, 1.0, PAR_MIXPOST2, nxt)

        def rows(name):
            t = I[name]
            return t.rearrange("l (c p) -> (l c) p", p=P)

        P1 = ["ffn1_pre_g", "ffn1_post_g", "mix_pre_g", "mix_post_g", "ffn2_pre_g", "ffn2_post_g"]
        P2 = ["mix_pre_g_2", "mix_post_g_2", "ffn_pre_g_2", "ffn_post_g_2", "head_g_2"]
        P2B = ["a_dw_b_2", "a_ln_g_2", "a_ln_b_2"]
        PSIZE = [96, 106, 124, 88, 88, 88]
        PCOL = [0, 96, 202, 326, 414, 502]
        NLD_PAR = 6 + 5 + 3 + 2 + 1 + 1 + 6

        def sp_setup(sp):
            sp.dma_start(xin, I["x"].rearrange("b (a p) d -> p (b a) d", p=P)).then_inc(s_ld[0], 16)
            sp.dma_start(metain[:, :], I["meta_tokens_2"]).then_inc(s_ld[1], 16)
            for i, n_ in enumerate(P1):
                sp.dma_start(prow[0][16 * i:16 * i + 16, :], rows(n_)).then_inc(s_ld[2], 16)
            for i, n_ in enumerate(P2):
                sp.dma_start(prow[1][16 * i:16 * i + 16, :], rows(n_)).then_inc(s_ld[2], 16)
            for i, n_ in enumerate(P2B):
                sp.dma_start(prow[1][80 + 4 * i:84 + 4 * i, :], rows(n_)).then_inc(s_ld[2], 16)
            for i in range(2):
                sp.dma_start(prow[1][92:94, 64 * i:64 * i + 64], I["diff_subln_g"]).then_inc(s_ld[2], 16)
            sp.dma_start(prow[1][94:106, :], I["sc_conv_w_2"].rearrange("l k (c p) -> (l k c) p", p=P)).then_inc(s_ld[2], 16)
            sp.dma_start(prow[2][0:124, :], I["a_dw_w_2"].rearrange("l k (c p) -> (l k c) p", p=P)).then_inc(s_ld[2], 16)
            for k in range(3):
                for l in range(LAYERS):
                    sp.dma_start(prow[3 + k][44 * l:44 * l + 44, :],
                                 I["ffn_conv_w_2"][l, k, :].rearrange("(c p) -> c p", p=P)).then_inc(s_ld[2], 16)
            sp.dma_start(relin[:, :], I["rel_bias"].rearrange("l h r -> (l h) r")).then_inc(s_ld[3], 16)
            for i, n_ in enumerate(["diff_lambda_q1", "diff_lambda_k1", "diff_lambda_q2", "diff_lambda_k2"]):
                sp.dma_start(lam_in[:, i, :, :].rearrange("p l d -> p (l d)"),
                             I[n_].rearrange("l d -> (l d)").partition_broadcast(P)).then_inc(s_ld[4], 16)
            with nc.allow_non_contiguous_dma(reason="sixteen forget biases"):
                sp.dma_start(bf[:, :], I["b_forget_2"].rearrange("l h -> h l")).then_inc(s_ld[5], 16)
            sp.wait_ge(s_rev, 2)
            sp.dma_start(rev_dram, rev[:, :]).then_inc(s_revd, 16)
            sp.wait_ge(s_revd, 16)
            b0 = rev_dram[0:1, P - 1:P]
            src = bass.AP(tensor=b0.tensor, offset=b0.offset, ap=[[640, 12], [-1, P], [1, SEQ]])
            sp.dma_start(tbias_dram, src).then_inc(s_tbias, 16)

        def pool_setup(pool):
            pool.memset(ident[:, :], 0.0).then_inc(s_mask, 1)
            pool.wait_ge(s_mask, 1)
            pool.affine_select(out=ident[:, :], in_=ident[:, :], compare_op=ALU.not_equal, fill=1.0, base=0,
                               pattern=[[-1, P]], channel_multiplier=1).then_inc(s_const, 1)

            pool.iota(dist[:, :], pattern=[[-1, SEQ]], base=SEQ - P, channel_multiplier=1,
                      allow_small_or_imprecise_dtypes=True).then_inc(s_set, 1)
            pool.memset(strict[:, :], 1.0).then_inc(s_set, 1)
            pool.memset(negs[:, :], 0.0).then_inc(s_set, 1)
            pool.memset(bd[:, :], 0.0).then_inc(s_set, 1)
            pool.wait_ge(s_set, 4)
            pool.affine_select(out=strict[:, :], in_=strict[:, :], compare_op=ALU.is_gt, fill=0.0, base=0,
                               pattern=[[-1, P]], channel_multiplier=1).then_inc(s_set, 1)
            pool.affine_select(out=negs[:, :], in_=negs[:, :], compare_op=ALU.is_gt, fill=NEG, base=0,
                               pattern=[[-1, P]], channel_multiplier=1).then_inc(s_set, 1)
            for h in range(2):
                pool.wait_ge(s_set, 6 + h)
                pool.memset(bd[64 * h:64 * h + 64, 64 * h:64 * h + 64], 1.0).then_inc(s_set, 1)
            pool.wait_ge(s_dist, 1)
            pool.memset(dist[0:64, SEQ - 64:SEQ], -NEG).then_inc(s_set, 1)
            pool.memset(negc[:, :], 0.0).then_inc(s_set, 1)
            pool.wait_ge(s_set, 10)
            pool.affine_select(out=negc[:, :], in_=negc[:, :], compare_op=ALU.is_ge, fill=NEG, base=0,
                               pattern=[[-1, P]], channel_multiplier=1).then_inc(s_set, 1)

        def dve_setup(dve, ch):
            dve.memset(ones[:, :], 1.0).then_inc(s_ones, 1)
            dve.memset(eps[:, :], EPS).then_inc(s_ones, 1)
            dve.memset(lneps[:, :], LN_EPS).then_inc(s_ones, 1)
            for sm in (b1.s.weights_split, b1.s.hidden_free, b1.s.columns_out, b1.s.scores_free, b2.s.hidden_free, b2.s.columns_out, b2.s.scores_free):
                dve.sem_inc(sm, CR)
            dve.sem_inc(b1.s.o_lo_out, 1)
            for c in range(KD):
                dve.wait_ge(s_xt, c + 1)
                dve.tensor_copy(x[:, c, META:TM], ps[:, c, :]).then_inc(b1.s.x_new, 1)
            dve.wait_ge(s_xt, KD + 1)
            ch(dve.tensor_copy(x[:, :, 0:META], ps[:, 0, 0:KD * META].rearrange("p (k t) -> p k t", k=KD)))
            ch.wait()
            dve.sem_inc(s_xc, 1)
            for i in range(6):
                dve.wait_ge(s_pt, i + 1)
                ins = dve.tensor_copy(par[:, PCOL[i]:PCOL[i] + PSIZE[i]], ps[:, 1 + i, 0:PSIZE[i]])
                ins.then_inc(s_pc, 1)
            dve.wait_ge(s_pc, 6)
            for l in range(LAYERS):
                li = 0.8 - 0.6 * math.exp(-0.3 * l)
                c = PAR_SUBLN + l
                ch(dve.tensor_scalar(par[:, c:c + 1], par[:, c:c + 1], 1.0 - li, None, ALU.mult))
            dve.wait_ge(s_ones, 3)
            dve.wait_ge(s_set, 11)
            dve.wait_ge(s_ld[5], 16)
            dve.wait_ge(s_ld[3], 16)
            dve.tensor_copy(rev[:, 640 - 257:640], relin[:, ::-1]).then_inc(s_rev, 1)
            dve.tensor_scalar(rev[:, 0:640 - 257], ones[0:12, 0:640 - 257], relin[:, 256:257], None,
                              ALU.mult).then_inc(s_rev, 1)
            dve.wait_ge(s_ld[4], 64)
            for i in range(2):
                ch(dve.tensor_tensor(lam_pr[:, i, :, :], lam_in[:, 2 * i, :, :], lam_in[:, 2 * i + 1, :, :], ALU.mult))
            ch.wait()
            dve.tensor_reduce(lam_s[:, :, :], lam_pr[:, :, :, :], AX.X, ALU.add).then_inc(s_lam, 1)
            dve.wait_ge(s_lam, 2)
            ch(dve.tensor_tensor(nlam[:, :], lam_e[:, 1, :], lam_e[:, 0, :], ALU.subtract))
            ch.wait()
            for l in range(LAYERS):
                li = 0.8 - 0.6 * math.exp(-0.3 * l)
                ch(dve.tensor_scalar(nlam[:, l:l + 1], nlam[:, l:l + 1], -li, None, ALU.add))
            ch.wait()

        def act_setup(act):
            for b in (b1, b2):
                act.sem_inc(b.s.out_free, CR)
                act.sem_inc(b.s.o_hi_out, 1)
                act.sem_inc(b.s.transposed_out, 1)
            act.wait_ge(s_set, 8)
            act.activation(dist[:, :], dist[:, :], ACT.Abs).then_inc(s_dist, 1)
            act.wait_ge(s_lam, 1)
            act.activation(lam_e[:, :, :], lam_s[:, :, :], ACT.Exp).then_inc(s_lam, 1)
            act.wait_ge(s_pc, 6)
            act.wait_ge(s_ones, 3)

        def pe_setup(pe):
            pe.sem_inc(b1.s.granules_done, CR)
            pe.wait_ge(s_const, 1)
            pe.wait_ge(s_ld[0], 16)
            for c in range(KD):
                for a in range(4):
                    ins = pe.transpose(ps[:, c, P * a:P * a + P], xin[:, a, P * c:P * c + P], ident[:, :])
                ins.then_inc(s_xt, 1)
            pe.wait_ge(s_ld[1], 16)
            pe.wait_ge(b1.s.x_new, 8)
            for c in range(KD):
                ins = pe.transpose(ps[:, 0, META * c:META * c + META], metain[:, P * c:P * c + P], ident[0:META, 0:META])
            ins.then_inc(s_xt, 1)
            pe.wait_ge(s_ld[2], 16 * NLD_PAR)
            for i in range(6):
                n_ = PSIZE[i]
                pe.transpose(ps[:, 1 + i, 0:n_], prow[i][0:n_, :], ident[0:n_, 0:n_]).then_inc(s_pt, 1)
            pe.wait_ge(s_ones, 3)
            pe.wait_ge(s_pc, 6)
            pe.wait_ge(s_xc, 1)
            pe.wait_ge(s_set, 11)
            pe.wait_ge(s_ld[5], 16)

        block = ctx.enter_context(nc.Block())

        nx_m1 = (PAR_MIXPRE, mgb, mgb2)
        nx_f2 = (PAR_FF2PRE, f2.gb, f2.gb2)

        @block.sync
        def _(sp):
            sp_setup(sp)
            with sp.Fori(0, LAYERS) as l:
                sp_ffn(sp, b1, l, f1)
                sp_mix1(sp, l)
                sp_ffn(sp, b1, l, f2)
            with sp.Fori(0, LAYERS) as l:
                sp_mix2(sp, l)
                sp_ffn(sp, b2, l, fg)
            for a in range(4):
                sp.wait_ge(s_oc, a + 1)
                sp.dma_start(out[0, P * a:P * a + P, :], xin[:, a, :]).then_inc(s_out, 16)
            sp.wait_ge(s_out, 64)

        @block.gpsimd
        def _(pool):
            pool_setup(pool)
            with pool.Fori(0, LAYERS) as l:
                pool_x(pool, b1, l * 3)
                pool_y(pool, b1, l * 3)
                pool_x(pool, b1, l * 3 + 1)
                pool_y(pool, b1, l * 3 + 1)
                pool_x(pool, b1, l * 3 + 2)
                pool_y(pool, b1, l * 3 + 2)
            with pool.Fori(0, LAYERS) as l:
                for sub in range(2):
                    pool_x(pool, b2, l * 2 + sub)
                    pool_y(pool, b2, l * 2 + sub)

        @block.scalar
        def _(act):
            act_setup(act)
            with act.Fori(0, LAYERS) as l:
                act_next(act, b1, l, l * 3, PAR_FF1PRE, f1.gb, f1.gb2)
                act_ffn(act, b1, l, f1, nx_m1)
                act_mix1(act, l, nx_f2)
                act_ffn(act, b1, l, f2, None)
            with act.Fori(0, LAYERS) as l:
                act_next(act, b2, l, l * 2, PAR_MIXPRE2, g2b, g2b2)
                act_mix2(act, l, (PAR_FFPRE2, fg.gb, fg.gb2))
                act_ffn(act, b2, l, fg, None)

        @block.vector
        def _(dve):
            ch = Chain(dve, b1.s.dve_steps, 0)
            dve_setup(dve, ch)
            base = ch.n
            with dve.Fori(0, LAYERS) as l:
                ch.base, n0 = l * CHAIN1, ch.n
                dve_first(dve, b1, l, l * 3, PAR_FF1PRE, f1.gb)
                dve_ffn(dve, b1, l, f1, ch, 0.5, PAR_FF1POST, nx_m1)
                dve_mix1(dve, l, ch, nx_f2)
                dve_ffn(dve, b1, l, f2, ch, 0.5, PAR_FF2POST, None)
                if ch.n - n0 != CHAIN1:
                    raise ValueError(f"CHAIN1 is {ch.n - n0}")
            dve.wait_ge(b1.s.weights_split, LAYERS * b1.GL + CR)
            dve.sem_inc(b2.s.weights_split, CR)
            dve.wait_ge(b1.s.x_new, 8 * 3 * LAYERS + 8)
            dve.sem_inc(b2.s.x_new, 8)
            chain1_end = base + LAYERS * CHAIN1
            ch.base, ch.n = 0, chain1_end
            with dve.Fori(0, LAYERS) as l:
                ch.base, n0 = l * CHAIN2, ch.n
                dve_first(dve, b2, l, l * 2, PAR_MIXPRE2, g2b)
                dve_mix2(dve, l, ch, (PAR_FFPRE2, fg.gb))
                dve_ffn(dve, b2, l, fg, ch, 1.0, PAR_FFPOST2, None)
                if ch.n - n0 != CHAIN2:
                    raise ValueError(f"CHAIN2 is {ch.n - n0}")
            ch.base, ch.n = 0, chain1_end + LAYERS * CHAIN2
            for a in range(4):
                for h in range(2):
                    dve.wait_ge(s_ot, 2 * a + h + 1)
                    ch(dve.tensor_copy(xin[:, a, 512 * h:512 * h + 512], ps[:, 2 * a + h, :]))
                ch.wait()
                dve.sem_inc(s_oc, 1)

        @block.tensor
        def _(pe):
            pe_setup(pe)
            with pe.Fori(0, LAYERS) as l:
                pe_ffn(pe, b1, l, f1)
                pe_mix1(pe, l)
                pe_ffn(pe, b1, l, f2)
            pe.wait_ge(b1.s.granules_done, LAYERS * b1.GL + CR)
            pe.sem_inc(b2.s.granules_done, CR)
            with pe.Fori(0, LAYERS) as l:
                pe_mix2(pe, l)
                pe_ffn(pe, b2, l, fg)
            pe.wait_ge(b2.s.x_new, 8 * 2 * LAYERS + 8)
            for a in range(4):
                for h in range(2):
                    for c in range(4):
                        t0 = META + P * a
                        ins = pe.transpose(ps[:, 2 * a + h, P * c:P * c + P], x[:, 4 * h + c, t0:t0 + P], ident[:, :])
                    ins.then_inc(s_ot, 1)


CHAIN1 = 315
CHAIN2 = 224

_INS = ["x", "ffn1_pre_g", "ffn1_w_gate", "ffn1_w_up", "ffn1_w_down", "ffn1_post_g", "mix_pre_g", "w_in", "rel_bias",
        "diff_lambda_q1", "diff_lambda_k1", "diff_lambda_q2", "diff_lambda_k2", "diff_subln_g", "w_out",
        "mix_post_g", "ffn2_pre_g", "ffn2_w_gate", "ffn2_w_up", "ffn2_w_down", "ffn2_post_g", "meta_tokens_2",
        "mix_pre_g_2", "mix_post_g_2", "w_in_2", "b_forget_2", "a_dw_w_2", "a_dw_b_2", "a_ln_g_2", "a_ln_b_2",
        "a_pw_w_2", "sc_conv_w_2", "head_g_2", "w_out_2", "ffn_pre_g_2", "ffn_post_g_2", "ffn_w_up_2",
        "ffn_conv_w_2", "ffn_w_down_2"]


def kernel(**inputs):
    import numpy as np
    import concourse.bacc as bacc
    from concourse.bass_utils import run_bass_kernel_spmd

    nc = bacc.Bacc("TRN2", target_bir_lowering=False, num_devices=1)
    arrays, tensors = {}, {}
    for name in _INS:
        a = np.ascontiguousarray(inputs[name])
        arrays[f"in_{name}_dram"] = a
        tensors[name] = nc.dram_tensor(f"in_{name}_dram", a.shape, mybir.dt.from_np(a.dtype), kind="ExternalInput").ap()
    out = nc.dram_tensor("out_0_dram", (1, SEQ, D), F32, kind="ExternalOutput").ap()
    program(nc, tensors, out)
    r = run_bass_kernel_spmd(nc, [arrays], core_ids=[0])
    return r.results[0]["out_0_dram"]
```

```python
import math
from contextlib import ExitStack

import concourse.bass as bass
from concourse import mybir

F32 = mybir.dt.float32
F32R = mybir.dt.float32r
ALU = mybir.AluOpType
ACT = mybir.ActivationFunctionType
AX = mybir.AxisListType

P = 128
D = 1024
KD = D // P
FF = 2816
KF = FF // P
SEQ = 512
META = 16
LAYERS = 2
PAIR = 2 * P
UP_ITERS = FF // PAIR
UP_GRAN = 4 * UP_ITERS
DOWN_PAIRS = D // PAIR
DOWN_Q = [4, 4, 4, 4, 4, 2]
DOWN_GRAN = DOWN_PAIRS * len(DOWN_Q)
FFN_GRAN = UP_GRAN + DOWN_GRAN
OUT_Q = [4, 4]
OUT_GRAN = DOWN_PAIRS * len(OUT_Q)
EPS = 1e-6
LN_EPS = 1e-5
NEG = -1e30

KINDS = "AAABBCCC"
QKV1 = [(128 * c, 384 + 128 * c, 768 + 128 * c) for c in range(3)]
QKV1 += [(1152 + 128 * c, 1408 + 128 * c, 1664 + 128 * c) for c in range(2)]
QKV1 += [(1920 + 128 * c, 2304 + 128 * c, 2688 + 128 * c) for c in range(3)]
IN1 = 3072
MIX1_GRAN = 24 + OUT_GRAN
UNITS1 = 64
SLOPE = [2.0 ** (-2 * (h + 1)) for h in range(4)]
B_SCALE = 32.0 ** -0.5

IN2 = 2824
F_COL = 1536
ACOL = 1544
COLS2 = [F_COL] + [ACOL + 128 * c for c in (0, 2, 1, 3)]
_SC = [ACOL + 512 + 128 * c for c in (0, 2, 4, 1, 3, 5)]
for _p in range(4):
    COLS2 += [128 * _p, 512 + 128 * _p, 1024 + 128 * _p]
    if _p > 0:
        COLS2 += [_SC[_p - 1]]
COLS2 += _SC[3:]
QKV2 = [5, 8, 12, 16]
SC_B2, SC_C2, SC_X2 = (11, 20), (15, 21), (19, 22)
MIX2_GRAN = len(COLS2) + 1 + OUT_GRAN
TAPS = 31
QB = 5
UNITS2 = 4 * QB * 2

PAR_FF1PRE, PAR_FF1POST, PAR_MIXPRE, PAR_MIXPOST, PAR_FF2PRE, PAR_FF2POST = (16 * i for i in range(6))
PAR_MIXPRE2, PAR_MIXPOST2, PAR_FFPRE2, PAR_FFPOST2, PAR_HEADG = (96 + 16 * i for i in range(5))
PAR_DWB, PAR_LNG, PAR_LNB, PAR_SUBLN, PAR_SCW = 176, 180, 184, 188, 190
PAR_DW = 202
PAR_FCW = 326
PAR_COLS = PAR_FCW + 3 * 88


class Record:
    pass


class Step:

    def __init__(self):
        self.vt = self.sc = None
        self.tiles, self.tr = [], []
        self.pairs, self.done = [], []


class Stack:

    def __init__(self, n, s, T, off, nh, TW, NT, GL, evf_layer, conv):
        self.n, self.s = n, s
        self.T, self.off = T, off
        self.nh, self.w = nh, T // nh
        self.TW, self.NT = TW, NT
        self.GL = GL
        self.evf_layer = evf_layer
        self.conv = conv


class Ffn:

    def __init__(self, sub, gb, gb2, ev, hb, gate, up, upoff, down):
        self.sub, self.gb, self.gb2, self.ev, self.hb = sub, gb, gb2, ev, hb
        self.gate, self.up, self.upoff, self.down = gate, up, upoff, down


def schedule(pairs, units_per_pair, fill):
    n = pairs * units_per_pair
    steps = [Step() for s in range(n + LAG)]
    for s, st in enumerate(steps):
        if s < n:
            st.sc = s
            if s % units_per_pair == 1:
                st.vt = s // units_per_pair
        if s >= LAG:
            st.tr = [s - LAG]
            if (s - LAG) % units_per_pair == units_per_pair - 1:
                st.pairs = [(s - LAG) // units_per_pair]
    for p, (grans, per_step) in enumerate(fill):
        tiles = [(g, t) for g in grans for t in range(8)]
        assert sum(per_step) == len(tiles)
        for s, k in enumerate(per_step):
            st = steps[p * units_per_pair + s]
            st.tiles = tiles[:k]
            st.done = [g for g, t in tiles[:k] if t == 7]
            tiles = tiles[k:]
    return steps


def t_events(steps):
    order = []
    for st in steps:
        order += [("p", u) for u in st.tr]
        if st.vt is not None:
            order.append(("v", st.vt))
    return {e: n for n, e in enumerate(order)}


LAG = 2
STEPS1 = schedule(8, 8, [([3 * p + 3, 3 * p + 4, 3 * p + 5], [3] * 8) for p in range(7)])
TEV1 = t_events(STEPS1)
FILL2 = [4, 4, 3, 3, 2, 4, 4, 3, 3, 2]
STEPS2 = schedule(4, 2 * QB, [(list(range(8 + 4 * p, 12 + 4 * p)), FILL2) for p in range(3)]
                  + [(list(range(20, 23)), [3, 3, 2, 3, 3, 2, 3, 3, 2, 0])])
TEV2 = t_events(STEPS2)
DW_OPS = [(t, c) for t in range(TAPS) for c in range(2)]
DW_PER_STEP = 2


class Chain:

    def __init__(self, eng, sem, per_layer):
        self.eng, self.sem, self.per_layer = eng, sem, per_layer
        self.base, self.n = 0, 0

    def __call__(self, ins):
        ins.then_inc(self.sem, 1)
        self.n += 1
        return ins

    def wait(self):
        self.eng.wait_ge(self.sem, self.base + self.n)


def program(nc, I, out):
    with ExitStack() as ctx:
        def sb(name, shape, dt=F32):
            return ctx.enter_context(nc.sbuf_tensor(name, shape, dt))

        def sem(name):
            return ctx.enter_context(nc.semaphore(name))

        TM = SEQ + META
        x = sb("x", [P, KD, TM])
        y = sb("y", [P, KD, TM])
        xhi, xlo = sb("xhi", [P, KD, TM], F32R), sb("xlo", [P, KD, TM], F32R)
        raw = [sb(f"raw{i}", [P, 1024]) for i in range(2)]
        whi = [sb(f"whi{i}", [P, 1024], F32R) for i in range(2)]
        wlo = [sb(f"wlo{i}", [P, 1024], F32R) for i in range(2)]
        S = [sb(f"S{i}", [P, TM + 2]) for i in range(6)]
        r = sb("r", [P, TM])
        par = sb("par", [P, PAR_COLS])
        ident = sb("ident", [P, P])
        ones = sb("ones", [P, SEQ])
        eps = sb("eps", [P, 1])
        sqrt_warm = sb("sqrt_warm", [P, 1])
        rms = sb("rms", [P, 6])
        rinv = sb("rinv", [P, 6])
        dist = sb("dist", [P, SEQ])
        strict = sb("strict", [P, P])
        later = sb("later", [P, P])
        bd = sb("bd", [P, P])
        negc = sb("negc", [P, P])
        bf = sb("bf", [8, LAYERS])
        lneps = sb("lneps", [P, 1])
        nlam = sb("nlam", [P, LAYERS])
        tbias_dram = nc.dram_tensor("tbias_scratch", (LAYERS * 6, P, SEQ), F32).ap()
        rev_dram = nc.dram_tensor("rev_scratch", (LAYERS * 6, 640), F32).ap()
        ps = ctx.enter_context(nc.psum_tensor("ps", [P, 8, 512], F32))
        xin = y[:, :, :].rearrange("p k t -> p (k t)")[:, 0:4 * D].rearrange("p (a d) -> p a d", a=4)

        sq = S[0:2]
        tt = S[2:4]
        acc = S[4]
        diag = S[5]

        area = ExitStack()
        hhi = area.enter_context(nc.sbuf_tensor("hhi", [P, KF, TM], F32R))
        hlo = area.enter_context(nc.sbuf_tensor("hlo", [P, KF, TM], F32R))
        area.close()
        area = ExitStack()

        def ab(name, shape, dt=F32):
            return area.enter_context(nc.sbuf_tensor(name, shape, dt))

        m1 = Record()
        m1.ohi = ab("m1_ohi", [P, KD, SEQ], F32R)
        m1.olo = ab("m1_olo", [P, KD, SEQ], F32R)
        m1.q = [ab(f"m1_q{i}", [P, SEQ]) for i in range(2)]
        m1.k = [ab(f"m1_k{i}", [P, SEQ]) for i in range(2)]
        m1.vt = [ab(f"m1_vt{i}", [P, SEQ]) for i in range(2)]
        m1.v = [ab(f"m1_v{i}", [P, 4, P]) for i in range(2)]
        m1.w = [ab(f"m1_w{i}", [P, 2, SEQ]) for i in range(3)]
        m1.scan = ab("m1_scan", [P, SEQ + 1])
        m1.pt = [ab(f"m1_pt{i}", [P, 4, P]) for i in range(2)]
        m1.ob = ab("m1_ob", [P, 2, SEQ])
        m1.sqb = ab("m1_sqb", [P, 2, SEQ])
        m1.rb = ab("m1_rb", [P, 2, SEQ])
        m1.nmax = [ab(f"m1_nmax{i}", [P, 2]) for i in range(3)]
        m1.sums = [ab(f"m1_sums{i}", [P, 2]) for i in range(3)]
        m1.inv = [ab(f"m1_inv{i}", [P, 2]) for i in range(3)]
        m1.c1 = [ab(f"m1_c1{i}", [P, 1]) for i in range(3)]
        tb = y[:, :, :].rearrange("p k t -> p (k t)")[:, 0:6 * SEQ].rearrange("p (h c) -> p h c", h=6)
        area.close()
        area = ExitStack()
        fb = ab("m2_fb", [P, 8, TM])
        apad = ab("m2_apad", [P, 2, TAPS - 1 + TM])
        aconv = ab("m2_aconv", [P, 2, TM])
        scx, scc, scb = ab("m2_scx", [P, 2 + TM]), ab("m2_scc", [P, TM]), ab("m2_scb", [P, TM])
        area.close()
        area = ExitStack()
        m2 = Record()
        m2.ohi = ab("m2_ohi", [P, KD, TM], F32R)
        m2.olo = ab("m2_olo", [P, KD, TM], F32R)
        m2.q = [ab(f"m2_q{i}", [P, TM]) for i in range(2)]
        m2.k = [ab(f"m2_k{i}", [P, TM]) for i in range(2)]
        m2.vt = [ab(f"m2_vt{i}", [P, TM]) for i in range(2)]
        m2.v = [ab(f"m2_v{i}", [P, QB, P]) for i in range(2)]
        m2.w = [ab(f"m2_w{i}", [P, TM]) for i in range(3)]
        m2.pt = [ab(f"m2_pt{i}", [P, QB, P]) for i in range(2)]
        m2.ahi = ab("m2_ahi", [P, 2, TM], F32R)
        m2.alo = ab("m2_alo", [P, 2, TM], F32R)
        m2.lsq = ab("m2_lsq", [P, 2, TM])
        m2.lrs = ab("m2_lrs", [P, TM])
        m2.u = ab("m2_u", [8, TM])
        m2.lf = ab("m2_lf", [8, TM])
        m2.nf = ab("m2_nf", [8, TM])
        m2.e = ab("m2_e", [8, TM])
        m2.nmax = [ab(f"m2_nmax{i}", [P, 1]) for i in range(3)]
        m2.sums = [ab(f"m2_sums{i}", [P, 1]) for i in range(3)]
        m2.inv = [ab(f"m2_inv{i}", [P, 1]) for i in range(3)]
        area.close()
        area = ExitStack()
        prow = [ab(f"prow{i}", [P, P]) for i in range(6)]
        metain = ab("metain", [META, D])
        relin = ab("relin", [12, 257])
        rev = ab("rev", [12, 640])
        lam_in = ab("lam_in", [P, 4, LAYERS, 32])
        lam_pr = ab("lam_pr", [P, 2, LAYERS, 32])
        lam_s = ab("lam_s", [P, 2, LAYERS])
        lam_e = ab("lam_e", [P, 2, LAYERS])
        area.close()

        def semaphores(b):
            s = Record()
            s.weights_landed = [sem(f"{b}_weights_landed{i}") for i in range(2)]
            s.weights_hi = sem(f"{b}_weights_hi")
            s.weights_split = sem(f"{b}_weights_split")
            s.granules_done = sem(f"{b}_granules_done")
            s.hidden_free = sem(f"{b}_hidden_free")
            s.out_free = sem(f"{b}_out_free")
            s.norm_sums = sem(f"{b}_norm_sums")
            s.norm_rms = sem(f"{b}_norm_rms")
            s.norm_diag = sem(f"{b}_norm_diag")
            s.norm_spread = sem(f"{b}_norm_spread")
            s.norm_r = sem(f"{b}_norm_r")
            s.x_new = sem(f"{b}_x_new")
            s.x_hi = sem(f"{b}_x_hi")
            s.x_lo = sem(f"{b}_x_lo")
            s.x_squared = sem(f"{b}_x_squared")
            s.x_summed = sem(f"{b}_x_summed")
            s.y_squared = sem(f"{b}_y_squared")
            s.y_summed = sem(f"{b}_y_summed")
            s.gate_in = sem(f"{b}_gate_in")
            s.silu_done = sem(f"{b}_silu_done")
            s.hidden_done = sem(f"{b}_hidden_done")
            s.hidden_hi = sem(f"{b}_hidden_hi")
            s.hidden_lo = sem(f"{b}_hidden_lo")
            s.columns_out = sem(f"{b}_columns_out")
            s.scores_done = sem(f"{b}_scores_done")
            s.scores_free = sem(f"{b}_scores_free")
            s.max_done = sem(f"{b}_max_done")
            s.exp_done = sem(f"{b}_exp_done")
            s.probs_done = sem(f"{b}_probs_done")
            s.transposed = sem(f"{b}_transposed")
            s.transposed_out = sem(f"{b}_transposed_out")
            s.pv_done = sem(f"{b}_pv_done")
            s.o_hi_out = sem(f"{b}_o_hi_out")
            return s

        def first_semaphores(b, s):
            s.o_lo_out = sem(f"{b}_o_lo_out")
            s.b_act_steps = sem(f"{b}_b_act_steps")
            s.b_sums = sem(f"{b}_b_sums")
            s.b_scaled = sem(f"{b}_b_scaled")
            s.b_hi = sem(f"{b}_b_hi")
            s.b_lo = sem(f"{b}_b_lo")
            s.dve_steps = sem(f"{b}_dve_steps")
            return s

        def second_semaphores(b, s):
            s.up_in = sem(f"{b}_up_in")
            s.last_tap = sem(f"{b}_last_tap")
            s.forget_in = sem(f"{b}_forget_in")
            s.forget_steps = sem(f"{b}_forget_steps")
            s.forget_sums = sem(f"{b}_forget_sums")
            s.forget_spread = sem(f"{b}_forget_spread")
            s.forget_out = sem(f"{b}_forget_out")
            s.inv_done = sem(f"{b}_inv_done")
            s.a_gate_in = sem(f"{b}_a_gate_in")
            s.a_gate_done = sem(f"{b}_a_gate_done")
            s.dw_taps = sem(f"{b}_dw_taps")
            s.ln_sums = sem(f"{b}_ln_sums")
            s.ln_centered = sem(f"{b}_ln_centered")
            s.ln_squared = sem(f"{b}_ln_squared")
            s.ln_steps = sem(f"{b}_ln_steps")
            s.ln_scaled = sem(f"{b}_ln_scaled")
            s.ln_silu = sem(f"{b}_ln_silu")
            s.a_lo = sem(f"{b}_a_lo")
            s.pw_out = sem(f"{b}_pw_out")
            s.short_done = sem(f"{b}_short_done")
            s.head_squared = sem(f"{b}_head_squared")
            s.head_sums = sem(f"{b}_head_sums")
            s.head_steps = sem(f"{b}_head_steps")
            s.head_scaled = sem(f"{b}_head_scaled")
            s.head_hi = sem(f"{b}_head_hi")
            s.head_lo = sem(f"{b}_head_lo")
            return s

        s_ld = [sem(f"s_ld{i}") for i in range(6)]
        s_ones = sem("s_ones")
        s_const = sem("s_const")
        s_xt, s_xc, s_pt, s_pc = sem("s_xt"), sem("s_xc"), sem("s_ptr"), sem("s_pcopy")
        s_rev, s_revd, s_tbias, s_tb, s_mask = sem("s_rev"), sem("s_revd"), sem("s_tbias"), sem("s_tb"), sem("s_mask")
        s_lam = sem("s_lam")
        s_set, s_dist = sem("s_set"), sem("s_dist")
        s_ot, s_oc, s_out = sem("s_ot"), sem("s_oc"), sem("s_out")
        CR = 2

        b1 = Stack(
            n=1, s=first_semaphores("b1", semaphores("b1")), T=SEQ, off=META, nh=1, TW=128, NT=4, GL=2 * FFN_GRAN + MIX1_GRAN,
            evf_layer=4 * UP_ITERS, conv=False)
        b2 = Stack(
            n=2, s=second_semaphores("b2", semaphores("b2")), T=TM, off=0, nh=2, TW=88, NT=6, GL=FFN_GRAN + MIX2_GRAN,
            evf_layer=2 * UP_ITERS, conv=True)

        def halves(b):
            return [(h * b.w, b.w) for h in range(b.nh)]

        def pview(b, bank, nh=None):
            return ps[:, bank:bank + b.nh, 0:b.w]

        def tview(b, ap):
            return ap.rearrange("p (h w) -> p h w", h=b.nh)

        def xs(b, t, c):
            return t[:, c, b.off:b.off + b.T] if b.n == 1 else t[:, c, 0:b.T]

        def gain(col, l, c):
            return par[:, bass.ds(l * KD + (col + c), 1)]

        def load_raw(sp, b, g, slot, src, shape):
            sp.wait_ge(b.s.weights_split, g + 1)
            k, c = shape
            dst = raw[slot][:, 0:k * c].rearrange("p (k c) -> p k c", k=k)
            sp.dma_start(dst, src.rearrange("(k p) c -> p k c", p=P)).then_inc(b.s.weights_landed[slot], 16)

        def split_hi(act, b, g, g2, slot, n=1024):
            act.wait_ge(b.s.weights_landed[slot], 16 * g2 + 16)
            act.wait_ge(b.s.granules_done, g + 1)
            act.activation(whi[slot][:, 0:n], raw[slot][:, 0:n], ACT.Copy).then_inc(b.s.weights_hi, 1)

        def split_lo(eng, b, g, slot, n=1024, handover=False):
            if handover:
                eng.wait_ge(b.s.weights_split, g + CR)
            eng.wait_ge(b.s.weights_hi, g + 1)
            eng.tensor_tensor(wlo[slot][:, 0:n], raw[slot][:, 0:n], whi[slot][:, 0:n].bitcast(F32),
                              ALU.subtract).then_inc(b.s.weights_split, 1)

        def tile_mm(pe, b, bank, slot, wcol, hi, lo, first, last):
            wh, wl = whi[slot][:, wcol:wcol + P], wlo[slot][:, wcol:wcol + P]
            for n, (t0, w) in enumerate(halves(b)):
                o = ps[:, bank + n, 0:w]
                pe.matmul(o, wh, hi[:, t0:t0 + w], start=first, stop=False)
                pe.matmul(o, wh, lo[:, t0:t0 + w], start=False, stop=False)
                ins = pe.matmul(o, wl, hi[:, t0:t0 + w], start=False, stop=last)
            return ins

        def pe_sum(pe, b, n, bank, srcs):
            for t in range(b.NT):
                for j, sc in enumerate(srcs):
                    ins = pe.matmul(ps[0:b.TW, bank, t:t + 1], sc[:, t * b.TW:(t + 1) * b.TW], ones[:, 0:1],
                                    start=(j == 0), stop=(j == len(srcs) - 1))
            ins.then_inc(b.s.norm_sums, 1)

        def act_sqrt_table(act):
            act.activation(sqrt_warm[:, :], eps[:, :], ACT.Sqrt)

        def act_rms(act, b, n, bank):
            act.wait_ge(b.s.norm_sums, n + 1)
            act.activation(rms[0:b.TW, 0:b.NT], ps[0:b.TW, bank, 0:b.NT], ACT.Sqrt,
                           bias=eps[0:b.TW, :], scale=1.0 / D).then_inc(b.s.norm_rms, 1)

        def dve_diag(dve, b, n, ch):
            dve.wait_ge(b.s.norm_rms, n + 1)
            ch(dve.reciprocal(rinv[0:b.TW, 0:b.NT], rms[0:b.TW, 0:b.NT]))
            ch.wait()
            dv = diag[0:b.TW, 0:b.T].rearrange("p (t n) -> p t n", t=b.NT)
            dve.tensor_tensor(dv, ident[0:b.TW, 0:b.TW].unsqueeze(1).to_broadcast([b.TW, b.NT, b.TW]),
                              rinv[0:b.TW, 0:b.NT].unsqueeze(2).to_broadcast([b.TW, b.NT, b.TW]),
                              ALU.mult).then_inc(b.s.norm_diag, 1)

        def pe_bc(pe, b, n, bank):
            pe.wait_ge(b.s.norm_diag, n + 1)
            for i, (t0, w) in enumerate(halves(b)):
                ins = pe.matmul(ps[:, bank + i, 0:w], ones[0:b.TW, 0:P], diag[0:b.TW, t0:t0 + w],
                                start=True, stop=True)
            ins.then_inc(b.s.norm_spread, 1)

        def act_r(act, b, n, bank):
            act.wait_ge(b.s.norm_spread, n + 1)
            act.activation(tview(b, r[:, 0:b.T]), pview(b, bank), ACT.Copy).then_inc(b.s.norm_r, 1)

        SUM_PRE, BC_PRE, SUM_POST, BC_POST = 4, 6, 0, 6

        def act_operand(act, b, l, sub, col, c):
            act.wait_ge(b.s.x_new, 8 * sub + c + 1)
            act.activation(xhi[:, c, 0:b.T], xs(b, x, c), ACT.Copy, scale=gain(col, l, c)).then_inc(b.s.x_hi, 1)
            if c == 0:
                act.activation(acc[:, 0:b.T], xs(b, x, c), ACT.Square).then_inc(b.s.x_squared, 1)
            else:
                if c > 2:
                    act.wait_ge(b.s.x_summed, 7 * sub + c - 2)
                act.activation(sq[c % 2][:, 0:b.T], xs(b, x, c), ACT.Square).then_inc(b.s.x_squared, 1)

        def dve_operand_lo(dve, b, l, sub, col, c):
            dve.wait_ge(b.s.x_hi, 8 * sub + c + 1)
            dve.scalar_tensor_tensor(out=xlo[:, c, 0:b.T], in0=xs(b, x, c), scalar=gain(col, l, c),
                                     in1=xhi[:, c, 0:b.T].bitcast(F32), op0=ALU.mult,
                                     op1=ALU.subtract).then_inc(b.s.x_lo, 1)

        def pool_x(pool, b, sub):
            for c in range(1, KD):
                pool.wait_ge(b.s.x_squared, 8 * sub + c + 1)
                if c > 1:
                    pool.wait_ge(b.s.x_summed, 7 * sub + c - 1)
                pool.tensor_tensor(acc[:, 0:b.T], acc[:, 0:b.T], sq[c % 2][:, 0:b.T], ALU.add).then_inc(b.s.x_summed, 1)

        def pool_y(pool, b, sub):
            for c in range(1, KD - 2):
                pool.wait_ge(b.s.y_squared, 8 * sub + c + 1)
                if c > 1:
                    pool.wait_ge(b.s.y_summed, 5 * sub + c - 1)
                pool.tensor_tensor(acc[:, 0:b.T], acc[:, 0:b.T], sq[c % 2][:, 0:b.T], ALU.add).then_inc(b.s.y_summed, 1)

        def act_yevac(act, b, sub, m):
            for o in range(2):
                c = 2 * m + o
                bank = 4 * (m % 2) + 2 * o
                act.activation(tview(b, y[:, c, 0:b.T]), pview(b, bank), ACT.Copy)
                if c > 2:
                    act.wait_ge(b.s.y_summed, 5 * sub + min(c - 2, 5))
                dst = acc if c == 0 else sq[c % 2]
                ins = act.activation(tview(b, dst[:, 0:b.T]), pview(b, bank), ACT.Square)
                ins.then_inc(b.s.y_squared, 1)
            act.wait_ge(b.s.y_squared, 8 * sub + 2 * m + 2)
            act.sem_inc(b.s.out_free, 1)

        def dve_residual(dve, b, l, sub, ch, factor, post, pre):
            dve.wait_ge(b.s.norm_spread, 2 * sub + 2)
            for c in range(KD + 1):
                if c < KD:
                    ch(dve.scalar_tensor_tensor(out=tview(b, tt[c % 2][:, 0:b.T]), in0=tview(b, y[:, c, 0:b.T]),
                                                scalar=factor, in1=pview(b, BC_POST), op0=ALU.mult, op1=ALU.mult))
                    ch.wait()
                    dve.scalar_tensor_tensor(out=xs(b, x, c), in0=tt[c % 2][:, 0:b.T], scalar=gain(post, l, c),
                                             in1=xs(b, x, c), op0=ALU.mult, op1=ALU.add).then_inc(b.s.x_new, 1)
                if c > 0 and pre is not None:
                    dve_operand_lo(dve, b, l, sub + 1, pre, c - 1)

        def sp_ffn(sp, b, l, f):
            with sp.Fori(0, UP_ITERS) as i:
                for q in range(4):
                    W = f.gate if q < 2 else f.up
                    src = W[bass.ds(l * D + (q % 2) * 512, 512), bass.ds(i * PAIR + f.upoff * (q // 2), PAIR)]
                    load_raw(sp, b, f.gb(l) + 4 * i + q, q % 2, src, (4, PAIR))
            for m in range(DOWN_PAIRS):
                for q, k in enumerate(DOWN_Q):
                    src = f.down[bass.ds(l * FF + q * 512, k * P), m * PAIR:(m + 1) * PAIR]
                    load_raw(sp, b, f.gb(l) + UP_GRAN + 6 * m + q, q % 2, src, (k, PAIR))

        def pe_up_granule(pe, b, l, f, i, q, between=None):
            g = f.gb(l) + 4 * i + q
            pe.wait_ge(b.s.weights_split, g + 1 + CR)
            first = q % 2 == 0
            if first:
                pe.wait_ge(b.s.hidden_free, f.ev(l) + 2 * i + q // 2 + 1)
            for o in range(2):
                for kk in range(4):
                    k = 4 * (q % 2) + kk
                    if isinstance(i, int) and i == 0 and q < 2 and o == 0:
                        pe.wait_ge(b.s.x_lo, 8 * f.sub(l) + k + 1)
                    ins = tile_mm(pe, b, 4 * (q // 2) + 2 * o, q % 2, kk * PAIR + o * P,
                                  xhi[:, k, :], xlo[:, k, :], first and kk == 0, not first and kk == 3)
                if o == 0 and between is not None:
                    between()
            ins.then_inc(b.s.granules_done, 1)

        def pe_out(pe, b, l, sub, gb, qs, hi, lo, ready, second=None):
            nq = len(qs)

            def pair_of(base, m, mi):
                pe.wait_ge(b.s.out_free, 4 * sub + base + m + 1)
                for q, kn in enumerate(qs):
                    pe.wait_ge(b.s.weights_split, gb + nq * (base + m) + q + 1 + CR)
                    for kk in range(kn):
                        k = 4 * q + kk
                        if ready is not None and mi == 0 and m == 0:
                            ready(k)
                        for o in range(2):
                            ins = tile_mm(pe, b, 4 * m + 2 * o, q % 2, kk * PAIR + o * P, hi[:, k, :], lo[:, k, :],
                                          q == 0 and kk == 0, q == nq - 1 and kk == kn - 1)
                    ins.then_inc(b.s.granules_done, 1)

            for mi in range(2):
                for m in range(2):
                    if second is not None and mi == 0 and m == 1:
                        second()
                    pair_of(2 * mi, m, mi)

        def pe_post(pe, b, sub):
            pe.wait_ge(b.s.y_squared, 8 * sub + 8)
            pe.wait_ge(b.s.y_summed, 5 * sub + 5)
            pe_sum(pe, b, 2 * sub + 1, SUM_POST, [acc, sq[0], sq[1]])
            pe_bc(pe, b, 2 * sub + 1, BC_POST)

        def pe_pre_sum(pe, b, sub):
            pe.wait_ge(b.s.x_summed, 7 * sub + 7)
            pe_sum(pe, b, 2 * sub, SUM_PRE, [acc])

        def pe_ffn(pe, b, l, f):
            sub = f.sub(l)
            pe.wait_ge(b.s.out_free, 4 * sub + CR)
            pe_up_granule(pe, b, l, f, 0, 0)
            pe_up_granule(pe, b, l, f, 0, 1, lambda: pe_pre_sum(pe, b, sub))
            pe_bc(pe, b, 2 * sub, BC_PRE)
            pe.wait_ge(b.s.norm_r, sub + 1)
            pe_up_granule(pe, b, l, f, 0, 2)
            pe_up_granule(pe, b, l, f, 0, 3)
            with pe.Fori(1, UP_ITERS) as i:
                for q in range(4):
                    pe_up_granule(pe, b, l, f, i, q)
            pe.wait_ge(b.s.hidden_free, f.ev(l) + 2 * UP_ITERS - 1 + CR)
            pe_out(pe, b, l, sub, f.gb(l) + UP_GRAN, DOWN_Q, hhi, hlo,
                   lambda k: pe.wait_ge(b.s.hidden_lo, f.hb(l) + k + 1),
                   lambda: pe.wait_ge(b.s.hidden_free, f.ev(l) + 2 * UP_ITERS + CR))
            pe_post(pe, b, sub)

        def act_ffn(act, b, l, f, nxt):
            sub, gb = f.sub(l), f.gb(l)

            def hi_split(i, q):
                split_hi(act, b, gb + 4 * i + q, f.gb2(l) + 2 * i + q // 2, q % 2)

            def first_tap(i, up):
                for o in range(2):
                    act.wait_ge(b.s.up_in, 2 * f.hb(l) + 4 * i + 2 * up + o + 1)
                    act.activation(S[2 + 2 * up + o][:, 0:b.T], S[o][:, 2:2 + b.T], ACT.Copy,
                                   scale=tap(l, 2, 2 * i + o, up)).then_inc(b.s.last_tap, 1)

            def silu(i):
                if b.conv:
                    first_tap(i, 0)
                for o in range(2):
                    act.wait_ge(b.s.gate_in, f.hb(l) + 2 * i + o + 1)
                    act.activation(S[2 + o][:, 0:b.T], S[2 + o][:, 0:b.T], ACT.Silu).then_inc(b.s.silu_done, 1)

            def hidden(i):
                if b.conv:
                    first_tap(i, 1)
                hi_split(i + 1, 2)
                for o in range(2):
                    act.wait_ge(b.s.hidden_done, f.hb(l) + 2 * i + o + 1)
                    act.activation(hhi[:, bass.ds(2 * i + o, 1), 0:b.T].rearrange("p a t -> p (a t)"),
                                   S[4 + o][:, 0:b.T], ACT.Copy).then_inc(b.s.hidden_hi, 1)

            hi_split(0, 2)
            act_rms(act, b, 2 * sub, SUM_PRE)
            act_r(act, b, 2 * sub, BC_PRE)
            hi_split(0, 3)
            silu(0)
            hi_split(1, 0)
            hi_split(1, 1)
            hidden(0)
            with act.Fori(1, UP_ITERS) as i:
                hi_split(i, 3)
                silu(i)
                hi_split(i + 1, 0)
                hi_split(i + 1, 1)
                hidden(i)
            act_out(act, b, l, sub, gb + UP_GRAN, f.gb2(l) + UP_GRAN // 2, DOWN_Q, 3)
            act_rms(act, b, 2 * sub + 1, SUM_POST)
            if nxt is not None:
                act_next(act, b, l, sub + 1, *nxt)

        def act_out(act, b, l, sub, gb, gb2, qs, first=2):
            nq = len(qs)
            n = DOWN_PAIRS * nq
            for j in range(n):
                if j == nq:
                    act_sqrt_table(act)
                if first <= j + 2 < n:
                    split_hi(act, b, gb + j + 2, gb2 + j // 2 + 1, j % 2, qs[(j + 2) % nq] * PAIR)
                if j % nq == nq - 1:
                    act.wait_ge(b.s.granules_done, gb + j + 1 + CR)
                    act_yevac(act, b, sub, j // nq)

        def act_next(act, b, l, sub, col, gb, gb2):
            for j in range(2):
                split_hi(act, b, gb(l) + j, gb2(l), j)
            for c in range(KD):
                act_operand(act, b, l, sub, col, c)

        def dve_ffn(dve, b, l, f, ch, factor, post, nxt):
            sub, gb = f.sub(l), f.gb(l)

            def lo_split(i, q):
                split_lo(dve, b, gb + 4 * i + q, q % 2)

            def conv(i, up):
                for o in range(2):
                    dve.tensor_tensor(tview(b, S[o][:, 2:2 + b.T]), pview(b, 4 * up + 2 * o), tview(b, r[:, 0:b.T]),
                                      ALU.mult).then_inc(b.s.up_in, 1)
                dve.wait_ge(b.s.up_in, 2 * f.hb(l) + 4 * i + 2 * up + 2)
                dve.sem_inc(b.s.hidden_free, 1)
                for k in (1, 0):
                    for o in range(2):
                        c_ = S[2 + 2 * up + o][:, 0:b.T]
                        if k:
                            dve.wait_ge(b.s.last_tap, 2 * f.hb(l) + 4 * i + 2 * up + o + 1)
                        ins = dve.scalar_tensor_tensor(out=c_, in0=S[o][:, k:k + b.T], scalar=tap(l, k, 2 * i + o, up),
                                                       in1=c_, op0=ALU.mult, op1=ALU.add)
                        if k == 0 and not up:
                            ins.then_inc(b.s.gate_in, 1)
                        else:
                            ch(ins)
                    if k or up:
                        ch.wait()

            def gate(i):
                dve.wait_ge(b.s.granules_done, gb + 4 * i + 2 + CR)
                if b.conv:
                    return conv(i, 0)
                for o in range(2):
                    ins = dve.tensor_tensor(tview(b, S[2 + o][:, 0:b.T]), pview(b, 2 * o), tview(b, r[:, 0:b.T]),
                                            ALU.mult).then_inc(b.s.gate_in, 1)
                dve.wait_ge(b.s.gate_in, f.hb(l) + 2 * i + 2)
                dve.sem_inc(b.s.hidden_free, 1)

            def up(i):
                dve.wait_ge(b.s.granules_done, gb + 4 * i + 4 + CR)
                if b.conv:
                    conv(i, 1)
                else:
                    for o in range(2):
                        ch(dve.tensor_tensor(tview(b, S[4 + o][:, 0:b.T]), pview(b, 4 + 2 * o),
                                             tview(b, r[:, 0:b.T]), ALU.mult))
                    ch.wait()
                    dve.sem_inc(b.s.hidden_free, 1)
                lo_split(i + 1, 2)
                for o in range(2):
                    dve.wait_ge(b.s.silu_done, f.hb(l) + 2 * i + o + 1)
                    dve.tensor_tensor(S[4 + o][:, 0:b.T], S[4 + o][:, 0:b.T], S[2 + o][:, 0:b.T],
                                      ALU.mult).then_inc(b.s.hidden_done, 1)
                for o in range(2):
                    dve.wait_ge(b.s.hidden_hi, f.hb(l) + 2 * i + o + 1)
                    h = bass.ds(2 * i + o, 1)
                    dve.tensor_tensor(hlo[:, h, 0:b.T].rearrange("p a t -> p (a t)"), S[4 + o][:, 0:b.T],
                                      hhi[:, h, 0:b.T].rearrange("p a t -> p (a t)").bitcast(F32),
                                      ALU.subtract).then_inc(b.s.hidden_lo, 1)

            split_lo(dve, b, gb + 2, 0, handover=True)
            dve_diag(dve, b, 2 * sub, ch)
            lo_split(0, 3)
            dve.wait_ge(b.s.norm_r, sub + 1)
            if b.conv:
                for o in range(2):
                    ch(dve.memset(S[o][:, 0:2], 0.0))
            gate(0)
            lo_split(1, 0)
            lo_split(1, 1)
            up(0)
            per = 6 if b.conv else 2
            with dve.Fori(1, UP_ITERS) as i:
                base, n0 = ch.base, ch.n
                ch.base = base + (i - 1) * per
                lo_split(i, 3)
                gate(i)
                lo_split(i + 1, 0)
                lo_split(i + 1, 1)
                up(i)
                assert ch.n == n0 + per, ch.n - n0
            ch.base, ch.n = base, n0 + per * (UP_ITERS - 1)
            dve_out(dve, b, l, sub, gb + UP_GRAN, DOWN_Q, ch, factor, post, nxt, 3)

        def dve_out(dve, b, l, sub, gb, qs, ch, factor, post, nxt, first=2):
            nq = len(qs)
            for j in range(first - 2, DOWN_PAIRS * nq - 2):
                split_lo(dve, b, gb + j + 2, j % 2, qs[(j + 2) % nq] * PAIR, handover=(qs is OUT_Q and j == 0))
            dve_diag(dve, b, 2 * sub + 1, ch)
            if nxt is not None:
                for j in range(2):
                    split_lo(dve, b, nxt[1](l) + j, j)
            dve_residual(dve, b, l, sub, ch, factor, post, None if nxt is None else nxt[0])

        def pool_first(pool, b, l, gb):
            for j in range(2):
                split_lo(pool, b, gb(l) + j, j, handover=True)

        def dve_first(dve, b, l, sub, col):
            for c in range(KD):
                dve_operand_lo(dve, b, l, sub, col, c)

        def tap(l, k, chunk, up):
            return par[:, bass.ds(l * 44 + chunk + (PAR_FCW + 88 * k + 22 * up), 1)]

        def ffn1(which):
            g0 = 0 if which == 0 else FFN_GRAN + MIX1_GRAN
            return Ffn(
                sub=lambda l: l * 3 + 2 * which, gb=lambda l: l * b1.GL + g0, gb2=lambda l: l * (b1.GL // 2) + g0 // 2,
                ev=lambda l: l * b1.evf_layer + 2 * UP_ITERS * which, hb=lambda l: l * 2 * KF + KF * which,
                gate=I[f"ffn{which + 1}_w_gate"].rearrange("l d f -> (l d) f"),
                up=I[f"ffn{which + 1}_w_up"].rearrange("l d f -> (l d) f"), upoff=0,
                down=I[f"ffn{which + 1}_w_down"].rearrange("l f d -> (l f) d"))

        f1, f2 = ffn1(0), ffn1(1)
        mgb = lambda l: l * b1.GL + FFN_GRAN
        mgb2 = lambda l: l * (b1.GL // 2) + FFN_GRAN // 2
        win1 = I["w_in"].rearrange("l d f -> (l d) f")
        wout1 = I["w_out"].rearrange("l d f -> (l d) f")

        def sp_mix1(sp, l):
            b = b1
            for p in range(8):
                for j in range(3):
                    g = 3 * p + j
                    src = win1[bass.ds(l * D, D), QKV1[p][j]:QKV1[p][j] + P]
                    load_raw(sp, b, mgb(l) + g, g % 2, src, (8, P))
                if p == 0:
                    sp.wait_ge(b.s.x_new, 8 * (l * 3 + 1) + 8)
                    sp.wait_ge(s_tbias, 16)
                    sp.dma_start(tb, tbias_dram[bass.ds(l * 6, 6), :, :].rearrange("h p c -> p h c")).then_inc(s_tb, 16)
            sp_wout(sp, b, l, mgb(l) + 24, wout1)

        def sp_wout(sp, b, l, gb, W):
            for m in range(DOWN_PAIRS):
                for q in range(2):
                    src = W[bass.ds(l * D + q * 512, 512), m * PAIR:(m + 1) * PAIR]
                    load_raw(sp, b, gb + 2 * m + q, q, src, (4, PAIR))

        def sbank(u):
            return 4 + 2 * (u % 2)

        def unit1(u):
            p, h, j = u // 8, (u // 4) % 2, u % 4
            return p, h, j, KINDS[p], P * (j + 1)

        def pe_mix1(pe, l):
            b, s = b1, b1.s
            sub = l * 3 + 1
            U = l * UNITS1

            def gtile(g, t):
                if t == 0:
                    pe.wait_ge(s.weights_split, mgb(l) + g + 1 + CR)
                    pe.wait_ge(s.columns_out, l * 24 + g + 1)
                if g == 0:
                    pe.wait_ge(s.x_lo, 8 * sub + t + 1)
                ins = tile_mm(pe, b, g % 2, g % 2, t * P, xhi[:, t, :], xlo[:, t, :], t == 0, t == 7)
                if t == 7:
                    ins.then_inc(s.granules_done, 1)

            def scores(u):
                p, h, j, kind, n = unit1(u)
                pe.wait_ge(s.columns_out, l * 24 + 3 * p + 2 + CR)
                pe.wait_ge(s.scores_free, U + u + 1)
                maps = 2 if kind == "B" else 1
                rows = 64 // maps
                for m in range(maps):
                    a = 64 * h + rows * m
                    ins = pe.matmul(ps[:, sbank(u) + m, 0:n], m1.q[p % 2][a:a + rows, P * j:P * j + P],
                                    m1.k[p % 2][a:a + rows, 0:n], start=True, stop=True)
                ins.then_inc(s.scores_done, 1)

            def vtrans(p):
                e = TEV1["v", p]
                pe.wait_ge(s.columns_out, l * 24 + 3 * p + 3 + CR)
                pe.wait_ge(s.transposed_out, l * len(TEV1) + e + 1)
                for t in range(4):
                    ins = pe.transpose(ps[:, 2, P * t:P * t + P], m1.vt[p % 2][:, P * t:P * t + P], ident[:, :])
                ins.then_inc(s.transposed, 1)

            def ptrans(u):
                p, h, j, kind, n = unit1(u)
                pe.wait_ge(s.probs_done, U + u + 1)
                pe.wait_ge(s.transposed_out, l * len(TEV1) + TEV1["p", u] + 1)
                for t in range(j + 1):
                    ins = pe.transpose(ps[:, 2, P * t:P * t + P], m1.w[u % 3][:, 0, P * t:P * t + P], ident[:, :])
                ins.then_inc(s.transposed, 1)

            def pv(u):
                p, h, j, kind, n = unit1(u)
                pe.wait_ge(s.transposed_out, l * len(TEV1) + TEV1["p", u] + 2)
                if u % 8 == 0:
                    pe.wait_ge(s.o_hi_out, l * 8 + p + 1)
                    pe.wait_ge(s.o_lo_out, l * 8 + p + 1)
                for t in range(j + 1):
                    ins = pe.matmul(ps[64 * h:64 * h + 64, 3, P * j:P * j + P], m1.v[p % 2][:, t, 64 * h:64 * h + 64],
                                    m1.pt[u % 2][:, t, :], start=(t == 0), stop=(t == j))
                ins.then_inc(s.pv_done, 1)

            pe.wait_ge(s.out_free, 4 * sub + CR)
            for g in range(3):
                for t in range(8):
                    gtile(g, t)
                if g == 0:
                    pe_pre_sum(pe, b, sub)
                if g == 1:
                    pe_bc(pe, b, 2 * sub, BC_PRE)
            pe.wait_ge(s.norm_r, sub + 1)
            for n_step, st in enumerate(STEPS1):
                for u in st.tr:
                    ptrans(u)
                if st.sc is not None:
                    scores(st.sc)
                for tile in st.tiles[:2]:
                    gtile(*tile)
                if st.vt is not None:
                    vtrans(st.vt)
                for tile in st.tiles[2:]:
                    gtile(*tile)
                for u in st.tr:
                    pv(u)
                if n_step == B_NORM:
                    pe.wait_ge(s.b_act_steps, l * 3 + 1)
                    for c in range(2):
                        ins = pe.matmul(ps[:, 5 + 2 * c, 0:SEQ], bd[:, :], m1.sqb[:, c, :], start=True, stop=True)
                    ins.then_inc(s.b_sums, 1)
            pe.wait_ge(s.o_lo_out, l * 8 + 9)
            pe.wait_ge(s.o_hi_out, l * 8 + 9)
            pe.wait_ge(s.b_lo, l + 1)
            pe_out(pe, b, l, sub, mgb(l) + 24, OUT_Q, m1.ohi, m1.olo, None)
            pe_post(pe, b, sub)

        B_NORM = 44

        def act_mix1(act, l, nxt):
            b, s = b1, b1.s
            sub = l * 3 + 1
            U = l * UNITS1

            def hi_split(g):
                split_hi(act, b, mgb(l) + g, mgb2(l) + g // 2, g % 2)

            hi_split(2)
            act_rms(act, b, 2 * sub, SUM_PRE)
            act_r(act, b, 2 * sub, BC_PRE)
            hi_split(3)
            hi_split(4)
            def outputs(p_):
                act.wait_ge(s.pv_done, U + 8 * p_ + 8)
                if KINDS[p_] == "B":
                    act.activation(m1.ob[:, p_ - 3, :], ps[:, 3, :], ACT.Copy).then_inc(s.o_hi_out, 1)
                    if p_ == 4:
                        act.wait_ge(s.o_hi_out, l * 8 + p_ + 2)
                        act.activation(m1.sqb[:, :, :], m1.ob[:, :, :], ACT.Square).then_inc(s.b_act_steps, 1)
                else:
                    act.activation(m1.ohi[:, p_, :], ps[:, 3, :], ACT.Copy).then_inc(s.o_hi_out, 1)

            for n_step, st in enumerate(STEPS1):
                for v in st.tr:
                    act.wait_ge(s.transposed, l * len(TEV1) + TEV1["p", v] + 1)
                    if v >= 2:
                        act.wait_ge(s.pv_done, U + v - 1)
                    nn = unit1(v)[4]
                    act.activation(m1.pt[v % 2][:, :, :].rearrange("p a b -> p (a b)")[:, 0:nn], ps[:, 2, 0:nn],
                                   ACT.Copy).then_inc(s.transposed_out, 1)
                if n_step > 0:
                    for p_ in STEPS1[n_step - 1].pairs:
                        outputs(p_)
                u = st.sc
                if u is not None:
                    p, h, j, kind, n = unit1(u)
                    w3 = m1.w[u % 3]
                    if kind in "AB":
                        act.wait_ge(s.max_done, l * 40 + u + 1)
                        for m in range(2 if kind == "B" else 1):
                            w = w3[:, m, 0:n]
                            ins = act.activation(w, w, ACT.Exp, bias=m1.nmax[u % 3][:, m:m + 1],
                                                 scale=B_SCALE if kind == "B" else 1.0,
                                                 accum_out=m1.sums[u % 3][:, m:m + 1])
                        ins.then_inc(s.exp_done, 1)
                    else:
                        act.wait_ge(s.scores_done, U + u + 1)
                        act.wait_ge(s.transposed, l * len(TEV1) + TEV1["p", u - 3] + 1)
                        S_ = ps[:, sbank(u), 0:n]
                        act.activation(w3[:, 0, 0:n], S_, ACT.Sigmoid)
                        act.activation(w3[:, 1, 0:n], S_, ACT.Sigmoid, scale=-1.0).then_inc(s.exp_done, 1)
                        act.wait_ge(s.exp_done, U + u + 1)
                        act.sem_inc(s.scores_free, 1)
                if st.vt is not None:
                    act.wait_ge(s.transposed, l * len(TEV1) + TEV1["v", st.vt] + 1)
                    act.activation(m1.v[st.vt % 2][:, :, :].rearrange("p a b -> p (a b)"), ps[:, 2, :],
                                   ACT.Copy).then_inc(s.transposed_out, 1)
                for g in st.done:
                    hi_split(g + 2)
                if n_step == B_NORM:
                    act.wait_ge(s.b_sums, l + 1)
                    for c in range(2):
                        ins = act.activation(m1.rb[:, c, :], ps[:, 5 + 2 * c, 0:SEQ], ACT.Ln, bias=eps[:, :],
                                             scale=1.0 / 64)
                    ins.then_inc(s.b_act_steps, 1)
                    act.wait_ge(s.b_act_steps, l * 3 + 2)
                    act.activation(m1.rb[:, :, :], m1.rb[:, :, :], ACT.Exp, scale=-0.5).then_inc(s.b_act_steps, 1)
                if n_step == B_NORM + 2:
                    act.wait_ge(s.b_scaled, l + 1)
                    for c in range(2):
                        ins = act.activation(m1.ohi[:, 3 + c, :], m1.ob[:, c, :], ACT.Copy,
                                             scale=par[:, bass.ds(l + PAR_SUBLN, 1)])
                    ins.then_inc(s.b_hi, 1)
            outputs(7)
            act_out(act, b, l, sub, mgb(l) + 24, mgb2(l) + 12, OUT_Q)
            act_rms(act, b, 2 * sub + 1, SUM_POST)
            act_next(act, b, l, sub + 1, *nxt)

        def dve_mix1(dve, l, ch, nxt):
            b, s = b1, b1.s
            sub = l * 3 + 1
            U = l * UNITS1

            def evac(g):
                p, j = divmod(g, 3)
                dve.wait_ge(s.granules_done, mgb(l) + g + 1 + CR)
                dst = (m1.q, m1.k, m1.vt)[j][p % 2]
                factor = 0.125 if j == 0 and KINDS[p] != "B" else 1.0
                dve.scalar_tensor_tensor(out=dst[:, :], in0=ps[:, g % 2, :], scalar=factor, in1=r[:, 0:SEQ],
                                         op0=ALU.mult, op1=ALU.mult).then_inc(s.columns_out, 1)

            dve_diag(dve, b, 2 * sub, ch)
            dve.wait_ge(s.norm_r, sub + 1)
            evac(0)
            evac(1)
            evac(2)
            dve.wait_ge(s_tb, 16 * l + 16)
            ch(dve.memset(tb[0:64, :, SEQ - 64:SEQ], NEG))
            ch.wait()
            ch(dve.memset(m1.scan[:, SEQ:SEQ + 1], 1.0))

            def probabilities(u):
                p, h, j, kind, n = unit1(u)
                w3 = m1.w[u % 3]
                w = w3[:, 0, 0:n]
                dve.wait_ge(s.exp_done, U + u + 1)
                if kind == "A":
                    ch(dve.reciprocal(m1.inv[u % 3][:, 0:1], m1.sums[u % 3][:, 0:1]))
                    ch.wait()
                    dve.tensor_scalar(w, w, m1.inv[u % 3][:, 0:1], None, ALU.mult).then_inc(s.probs_done, 1)
                elif kind == "B":
                    ch(dve.reciprocal(m1.inv[u % 3][:, 0:2], m1.sums[u % 3][:, 0:2]))
                    ch.wait()
                    ch(dve.tensor_tensor(m1.c1[u % 3][:, :], m1.inv[u % 3][:, 1:2], nlam[:, bass.ds(l, 1)], ALU.mult))
                    ch.wait()
                    ch(dve.tensor_scalar(w3[:, 1, 0:n], w3[:, 1, 0:n], m1.c1[u % 3][:, 0:1], None, ALU.mult))
                    ch.wait()
                    dve.scalar_tensor_tensor(out=w, in0=w, scalar=m1.inv[u % 3][:, 0:1], in1=w3[:, 1, 0:n],
                                             op0=ALU.mult, op1=ALU.add).then_inc(s.probs_done, 1)
                else:
                    d = w3[:, 1, n - P:n]
                    ch(dve.tensor_tensor(d, d, later[:, :], ALU.max))
                    ch.wait()
                    ch(dve.tensor_tensor_scan(m1.scan[:, SEQ - n:SEQ][:, ::-1], w3[:, 1, 0:n][:, ::-1], ones[:, 0:n],
                                              1.0, ALU.mult, ALU.mult))
                    ch.wait()
                    ch(dve.tensor_tensor(w, w, m1.scan[:, SEQ - n + 1:SEQ + 1], ALU.mult))
                    ch.wait()
                    d = w3[:, 0, n - P:n]
                    dve.tensor_tensor(d, d, strict[:, :], ALU.mult).then_inc(s.probs_done, 1)

            def logits(u):
                p, h, j, kind, n = unit1(u)
                w3 = m1.w[u % 3]
                w = w3[:, 0, 0:n]
                dve.wait_ge(s.scores_done, U + u + 1)
                if u >= 3:
                    dve.wait_ge(s.transposed, l * len(TEV1) + TEV1["p", u - 3] + 1)
                if kind == "A":
                    head = 2 * p + h
                    ch(dve.tensor_tensor(w, ps[:, sbank(u), 0:n], tb[:, head, SEQ - n:SEQ], ALU.add))
                    ch.wait()
                    dve.sem_inc(s.scores_free, 1)
                    dve.tensor_reduce(m1.nmax[u % 3][:, 0:1], w, AX.X, ALU.max, negate=True).then_inc(s.max_done, 1)
                else:
                    head = 2 * (p - 3) + h
                    for m in range(2):
                        ch(dve.scalar_tensor_tensor(
                            out=w3[:, m, 0:n], in0=dist[:, SEQ - n:SEQ], scalar=-SLOPE[head] / B_SCALE,
                            in1=ps[:, sbank(u) + m, 0:n], op0=ALU.mult, op1=ALU.add))
                    ch.wait()
                    dve.sem_inc(s.scores_free, 1)
                    ch(dve.tensor_reduce(m1.nmax[u % 3][:, 0:2], w3[:, :, 0:n], AX.X, ALU.max, negate=True))
                    ch.wait()
                    dve.tensor_scalar(m1.nmax[u % 3][:, 0:2], m1.nmax[u % 3][:, 0:2], B_SCALE, None,
                                      ALU.mult).then_inc(s.max_done, 1)

            def outputs(p_):
                dve.wait_ge(s.o_hi_out, l * 8 + p_ + 2)
                if KINDS[p_] == "B":
                    dve.sem_inc(s.o_lo_out, 1)
                else:
                    dve.tensor_tensor(m1.olo[:, p_, :], ps[:, 3, :], m1.ohi[:, p_, :].bitcast(F32),
                                      ALU.subtract).then_inc(s.o_lo_out, 1)

            for n_step, st in enumerate(STEPS1):
                if 1 <= n_step <= UNITS1:
                    probabilities(n_step - 1)
                if st.sc is not None and KINDS[st.sc // 8] != "C":
                    logits(st.sc)
                if n_step > 0:
                    for p_ in STEPS1[n_step - 1].pairs:
                        outputs(p_)
                for g in st.done:
                    evac(g)
                if n_step == B_NORM + 1:
                    dve.wait_ge(s.b_act_steps, l * 3 + 3)
                    dve.tensor_tensor(m1.ob[:, :, :], m1.ob[:, :, :], m1.rb[:, :, :], ALU.mult).then_inc(s.b_scaled, 1)
                if n_step == B_NORM + 3:
                    dve.wait_ge(s.b_scaled, l + 1)
                    dve.wait_ge(s.b_hi, l + 1)
                    dve.scalar_tensor_tensor(out=m1.olo[:, 3:5, :], in0=m1.ob[:, :, :],
                                             scalar=par[:, bass.ds(l + PAR_SUBLN, 1)],
                                             in1=m1.ohi[:, 3:5, :].bitcast(F32), op0=ALU.mult,
                                             op1=ALU.subtract).then_inc(s.b_lo, 1)
            outputs(7)
            dve_out(dve, b, l, sub, mgb(l) + 24, OUT_Q, ch, 1.0, PAR_MIXPOST, nxt)


        def pool_mix1(pool, l):
            for g in range(2, 26):
                split_lo(pool, b1, mgb(l) + g, g % 2, handover=(g == 2))

        fg = Ffn(
            sub=lambda l: l * 2 + 1, gb=lambda l: l * b2.GL + MIX2_GRAN, gb2=lambda l: l * (b2.GL // 2) + MIX2_GRAN // 2,
            ev=lambda l: l * b2.evf_layer, hb=lambda l: l * KF,
            gate=I["ffn_w_up_2"].rearrange("l d f -> (l d) f"), up=I["ffn_w_up_2"].rearrange("l d f -> (l d) f"),
            upoff=FF, down=I["ffn_w_down_2"].rearrange("l f d -> (l f) d"))
        g2b = lambda l: l * b2.GL
        g2b2 = lambda l: l * (b2.GL // 2)
        win2 = I["w_in_2"].rearrange("l d f -> (l d) f")
        wout2 = I["w_out_2"].rearrange("l d f -> (l d) f")
        pw2 = I["a_pw_w_2"].rearrange("l d f -> (l d) f")
        NCOL = len(COLS2)

        def sp_mix2(sp, l):
            for g, c0 in enumerate(COLS2):
                row = l * D if c0 else l * KD * P
                load_raw(sp, b2, g2b(l) + g, g % 2, win2[bass.ds(row, D), c0:c0 + P], (8, P))
            load_raw(sp, b2, g2b(l) + NCOL, NCOL % 2, pw2[bass.ds(l * 2 * P, 2 * P), :], (2, PAIR))
            sp_wout(sp, b2, l, g2b(l) + NCOL + 1, wout2)

        def n_of(g):
            return 512 if g == NCOL else 1024

        def gbank(g):
            return 2 if g < 8 and g % 2 == 0 else 0

        def unit2(u):
            p, qb, h = u // (2 * QB), (u // 2) % QB, u % 2
            return p, qb, h, (0 if qb == 0 else META + P * (qb - 1)), (META if qb == 0 else P), META + P * qb

        def s2(u, n):
            bank = 4 + 2 * (u % 2)
            return ps[:, bank:bank + 2, :].rearrange("p a b -> p (a b)")[:, SEQ - META:SEQ - META + n]

        HEADS_ORDER = [0, 1, 2, 3, 6, 7, 4, 5]

        def pe_mix2(pe, l):
            b, s = b2, b2.s
            sub = l * 2
            U = l * UNITS2
            TE = l * len(TEV2)

            def gtile(g, t):
                if t == 0:
                    pe.wait_ge(s.weights_split, g2b(l) + g + 1 + CR)
                    if g >= 2:
                        pe.wait_ge(s.columns_out, l * NCOL + g + CR - (1 if g < 8 else 0))
                if g == 0:
                    pe.wait_ge(s.x_lo, 8 * sub + t + 1)
                ins = tile_mm(pe, b, gbank(g), g % 2, t * P, xhi[:, t, :], xlo[:, t, :], t == 0, t == 7)
                if t == 7:
                    ins.then_inc(s.granules_done, 1)

            def scores(u):
                p, qb, h, t0, nq, n = unit2(u)
                pe.wait_ge(s.columns_out, l * NCOL + QKV2[p] + 2 + CR)
                pe.wait_ge(s.scores_free, U + u + 1)
                bank = 4 + 2 * (u % 2)
                a = 64 * h
                lhs = m2.q[p % 2][a:a + 64, t0:t0 + P]
                ins = pe.matmul(ps[:, bank, SEQ - META:SEQ], lhs, m2.k[p % 2][a:a + 64, 0:META], start=True, stop=True)
                if qb:
                    ins = pe.matmul(ps[0:nq, bank + 1, 0:P * qb], lhs, m2.k[p % 2][a:a + 64, META:n],
                                    start=True, stop=True)
                ins.then_inc(s.scores_done, 1)

            def vtrans(p):
                pe.wait_ge(s.columns_out, l * NCOL + QKV2[p] + 3 + CR)
                pe.wait_ge(s.transposed_out, TE + TEV2["v", p] + 1)
                pe.wait_ge(s.scores_free, U + 2 * QB * p + 1 + CR)
                pe.transpose(ps[0:META, 4, 0:P], m2.vt[p % 2][:, 0:META], ident[:, :])
                for t in range(4):
                    t0 = META + P * t
                    ins = pe.transpose(ps[:, 2, P * t:P * t + P], m2.vt[p % 2][:, t0:t0 + P], ident[:, :])
                ins.then_inc(s.transposed, 1)

            def ptrans(u):
                p, qb, h, t0, nq, n = unit2(u)
                pe.wait_ge(s.probs_done, U + u + 1)
                pe.wait_ge(s.transposed_out, TE + TEV2["p", u] + 1)
                pe.wait_ge(s.scores_free, U + min(u + 2, UNITS2) + CR)
                ins = pe.transpose(ps[0:META, 6 - 2 * (u % 2), 0:P], m2.w[u % 3][:, 0:META], ident[:, :])
                for t in range(qb):
                    ins = pe.transpose(ps[:, 2, P * t:P * t + P], m2.w[u % 3][:, META + P * t:META + P * t + P], ident[:, :])
                ins.then_inc(s.transposed, 1)

            def pv(u):
                p, qb, h, t0, nq, n = unit2(u)
                pe.wait_ge(s.transposed_out, TE + TEV2["p", u] + 2)
                if h == 0 and qb < 2:
                    pe.wait_ge(s.o_hi_out, l * 8 + 2 * p + qb + 1)
                c0 = P * max(qb - 1, 0)
                o = ps[64 * h:64 * h + 64, 3, c0:c0 + nq]
                ins = pe.matmul(o, m2.v[p % 2][0:META, 0, 64 * h:64 * h + 64], m2.pt[u % 2][0:META, 0, 0:nq],
                                start=True, stop=(qb == 0))
                for t in range(qb):
                    ins = pe.matmul(o, m2.v[p % 2][:, 1 + t, 64 * h:64 * h + 64], m2.pt[u % 2][:, 1 + t, :],
                                    start=False, stop=(t == qb - 1))
                ins.then_inc(s.pv_done, 1)

            def forget(h):
                pe.wait_ge(s.forget_sums, l + 1)
                if h >= 2:
                    pe.wait_ge(s.forget_out, l * 8 + h - 1)
                for i, (t0, w) in enumerate(halves(b)):
                    ins = pe.matmul(ps[:, 4 + 2 * (h % 2) + i, 0:w], ident[0:8, h:h + 1].to_broadcast([8, P]), m2.nf[:, t0:t0 + w], start=True, stop=True)
                ins.then_inc(s.forget_spread, 1)

            pe.wait_ge(s.out_free, 4 * sub + CR)
            for g in range(8):
                for t in range(8):
                    gtile(g, t)
                if g == 0:
                    pe_pre_sum(pe, b, sub)
                if g == 1:
                    pe_bc(pe, b, 2 * sub, BC_PRE)
                    pe.wait_ge(s.norm_r, sub + 1)
                if g >= 4:
                    forget(2 * g - 8)
                    forget(2 * g - 7)
            pe.wait_ge(s.forget_out, l * 8 + 8)
            for st in STEPS2:
                for u in st.tr:
                    ptrans(u)
                if st.sc is not None:
                    scores(st.sc)
                for tile in st.tiles[:2]:
                    gtile(*tile)
                if st.vt is not None:
                    vtrans(st.vt)
                for tile in st.tiles[2:]:
                    gtile(*tile)
                for u in st.tr:
                    pv(u)
            for j in range(2):
                if j == 0:
                    pe.wait_ge(s.dw_taps, l * len(DW_OPS) + len(DW_OPS))
                else:
                    pe.wait_ge(s.ln_squared, l + 1)
                src = aconv if j == 0 else m2.lsq
                for i, (t0, w) in enumerate(halves(b)):
                    for c in range(2):
                        ins = pe.matmul(ps[:, 4 + 2 * j + i, 0:w], ones[:, 0:P], src[:, c, t0:t0 + w],
                                        start=(c == 0), stop=(c == 1))
                ins.then_inc(s.ln_sums, 1)
            for i, c in enumerate(HEADS_ORDER):
                if i == 6:
                    pe.wait_ge(s.weights_split, g2b(l) + NCOL + 1 + CR)
                    pe.wait_ge(s.a_lo, l + 1)
                    pe.wait_ge(s.o_hi_out, l * 8 + 9)
                    for o in range(2):
                        for k in range(2):
                            ins = tile_mm(pe, b, 2 * o, NCOL % 2, k * PAIR + o * P, m2.ahi[:, k, :], m2.alo[:, k, :],
                                          k == 0, k == 1)
                    ins.then_inc(s.granules_done, 1)
                pe.wait_ge(s.head_squared, l * 8 + i + 1)
                if i >= 2:
                    pe.wait_ge(s.head_steps, 2 * (l * 8 + i - 2) + 1)
                if i == 0:
                    pe.wait_ge(s.ln_centered, l + 1)
                if i == 1:
                    pe.wait_ge(s.ln_steps, l * 2 + 1)
                for j, (t0, w) in enumerate(halves(b)):
                    ins = pe.matmul(ps[:, 4 + 2 * (i % 2) + j, 0:w], bd[:, :], S[i % 2][:, t0:t0 + w], start=True, stop=True)
                ins.then_inc(s.head_sums, 1)
            pe.wait_ge(s.pw_out, l + 1)
            pe.wait_ge(s.head_steps, 2 * (l * 8 + 7) + 1)
            pe_out(pe, b, l, sub, g2b(l) + NCOL + 1, OUT_Q, m2.ohi, m2.olo,
                   lambda k: pe.wait_ge(s.head_lo, l * 8 + HEADS_ORDER.index(k) + 1))
            pe_post(pe, b, sub)

        def act_mix2(act, l, nxt):
            b, s = b2, b2.s
            sub = l * 2
            U = l * UNITS2
            TE = l * len(TEV2)

            def hi_split(g):
                split_hi(act, b, g2b(l) + g, g2b2(l) + g // 2, g % 2, n_of(g))

            def forget(h):
                act.wait_ge(s.forget_spread, l * 8 + h + 1)
                act.activation(tview(b, fb[:, h, :]), pview(b, 4 + 2 * (h % 2)), ACT.Copy).then_inc(s.forget_out, 1)

            hi_split(2)
            act_rms(act, b, 2 * sub, SUM_PRE)
            act_r(act, b, 2 * sub, BC_PRE)
            hi_split(3)
            act.wait_ge(s.forget_in, l + 1)
            act.activation(m2.e[:, :], m2.u[:, :], ACT.Abs).then_inc(s.forget_steps, 1)
            act.wait_ge(s.forget_steps, l * 3 + 1)
            act.activation(m2.e[:, :], m2.e[:, :], ACT.Exp, scale=-1.0).then_inc(s.forget_steps, 1)
            act.wait_ge(s.forget_steps, l * 3 + 2)
            act.activation(m2.e[:, :], m2.e[:, :], ACT.Ln, bias=1.0).then_inc(s.forget_steps, 1)
            for g in range(2, 8):
                hi_split(g + 2)
                if g == 4:
                    act.wait_ge(s.a_gate_in, l + 1)
                    act.activation(aconv[:, :, :], aconv[:, :, :], ACT.Sigmoid).then_inc(s.a_gate_done, 1)
                if g >= 4:
                    forget(2 * g - 8)
                    forget(2 * g - 7)
            def outputs(v):
                p, qb, h, t0, nq, n = unit2(v)
                if h == 1 and qb in (0, QB - 1):
                    act.wait_ge(s.pv_done, U + v + 1)
                    dst, src = (y[:, p, 0:META], ps[:, 3, 0:META]) if qb == 0 else (y[:, p, META:TM], ps[:, 3, :])
                    act.activation(dst, src, ACT.Copy).then_inc(s.o_hi_out, 1)

            for n_step, st in enumerate(STEPS2):
                for v in st.tr:
                    p, qb, h, t0, nq, n = unit2(v)
                    act.wait_ge(s.transposed, TE + TEV2["p", v] + 1)
                    if v >= 2:
                        act.wait_ge(s.pv_done, U + v - 1)
                    ins = act.activation(m2.pt[v % 2][0:META, 0, :], ps[0:META, 6 - 2 * (v % 2), 0:P], ACT.Copy)
                    if qb:
                        ins = act.activation(m2.pt[v % 2][:, 1:1 + qb, :].rearrange("p a b -> p (a b)"),
                                             ps[:, 2, 0:P * qb], ACT.Copy)
                    ins.then_inc(s.transposed_out, 1)
                if n_step > LAG:
                    outputs(n_step - LAG - 1)
                if 1 <= n_step <= UNITS2:
                    u = n_step - 1
                    w = m2.w[u % 3][:, 0:unit2(u)[5]]
                    act.wait_ge(s.inv_done, U + u + 1)
                    act.activation(w, w, ACT.Copy, scale=m2.inv[u % 3][:, :]).then_inc(s.probs_done, 1)
                u = st.sc
                if u is not None:
                    p, qb, h, t0, nq, n = unit2(u)
                    act.wait_ge(s.max_done, U + u + 1)
                    w = m2.w[u % 3][:, 0:n]
                    act.activation(w, w, ACT.Exp, bias=m2.nmax[u % 3][:, :], scale=1.0,
                                   accum_out=m2.sums[u % 3][:, :]).then_inc(s.exp_done, 1)
                if st.vt is not None:
                    act.wait_ge(s.transposed, TE + TEV2["v", st.vt] + 1)
                    act.activation(m2.v[st.vt % 2][0:META, 0, :], ps[0:META, 4, 0:P], ACT.Copy)
                    act.activation(m2.v[st.vt % 2][:, 1:QB, :].rearrange("p a b -> p (a b)"), ps[:, 2, :],
                                   ACT.Copy).then_inc(s.transposed_out, 1)
                for g in st.done:
                    hi_split(g + 2)
            outputs(UNITS2 - 1)
            act_heads(act, l)
            act_out(act, b, l, sub, g2b(l) + NCOL + 1, g2b2(l) + (NCOL + 1) // 2, OUT_Q)
            act_rms(act, b, 2 * sub + 1, SUM_POST)
            act_next(act, b, l, sub + 1, *nxt)

        def act_heads(act, l):
            b, s = b2, b2.s

            def square(i):
                c = HEADS_ORDER[i]
                if c < 4:
                    act.wait_ge(s.o_hi_out, l * 8 + 2 * c + 3)
                elif c >= 6:
                    act.wait_ge(s.short_done, l * 2 + c - 5)
                else:
                    act.wait_ge(s.pw_out, l + 1)
                if i >= 2:
                    act.wait_ge(s.head_sums, l * 8 + i - 1)
                act.activation(S[i % 2][:, 0:TM], y[:, c, :], ACT.Square).then_inc(s.head_squared, 1)

            def inverse(i):
                act.wait_ge(s.head_sums, l * 8 + i + 1)
                if i >= 2:
                    act.wait_ge(s.head_scaled, l * 8 + i - 1)
                t = tview(b, S[2 + i % 2][:, 0:TM])
                act.activation(t, pview(b, 4 + 2 * (i % 2)), ACT.Ln, bias=eps[:, :], scale=1.0 / 64).then_inc(s.head_steps, 1)
                act.wait_ge(s.head_steps, 2 * (l * 8 + i) + 1)
                act.activation(t, t, ACT.Exp, scale=-0.5).then_inc(s.head_steps, 1)

            def hi(i):
                c = HEADS_ORDER[i]
                act.wait_ge(s.head_scaled, l * 8 + i + 1)
                act.activation(m2.ohi[:, c, :], y[:, c, :], ACT.Copy, scale=gain(PAR_HEADG, l, c)).then_inc(s.head_hi, 1)

            square(0)
            square(1)
            act.wait_ge(s.ln_centered, l + 1)
            act.activation(m2.lsq[:, :, :], aconv[:, :, :], ACT.Square).then_inc(s.ln_squared, 1)
            act.wait_ge(s.ln_sums, l * 2 + 2)
            t = tview(b, m2.lrs[:, :])
            act.activation(t, pview(b, 6), ACT.Ln, bias=lneps[:, :], scale=1.0 / 256).then_inc(s.ln_steps, 1)
            act.wait_ge(s.ln_steps, l * 2 + 1)
            act.activation(t, t, ACT.Exp, scale=-0.5).then_inc(s.ln_steps, 1)
            inverse(0)
            inverse(1)
            square(2)
            square(3)
            inverse(2)
            inverse(3)
            square(4)
            square(5)
            inverse(4)
            inverse(5)
            act.wait_ge(s.ln_scaled, l + 1)
            for c in range(2):
                ins = act.activation(aconv[:, c, :], aconv[:, c, :], ACT.Silu,
                                     bias=par[:, bass.ds(l * 2 + (PAR_LNB + c), 1)],
                                     scale=par[:, bass.ds(l * 2 + (PAR_LNG + c), 1)])
            ins.then_inc(s.ln_silu, 1)
            act.wait_ge(s.ln_silu, 2 * l + 1)
            act.activation(m2.ahi[:, :, :], aconv[:, :, :], ACT.Copy).then_inc(s.ln_silu, 1)
            for i in range(6):
                if i == 0:
                    act.wait_ge(s.a_lo, l + 1)
                hi(i)
            act.wait_ge(s.granules_done, g2b(l) + NCOL + 1 + CR)
            for o in range(2):
                ins = act.activation(tview(b, y[:, 4 + o, :]), pview(b, 2 * o), ACT.Copy)
            ins.then_inc(s.pw_out, 1)
            split_hi(act, b, g2b(l) + NCOL + 2, g2b2(l) + (NCOL + 1) // 2, (NCOL + 2) % 2)
            for i in (6, 7):
                square(i)
            for i in (6, 7):
                inverse(i)
            for i in (6, 7):
                hi(i)

        def dve_mix2(dve, l, ch, nxt):
            b, s = b2, b2.s
            sub = l * 2
            U = l * UNITS2
            TE = l * len(TEV2)

            def scaled(dst, g, rows=P, factor=None):
                src = ps[0:rows, gbank(g):gbank(g) + 2, 0:b.w]
                rr = tview(b, r[0:rows, 0:TM])
                if factor is None:
                    return dve.tensor_tensor(tview(b, dst), src, rr, ALU.mult)
                return dve.scalar_tensor_tensor(out=tview(b, dst), in0=src, scalar=factor, in1=rr,
                                                op0=ALU.mult, op1=ALU.mult)

            def evac(g):
                dve.wait_ge(s.granules_done, g2b(l) + g + 1 + CR)
                if g == 0:
                    dst = m2.u[:, :]
                elif g < 5:
                    c = (g - 1) // 2
                    dst = aconv[:, c, :] if g % 2 == 0 else apad[:, c, TAPS - 1:]
                elif g in SC_B2 + SC_C2 + SC_X2:
                    dst = scb[:, :] if g in SC_B2 else scc[:, :] if g in SC_C2 else scx[:, 2:]
                else:
                    p = max(i for i in range(4) if g >= QKV2[i])
                    dst = (m2.q, m2.k, m2.vt)[g - QKV2[p]][p % 2][:, :]
                scaled(dst, g, 8 if g == 0 else P, 0.125 if g in QKV2 else None).then_inc(s.columns_out, 1)

            def short_conv(c):
                dve.wait_ge(s.columns_out, l * NCOL + SC_X2[c] + 1 + CR)
                ch(dve.tensor_tensor(scx[:, 2:], scx[:, 2:], scc[:, :], ALU.mult))
                ch.wait()
                for k in (2, 1, 0):
                    w = par[:, bass.ds(l * 6 + (PAR_SCW + 2 * k + c), 1)]
                    if k == 2:
                        ch(dve.tensor_scalar(scc[:, :], scx[:, 2:2 + TM], w, None, ALU.mult))
                    else:
                        ch(dve.scalar_tensor_tensor(out=scc[:, :], in0=scx[:, k:k + TM], scalar=w, in1=scc[:, :],
                                                    op0=ALU.mult, op1=ALU.add))
                    ch.wait()
                dve.tensor_tensor(y[:, 6 + c, :], scb[:, :], scc[:, :], ALU.mult).then_inc(s.short_done, 1)

            dw_at = [0]

            def depthwise(n):
                for t, c in DW_OPS[dw_at[0]:dw_at[0] + n]:
                    w = par[:, bass.ds(l * 2 * TAPS + (PAR_DW + 2 * t + c), 1)]
                    src, dst = apad[:, c, t:t + TM], aconv[:, c, :]
                    if t == 0:
                        dve.tensor_scalar(dst, src, w, par[:, bass.ds(l * 2 + (PAR_DWB + c), 1)], ALU.mult,
                                          ALU.add).then_inc(s.dw_taps, 1)
                    else:
                        dve.wait_ge(s.dw_taps, l * len(DW_OPS) + 2 * (t - 1) + c + 1)
                        dve.scalar_tensor_tensor(out=dst, in0=src, scalar=w, in1=dst, op0=ALU.mult,
                                                 op1=ALU.add).then_inc(s.dw_taps, 1)
                dw_at[0] += n

            dve_diag(dve, b, 2 * sub, ch)
            ch(dve.memset(apad[:, :, 0:TAPS - 1], 0.0))
            ch(dve.memset(scx[:, 0:2], 0.0))
            dve.wait_ge(s.norm_r, sub + 1)
            evac(0)
            dve.wait_ge(s.columns_out, l * NCOL + 1 + CR)
            dve.tensor_scalar(m2.u[:, :], m2.u[:, :], bf[:, bass.ds(l, 1)], None, ALU.add).then_inc(s.forget_in, 1)
            evac(1)
            dve.wait_ge(s.forget_steps, l * 3 + 3)
            ch(dve.scalar_tensor_tensor(out=m2.lf[:, :], in0=m2.u[:, :], scalar=0.0, in1=m2.e[:, :], op0=ALU.min,
                                        op1=ALU.subtract))
            ch.wait()
            for a, n in ((0, SEQ), (SEQ, META)):
                ch(dve.tensor_tensor_scan(m2.nf[:, a:a + n], ones[0:8, 0:n], m2.lf[:, a:a + n],
                                          0.0 if a == 0 else m2.nf[:, a - 1:a], ALU.mult, ALU.subtract))
                ch.wait()
            dve.sem_inc(s.forget_sums, 1)
            for g in range(2, 8):
                evac(g)
                if g == 4:
                    dve.wait_ge(s.columns_out, l * NCOL + 5 + CR)
                    dve.sem_inc(s.a_gate_in, 1)
                if g == 5:
                    dve.wait_ge(s.a_gate_done, l + 1)
                    ch(dve.tensor_tensor(apad[:, :, TAPS - 1:], apad[:, :, TAPS - 1:], aconv[:, :, :], ALU.mult))
                    ch.wait()
            dve.wait_ge(s.forget_out, l * 8 + 8)
            for n_step, st in enumerate(STEPS2):
                if 1 <= n_step <= UNITS2:
                    u = n_step - 1
                    dve.wait_ge(s.exp_done, U + u + 1)
                    dve.reciprocal(m2.inv[u % 3][:, :], m2.sums[u % 3][:, :]).then_inc(s.inv_done, 1)
                u = st.sc
                if u is not None:
                    p, qb, h, t0, nq, n = unit2(u)
                    w = m2.w[u % 3]
                    dve.wait_ge(s.scores_done, U + u + 1)
                    if u >= 3:
                        dve.wait_ge(s.transposed, TE + TEV2["p", u - 3] + 1)
                    ch(dve.tensor_tensor(w[:, 0:n], s2(u, n)[:, :], fb[:, 2 * p + h, 0:n], ALU.add))
                    ch.wait()
                    dve.sem_inc(s.scores_free, 1)
                    ch(dve.tensor_tensor(w[:, n - nq:n], w[:, n - nq:n], negc[:, 0:nq], ALU.add))
                    ch.wait()
                    dve.tensor_reduce(m2.nmax[u % 3][:, :], w[:, 0:n], AX.X, ALU.max, negate=True).then_inc(s.max_done, 1)
                for g in st.done:
                    evac(g)
                    if g in SC_X2:
                        short_conv(SC_X2.index(g))
                depthwise(DW_PER_STEP)
            assert dw_at[0] >= len(DW_OPS)
            dve.wait_ge(s.ln_sums, l * 2 + 1)
            for c in range(2):
                ch(dve.scalar_tensor_tensor(out=tview(b, aconv[:, c, :]), in0=pview(b, 4), scalar=-1.0 / 256,
                                            in1=tview(b, aconv[:, c, :]), op0=ALU.mult, op1=ALU.add))
            ch.wait()
            dve.sem_inc(s.ln_centered, 1)
            dve.wait_ge(s.ln_steps, l * 2 + 2)
            dve.tensor_tensor(aconv[:, :, :], aconv[:, :, :], m2.lrs[:, :].unsqueeze(1).to_broadcast([P, 2, TM]),
                              ALU.mult).then_inc(s.ln_scaled, 1)

            def mul(i):
                c = HEADS_ORDER[i]
                dve.wait_ge(s.head_steps, 2 * (l * 8 + i) + 2)
                dve.tensor_tensor(y[:, c, :], y[:, c, :], S[2 + i % 2][:, 0:TM], ALU.mult).then_inc(s.head_scaled, 1)

            def lo(i):
                c = HEADS_ORDER[i]
                dve.wait_ge(s.head_hi, l * 8 + i + 1)
                dve.scalar_tensor_tensor(out=m2.olo[:, c, :], in0=y[:, c, :], scalar=gain(PAR_HEADG, l, c),
                                         in1=m2.ohi[:, c, :].bitcast(F32), op0=ALU.mult,
                                         op1=ALU.subtract).then_inc(s.head_lo, 1)

            for i in range(6):
                mul(i)
            dve.wait_ge(s.ln_silu, 2 * l + 2)
            dve.tensor_tensor(m2.alo[:, :, :], aconv[:, :, :], m2.ahi[:, :, :].bitcast(F32),
                              ALU.subtract).then_inc(s.a_lo, 1)
            for i in range(6):
                lo(i)
            split_lo(dve, b, g2b(l) + NCOL + 2, (NCOL + 2) % 2, handover=True)
            mul(6)
            mul(7)
            lo(6)
            lo(7)
            dve_out(dve, b, l, sub, g2b(l) + NCOL + 1, OUT_Q, ch, 1.0, PAR_MIXPOST2, nxt)

        def pool_mix2(pool, l):
            for g in range(2, NCOL + 2):
                split_lo(pool, b2, g2b(l) + g, g % 2, n_of(g), handover=(g == 2))

        def rows(name):
            t = I[name]
            return t.rearrange("l (c p) -> (l c) p", p=P)

        P1 = ["ffn1_pre_g", "ffn1_post_g", "mix_pre_g", "mix_post_g", "ffn2_pre_g", "ffn2_post_g"]
        P2 = ["mix_pre_g_2", "mix_post_g_2", "ffn_pre_g_2", "ffn_post_g_2", "head_g_2"]
        P2B = ["a_dw_b_2", "a_ln_g_2", "a_ln_b_2"]
        PSIZE = [96, 106, 124, 88, 88, 88]
        PCOL = [0, 96, 202, 326, 414, 502]
        NLD_PAR = 6 + 5 + 3 + 2 + 1 + 1 + 6

        def sp_setup(sp):
            sp.dma_start(xin, I["x"].rearrange("b (a p) d -> p (b a) d", p=P)).then_inc(s_ld[0], 16)
            sp.dma_start(metain[:, :], I["meta_tokens_2"]).then_inc(s_ld[1], 16)
            for i, n_ in enumerate(P1):
                sp.dma_start(prow[0][16 * i:16 * i + 16, :], rows(n_)).then_inc(s_ld[2], 16)
            for i, n_ in enumerate(P2):
                sp.dma_start(prow[1][16 * i:16 * i + 16, :], rows(n_)).then_inc(s_ld[2], 16)
            for i, n_ in enumerate(P2B):
                sp.dma_start(prow[1][80 + 4 * i:84 + 4 * i, :], rows(n_)).then_inc(s_ld[2], 16)
            for i in range(2):
                sp.dma_start(prow[1][92:94, 64 * i:64 * i + 64], I["diff_subln_g"]).then_inc(s_ld[2], 16)
            sp.dma_start(prow[1][94:106, :], I["sc_conv_w_2"].rearrange("l k (c p) -> (l k c) p", p=P)).then_inc(s_ld[2], 16)
            sp.dma_start(prow[2][0:124, :], I["a_dw_w_2"].rearrange("l k (c p) -> (l k c) p", p=P)).then_inc(s_ld[2], 16)
            for k in range(3):
                for l in range(LAYERS):
                    sp.dma_start(prow[3 + k][44 * l:44 * l + 44, :],
                                 I["ffn_conv_w_2"][l, k, :].rearrange("(c p) -> c p", p=P)).then_inc(s_ld[2], 16)
            sp.dma_start(relin[:, :], I["rel_bias"].rearrange("l h r -> (l h) r")).then_inc(s_ld[3], 16)
            for i, n_ in enumerate(["diff_lambda_q1", "diff_lambda_k1", "diff_lambda_q2", "diff_lambda_k2"]):
                sp.dma_start(lam_in[:, i, :, :].rearrange("p l d -> p (l d)"),
                             I[n_].rearrange("l d -> (l d)").partition_broadcast(P)).then_inc(s_ld[4], 16)
            with nc.allow_non_contiguous_dma(reason="sixteen forget biases"):
                sp.dma_start(bf[:, :], I["b_forget_2"].rearrange("l h -> h l")).then_inc(s_ld[5], 16)
            sp.wait_ge(s_rev, 2)
            sp.dma_start(rev_dram, rev[:, :]).then_inc(s_revd, 16)
            sp.wait_ge(s_revd, 16)
            b0 = rev_dram[0:1, P - 1:P]
            src = bass.AP(tensor=b0.tensor, offset=b0.offset, ap=[[640, 12], [-1, P], [1, SEQ]])
            sp.dma_start(tbias_dram, src).then_inc(s_tbias, 16)

        def pool_setup(pool):
            pool.memset(ident[:, :], 0.0).then_inc(s_mask, 1)
            pool.wait_ge(s_mask, 1)
            pool.affine_select(out=ident[:, :], in_=ident[:, :], compare_op=ALU.not_equal, fill=1.0, base=0,
                               pattern=[[-1, P]], channel_multiplier=1).then_inc(s_const, 1)

            pool.iota(dist[:, :], pattern=[[-1, SEQ]], base=SEQ - P, channel_multiplier=1,
                      allow_small_or_imprecise_dtypes=True).then_inc(s_set, 1)
            pool.memset(strict[:, :], 1.0).then_inc(s_set, 1)
            pool.memset(later[:, :], 0.0).then_inc(s_set, 1)
            pool.memset(bd[:, :], 0.0).then_inc(s_set, 1)
            pool.wait_ge(s_set, 4)
            pool.affine_select(out=strict[:, :], in_=strict[:, :], compare_op=ALU.is_gt, fill=0.0, base=0,
                               pattern=[[-1, P]], channel_multiplier=1).then_inc(s_set, 1)
            pool.affine_select(out=later[:, :], in_=later[:, :], compare_op=ALU.is_gt, fill=1.0, base=0,
                               pattern=[[-1, P]], channel_multiplier=1).then_inc(s_set, 1)
            for h in range(2):
                pool.wait_ge(s_set, 6 + h)
                pool.memset(bd[64 * h:64 * h + 64, 64 * h:64 * h + 64], 1.0).then_inc(s_set, 1)
            pool.wait_ge(s_dist, 1)
            pool.memset(dist[0:64, SEQ - 64:SEQ], -NEG).then_inc(s_set, 1)
            pool.memset(negc[:, :], 0.0).then_inc(s_set, 1)
            pool.wait_ge(s_set, 10)
            pool.affine_select(out=negc[:, :], in_=negc[:, :], compare_op=ALU.is_ge, fill=NEG, base=0,
                               pattern=[[-1, P]], channel_multiplier=1).then_inc(s_set, 1)

        def dve_setup(dve, ch):
            dve.memset(ones[:, :], 1.0).then_inc(s_ones, 1)
            dve.memset(eps[:, :], EPS).then_inc(s_ones, 1)
            dve.memset(lneps[:, :], LN_EPS).then_inc(s_ones, 1)
            for sm in (b1.s.weights_split, b1.s.hidden_free, b1.s.columns_out, b1.s.scores_free, b2.s.hidden_free, b2.s.columns_out, b2.s.scores_free):
                dve.sem_inc(sm, CR)
            dve.sem_inc(b1.s.o_lo_out, 1)
            for c in range(KD):
                dve.wait_ge(s_xt, c + 1)
                dve.tensor_copy(x[:, c, META:TM], ps[:, c, :]).then_inc(b1.s.x_new, 1)
            dve.wait_ge(s_xt, KD + 1)
            ch(dve.tensor_copy(x[:, :, 0:META], ps[:, 0, 0:KD * META].rearrange("p (k t) -> p k t", k=KD)))
            ch.wait()
            dve.sem_inc(s_xc, 1)
            for i in range(6):
                dve.wait_ge(s_pt, i + 1)
                ins = dve.tensor_copy(par[:, PCOL[i]:PCOL[i] + PSIZE[i]], ps[:, 1 + i, 0:PSIZE[i]])
                ins.then_inc(s_pc, 1)
            dve.wait_ge(s_pc, 6)
            for l in range(LAYERS):
                li = 0.8 - 0.6 * math.exp(-0.3 * l)
                c = PAR_SUBLN + l
                ch(dve.tensor_scalar(par[:, c:c + 1], par[:, c:c + 1], 1.0 - li, None, ALU.mult))
            dve.wait_ge(s_ones, 3)
            dve.wait_ge(s_set, 11)
            dve.wait_ge(s_ld[5], 16)
            dve.wait_ge(s_ld[3], 16)
            dve.tensor_copy(rev[:, 640 - 257:640], relin[:, ::-1]).then_inc(s_rev, 1)
            dve.tensor_scalar(rev[:, 0:640 - 257], ones[0:12, 0:640 - 257], relin[:, 256:257], None,
                              ALU.mult).then_inc(s_rev, 1)
            dve.wait_ge(s_ld[4], 64)
            for i in range(2):
                ch(dve.tensor_tensor(lam_pr[:, i, :, :], lam_in[:, 2 * i, :, :], lam_in[:, 2 * i + 1, :, :], ALU.mult))
            ch.wait()
            dve.tensor_reduce(lam_s[:, :, :], lam_pr[:, :, :, :], AX.X, ALU.add).then_inc(s_lam, 1)
            dve.wait_ge(s_lam, 2)
            ch(dve.tensor_tensor(nlam[:, :], lam_e[:, 1, :], lam_e[:, 0, :], ALU.subtract))
            ch.wait()
            for l in range(LAYERS):
                li = 0.8 - 0.6 * math.exp(-0.3 * l)
                ch(dve.tensor_scalar(nlam[:, l:l + 1], nlam[:, l:l + 1], -li, None, ALU.add))
            ch.wait()

        def act_setup(act):
            for b in (b1, b2):
                act.sem_inc(b.s.out_free, CR)
                act.sem_inc(b.s.o_hi_out, 1)
                act.sem_inc(b.s.transposed_out, 1)
            act.wait_ge(s_set, 8)
            act.activation(dist[:, :], dist[:, :], ACT.Abs).then_inc(s_dist, 1)
            act.wait_ge(s_lam, 1)
            act.activation(lam_e[:, :, :], lam_s[:, :, :], ACT.Exp).then_inc(s_lam, 1)
            act.wait_ge(s_pc, 6)
            act.wait_ge(s_ones, 3)

        def pe_setup(pe):
            pe.sem_inc(b1.s.granules_done, CR)
            pe.wait_ge(s_const, 1)
            pe.wait_ge(s_ld[0], 16)
            for c in range(KD):
                for a in range(4):
                    ins = pe.transpose(ps[:, c, P * a:P * a + P], xin[:, a, P * c:P * c + P], ident[:, :])
                ins.then_inc(s_xt, 1)
            pe.wait_ge(s_ld[1], 16)
            pe.wait_ge(b1.s.x_new, 8)
            for c in range(KD):
                ins = pe.transpose(ps[:, 0, META * c:META * c + META], metain[:, P * c:P * c + P], ident[0:META, 0:META])
            ins.then_inc(s_xt, 1)
            pe.wait_ge(s_ld[2], 16 * NLD_PAR)
            for i in range(6):
                n_ = PSIZE[i]
                pe.transpose(ps[:, 1 + i, 0:n_], prow[i][0:n_, :], ident[0:n_, 0:n_]).then_inc(s_pt, 1)
            pe.wait_ge(s_ones, 3)
            pe.wait_ge(s_pc, 6)
            pe.wait_ge(s_xc, 1)
            pe.wait_ge(s_set, 11)
            pe.wait_ge(s_ld[5], 16)

        block = ctx.enter_context(nc.Block())

        nx_m1 = (PAR_MIXPRE, mgb, mgb2)
        nx_f2 = (PAR_FF2PRE, f2.gb, f2.gb2)

        @block.sync
        def _(sp):
            sp_setup(sp)
            with sp.Fori(0, LAYERS) as l:
                sp_ffn(sp, b1, l, f1)
                sp_mix1(sp, l)
                sp_ffn(sp, b1, l, f2)
            with sp.Fori(0, LAYERS) as l:
                sp_mix2(sp, l)
                sp_ffn(sp, b2, l, fg)
            for a in range(4):
                sp.wait_ge(s_oc, a + 1)
                sp.dma_start(out[0, P * a:P * a + P, :], xin[:, a, :]).then_inc(s_out, 16)
            sp.wait_ge(s_out, 64)

        @block.gpsimd
        def _(pool):
            pool_setup(pool)
            with pool.Fori(0, LAYERS) as l:
                pool_first(pool, b1, l, f1.gb)
                pool_x(pool, b1, l * 3)
                pool_y(pool, b1, l * 3)
                pool_x(pool, b1, l * 3 + 1)
                pool_mix1(pool, l)
                pool_y(pool, b1, l * 3 + 1)
                pool_x(pool, b1, l * 3 + 2)
                pool_y(pool, b1, l * 3 + 2)
            with pool.Fori(0, LAYERS) as l:
                pool_first(pool, b2, l, g2b)
                pool_x(pool, b2, l * 2)
                pool_mix2(pool, l)
                pool_y(pool, b2, l * 2)
                pool_x(pool, b2, l * 2 + 1)
                pool_y(pool, b2, l * 2 + 1)

        @block.scalar
        def _(act):
            act_setup(act)
            with act.Fori(0, LAYERS) as l:
                act_next(act, b1, l, l * 3, PAR_FF1PRE, f1.gb, f1.gb2)
                act_ffn(act, b1, l, f1, nx_m1)
                act_mix1(act, l, nx_f2)
                act_ffn(act, b1, l, f2, None)
            with act.Fori(0, LAYERS) as l:
                act_next(act, b2, l, l * 2, PAR_MIXPRE2, g2b, g2b2)
                act_mix2(act, l, (PAR_FFPRE2, fg.gb, fg.gb2))
                act_ffn(act, b2, l, fg, None)

        @block.vector
        def _(dve):
            ch = Chain(dve, b1.s.dve_steps, 0)
            dve_setup(dve, ch)
            base = ch.n
            with dve.Fori(0, LAYERS) as l:
                ch.base, n0 = l * CHAIN1, ch.n
                dve_first(dve, b1, l, l * 3, PAR_FF1PRE)
                dve_ffn(dve, b1, l, f1, ch, 0.5, PAR_FF1POST, nx_m1)
                dve_mix1(dve, l, ch, nx_f2)
                dve_ffn(dve, b1, l, f2, ch, 0.5, PAR_FF2POST, None)
                if ch.n - n0 != CHAIN1:
                    raise ValueError(f"CHAIN1 is {ch.n - n0}")
            dve.wait_ge(b1.s.weights_split, LAYERS * b1.GL + CR)
            dve.sem_inc(b2.s.weights_split, CR)
            dve.wait_ge(b1.s.x_new, 8 * 3 * LAYERS + 8)
            dve.sem_inc(b2.s.x_new, 8)
            chain1_end = base + LAYERS * CHAIN1
            ch.base, ch.n = 0, chain1_end
            with dve.Fori(0, LAYERS) as l:
                ch.base, n0 = l * CHAIN2, ch.n
                dve_first(dve, b2, l, l * 2, PAR_MIXPRE2)
                dve_mix2(dve, l, ch, (PAR_FFPRE2, fg.gb))
                dve_ffn(dve, b2, l, fg, ch, 1.0, PAR_FFPOST2, None)
                if ch.n - n0 != CHAIN2:
                    raise ValueError(f"CHAIN2 is {ch.n - n0}")
            ch.base, ch.n = 0, chain1_end + LAYERS * CHAIN2
            for a in range(4):
                for h in range(2):
                    dve.wait_ge(s_ot, 2 * a + h + 1)
                    ch(dve.tensor_copy(xin[:, a, 512 * h:512 * h + 512], ps[:, 2 * a + h, :]))
                ch.wait()
                dve.sem_inc(s_oc, 1)

        @block.tensor
        def _(pe):
            pe_setup(pe)
            with pe.Fori(0, LAYERS) as l:
                pe_ffn(pe, b1, l, f1)
                pe_mix1(pe, l)
                pe_ffn(pe, b1, l, f2)
            pe.wait_ge(b1.s.granules_done, LAYERS * b1.GL + CR)
            pe.sem_inc(b2.s.granules_done, CR)
            with pe.Fori(0, LAYERS) as l:
                pe_mix2(pe, l)
                pe_ffn(pe, b2, l, fg)
            pe.wait_ge(b2.s.x_new, 8 * 2 * LAYERS + 8)
            for a in range(4):
                for h in range(2):
                    for c in range(4):
                        t0 = META + P * a
                        ins = pe.transpose(ps[:, 2 * a + h, P * c:P * c + P], x[:, 4 * h + c, t0:t0 + P], ident[:, :])
                    ins.then_inc(s_ot, 1)


CHAIN1 = 292
CHAIN2 = 184

_INS = ["x", "ffn1_pre_g", "ffn1_w_gate", "ffn1_w_up", "ffn1_w_down", "ffn1_post_g", "mix_pre_g", "w_in", "rel_bias",
        "diff_lambda_q1", "diff_lambda_k1", "diff_lambda_q2", "diff_lambda_k2", "diff_subln_g", "w_out",
        "mix_post_g", "ffn2_pre_g", "ffn2_w_gate", "ffn2_w_up", "ffn2_w_down", "ffn2_post_g", "meta_tokens_2",
        "mix_pre_g_2", "mix_post_g_2", "w_in_2", "b_forget_2", "a_dw_w_2", "a_dw_b_2", "a_ln_g_2", "a_ln_b_2",
        "a_pw_w_2", "sc_conv_w_2", "head_g_2", "w_out_2", "ffn_pre_g_2", "ffn_post_g_2", "ffn_w_up_2",
        "ffn_conv_w_2", "ffn_w_down_2"]


def kernel(**inputs):
    import numpy as np
    import concourse.bacc as bacc
    from concourse.bass_utils import run_bass_kernel_spmd

    nc = bacc.Bacc("TRN2", target_bir_lowering=False, num_devices=1)
    arrays, tensors = {}, {}
    for name in _INS:
        a = np.ascontiguousarray(inputs[name])
        arrays[f"in_{name}_dram"] = a
        tensors[name] = nc.dram_tensor(f"in_{name}_dram", a.shape, mybir.dt.from_np(a.dtype), kind="ExternalInput").ap()
    out = nc.dram_tensor("out_0_dram", (1, SEQ, D), F32, kind="ExternalOutput").ap()
    program(nc, tensors, out)
    r = run_bass_kernel_spmd(nc, [arrays], core_ids=[0])
    return r.results[0]["out_0_dram"]
```

```python
import math
from contextlib import ExitStack

import concourse.bass as bass
from concourse import mybir

F32 = mybir.dt.float32
F32R = mybir.dt.float32r
ALU = mybir.AluOpType
ACT = mybir.ActivationFunctionType
AX = mybir.AxisListType

P = 128
D = 1024
KD = D // P
FF = 2816
KF = FF // P
SEQ = 512
META = 16
LAYERS = 2
PAIR = 2 * P
UP_ITERS = FF // PAIR
UP_GRAN = 4 * UP_ITERS
DOWN_PAIRS = D // PAIR
DOWN_Q = [4, 4, 4, 4, 4, 2]
DOWN_GRAN = DOWN_PAIRS * len(DOWN_Q)
FFN_GRAN = UP_GRAN + DOWN_GRAN
OUT_Q = [4, 4]
OUT_GRAN = DOWN_PAIRS * len(OUT_Q)
EPS = 1e-6
LN_EPS = 1e-5
NEG = -1e30

KINDS = "AAABBCCC"
QKV1 = [(128 * c, 384 + 128 * c, 768 + 128 * c) for c in range(3)]
QKV1 += [(1152 + 128 * c, 1408 + 128 * c, 1664 + 128 * c) for c in range(2)]
QKV1 += [(1920 + 128 * c, 2304 + 128 * c, 2688 + 128 * c) for c in range(3)]
IN1 = 3072
MIX1_GRAN = 24 + OUT_GRAN
UNITS1 = 64
SLOPE = [2.0 ** (-2 * (h + 1)) for h in range(4)]
B_SCALE = 32.0 ** -0.5

IN2 = 2824
F_COL = 1536
ACOL = 1544
COLS2 = [F_COL] + [ACOL + 128 * c for c in (0, 2, 1, 3)]
_SC = [ACOL + 512 + 128 * c for c in (0, 2, 4, 1, 3, 5)]
for _p in range(4):
    COLS2 += [128 * _p, 512 + 128 * _p, 1024 + 128 * _p]
    if _p > 0:
        COLS2 += [_SC[_p - 1]]
COLS2 += _SC[3:]
QKV2 = [5, 8, 12, 16]
SC_B2, SC_C2, SC_X2 = (11, 20), (15, 21), (19, 22)
MIX2_GRAN = len(COLS2) + 1 + OUT_GRAN
TAPS = 31
QB = 5
UNITS2 = 4 * QB * 2

PAR_FF1PRE, PAR_FF1POST, PAR_MIXPRE, PAR_MIXPOST, PAR_FF2PRE, PAR_FF2POST = (16 * i for i in range(6))
PAR_MIXPRE2, PAR_MIXPOST2, PAR_FFPRE2, PAR_FFPOST2, PAR_HEADG = (96 + 16 * i for i in range(5))
PAR_DWB, PAR_LNG, PAR_LNB, PAR_SUBLN, PAR_SCW = 176, 180, 184, 188, 190
PAR_DW = 202
PAR_FCW = 326
PAR_COLS = PAR_FCW + 3 * 88


class Record:
    pass


class Step:

    def __init__(self):
        self.vt = self.sc = None
        self.extra = None
        self.tiles, self.tr = [], []
        self.pairs, self.done = [], []


class Stack:

    def __init__(self, n, s, T, off, nh, TW, NT, GL, evf_layer, conv):
        self.n, self.s = n, s
        self.T, self.off = T, off
        self.nh, self.w = nh, T // nh
        self.TW, self.NT = TW, NT
        self.GL = GL
        self.evf_layer = evf_layer
        self.conv = conv


class Ffn:

    def __init__(self, first, sub, gb, gb2, ev, hb, gate, up, upoff, down):
        self.first = first
        self.sub, self.gb, self.gb2, self.ev, self.hb = sub, gb, gb2, ev, hb
        self.gate, self.up, self.upoff, self.down = gate, up, upoff, down


def schedule(pairs, units_per_pair, fill):
    n = pairs * units_per_pair
    steps = [Step() for s in range(n + LAG)]
    for s, st in enumerate(steps):
        if s < n:
            st.sc = s
            if s % units_per_pair == 1:
                st.vt = s // units_per_pair
        if s >= LAG:
            st.tr = [s - LAG]
            if (s - LAG) % units_per_pair == units_per_pair - 1:
                st.pairs = [(s - LAG) // units_per_pair]
    for p, (grans, per_step) in enumerate(fill):
        tiles = [(g, t) for g in grans for t in range(8)]
        assert sum(per_step) == len(tiles)
        for s, k in enumerate(per_step):
            st = steps[p * units_per_pair + s]
            st.tiles = tiles[:k]
            st.done = [g for g, t in tiles[:k] if t == 7]
            tiles = tiles[k:]
    return steps


def t_events(steps):
    order = []
    for st in steps:
        order += [("p", u) for u in st.tr]
        if st.vt is not None:
            order.append(("v", st.vt))
        if st.extra is not None:
            order.append(("x", st.extra))
    return {e: n for n, e in enumerate(order)}


LAG = 3
STEPS1 = schedule(8, 8, [([3 * p + 3, 3 * p + 4, 3 * p + 5], [3] * 8) for p in range(7)])
TEV1 = t_events(STEPS1)
FILL2 = [4, 4, 3, 3, 2, 4, 4, 3, 3, 2]
STEPS2 = schedule(4, 2 * QB, [(list(range(8 + 4 * p, 12 + 4 * p)), FILL2) for p in range(3)]
                  + [(list(range(20, 23)), [3, 3, 2, 3, 3, 2, 3, 3, 2, 0])])
EXTRAS = {14: 0, 22: "mean", 24: 1, 25: "variance", 33: 6, 34: 2, 41: 7}
for _s, _x in EXTRAS.items():
    STEPS2[_s].extra = _x
TEV2 = t_events(STEPS2)
SHORT_STEP = {29: (0, 0), 30: (0, 1), 31: (0, 2), 38: (1, 0), 39: (1, 1), 40: (1, 2)}
SQUARED = [0, 1, 6, 2, 7, 3, 4, 5]
SQUARE_STEP = {13: 0, 23: 1, 32: 2, 33: 3, 40: 4}
INVERSE_STEP, INVERSE_LATE = [0, 1, 6, 2], [3, 7, 4, 5]
HEADS_ORDER = [0, 1, 2, 3, 6, 7, 4, 5]
DW_OPS = [(t, c) for t in range(TAPS) for c in range(2)]
DW_PER_STEP = 3


class Chain:

    def __init__(self, eng, sem, per_layer):
        self.eng, self.sem, self.per_layer = eng, sem, per_layer
        self.base, self.n = 0, 0

    def __call__(self, ins):
        ins.then_inc(self.sem, 1)
        self.n += 1
        return ins

    def wait(self):
        self.eng.wait_ge(self.sem, self.base + self.n)


def program(nc, I, out):
    with ExitStack() as ctx:
        def sb(name, shape, dt=F32):
            return ctx.enter_context(nc.sbuf_tensor(name, shape, dt))

        def sem(name):
            return ctx.enter_context(nc.semaphore(name))

        TM = SEQ + META
        x = sb("x", [P, KD, TM])
        y = sb("y", [P, KD, TM])
        xhi, xlo = sb("xhi", [P, KD, TM], F32R), sb("xlo", [P, KD, TM], F32R)
        raw = [sb(f"raw{i}", [P, 1024]) for i in range(2)]
        whi = [sb(f"whi{i}", [P, 1024], F32R) for i in range(2)]
        wlo = [sb(f"wlo{i}", [P, 1024], F32R) for i in range(2)]
        S = [sb(f"S{i}", [P, TM + 2]) for i in range(6)]
        r = sb("r", [P, TM])
        par = sb("par", [P, PAR_COLS])
        ident = sb("ident", [P, P])
        ones = sb("ones", [P, SEQ])
        eps = sb("eps", [P, 1])
        rms = sb("rms", [P, 6])
        rinv = sb("rinv", [P, 6])
        sqrt_warm = sb("sqrt_warm", [P, 1])
        dist = sb("dist", [P, SEQ])
        strict = sb("strict", [P, P])
        later = sb("later", [P, P])
        bd = sb("bd", [P, P])
        negc = sb("negc", [P, P])
        bf = sb("bf", [8, LAYERS])
        lneps = sb("lneps", [P, 1])
        nlam = sb("nlam", [P, LAYERS])
        tbias_dram = nc.dram_tensor("tbias_scratch", (LAYERS * 6, P, SEQ), F32).ap()
        rev_dram = nc.dram_tensor("rev_scratch", (LAYERS * 6, 640), F32).ap()
        ps = ctx.enter_context(nc.psum_tensor("ps", [P, 8, 512], F32))
        xin = y[:, :, :].rearrange("p k t -> p (k t)")[:, 0:4 * D].rearrange("p (a d) -> p a d", a=4)

        sq = S[0:2]
        tt = S[2:4]
        acc = S[4]

        area = ExitStack()
        hhi = area.enter_context(nc.sbuf_tensor("hhi", [P, KF, TM], F32R))
        hlo = area.enter_context(nc.sbuf_tensor("hlo", [P, KF, TM], F32R))
        area.close()
        area = ExitStack()

        def ab(name, shape, dt=F32):
            return area.enter_context(nc.sbuf_tensor(name, shape, dt))

        m1 = Record()
        m1.ohi = ab("m1_ohi", [P, KD, SEQ], F32R)
        m1.olo = ab("m1_olo", [P, KD, SEQ], F32R)
        m1.q = [ab(f"m1_q{i}", [P, SEQ]) for i in range(2)]
        m1.k = [ab(f"m1_k{i}", [P, SEQ]) for i in range(2)]
        m1.vt = [ab(f"m1_vt{i}", [P, SEQ]) for i in range(2)]
        m1.v = [ab(f"m1_v{i}", [P, 4, P]) for i in range(2)]
        m1.w = [ab(f"m1_w{i}", [P, 2, SEQ]) for i in range(4)]
        m1.scan = ab("m1_scan", [P, SEQ + 1])
        m1.pt = [ab(f"m1_pt{i}", [P, 4, P]) for i in range(2)]
        m1.ob = ab("m1_ob", [P, 2, SEQ])
        m1.sqb = ab("m1_sqb", [P, 2, SEQ])
        m1.rb = ab("m1_rb", [P, 2, SEQ])
        m1.nmax = [ab(f"m1_nmax{i}", [P, 2]) for i in range(4)]
        m1.sums = [ab(f"m1_sums{i}", [P, 2]) for i in range(4)]
        m1.inv = [ab(f"m1_inv{i}", [P, 2]) for i in range(4)]
        m1.c1 = [ab(f"m1_c1{i}", [P, 1]) for i in range(4)]
        tb = y[:, :, :].rearrange("p k t -> p (k t)")[:, 0:6 * SEQ].rearrange("p (h c) -> p h c", h=6)
        area.close()
        area = ExitStack()
        fb = ab("m2_fb", [P, 8, TM])
        apad = ab("m2_apad", [P, 2, TAPS - 1 + TM])
        aconv = ab("m2_aconv", [P, 2, TM])
        scx, scc, scb = ab("m2_scx", [P, 2 + TM]), ab("m2_scc", [P, TM]), ab("m2_scb", [P, TM])
        area.close()
        area = ExitStack()
        m2 = Record()
        m2.ohi = ab("m2_ohi", [P, KD, TM], F32R)
        m2.olo = ab("m2_olo", [P, KD, TM], F32R)
        m2.q = [ab(f"m2_q{i}", [P, TM]) for i in range(2)]
        m2.k = [ab(f"m2_k{i}", [P, TM]) for i in range(2)]
        m2.vt = [ab(f"m2_vt{i}", [P, TM]) for i in range(2)]
        m2.v = [ab(f"m2_v{i}", [P, QB, P]) for i in range(2)]
        m2.w = [ab(f"m2_w{i}", [P, TM]) for i in range(4)]
        m2.pt = [ab(f"m2_pt{i}", [P, QB, P]) for i in range(2)]
        m2.ahi = ab("m2_ahi", [P, 2, TM], F32R)
        m2.alo = ab("m2_alo", [P, 2, TM], F32R)
        m2.lsq = ab("m2_lsq", [P, 2, TM])
        m2.lrs = ab("m2_lrs", [P, TM])
        m2.u = ab("m2_u", [8, TM])
        m2.lf = ab("m2_lf", [8, TM])
        m2.nf = ab("m2_nf", [8, TM])
        m2.e = ab("m2_e", [8, TM])
        m2.nmax = [ab(f"m2_nmax{i}", [P, 1]) for i in range(4)]
        m2.sums = [ab(f"m2_sums{i}", [P, 1]) for i in range(4)]
        m2.inv = [ab(f"m2_inv{i}", [P, 1]) for i in range(4)]
        area.close()
        area = ExitStack()
        prow = [ab(f"prow{i}", [P, P]) for i in range(6)]
        metain = ab("metain", [META, D])
        relin = ab("relin", [12, 257])
        rev = ab("rev", [12, 640])
        lam_in = ab("lam_in", [P, 4, LAYERS, 32])
        lam_pr = ab("lam_pr", [P, 2, LAYERS, 32])
        lam_s = ab("lam_s", [P, 2, LAYERS])
        lam_e = ab("lam_e", [P, 2, LAYERS])
        area.close()

        def semaphores(b):
            s = Record()
            s.weights_landed = [sem(f"{b}_weights_landed{i}") for i in range(2)]
            s.weights_hi = sem(f"{b}_weights_hi")
            s.weights_split = sem(f"{b}_weights_split")
            s.granules_done = sem(f"{b}_granules_done")
            s.hidden_free = sem(f"{b}_hidden_free")
            s.out_free = sem(f"{b}_out_free")
            s.norm_sums = sem(f"{b}_norm_sums")
            s.norm_rms = sem(f"{b}_norm_rms")
            s.norm_inv = sem(f"{b}_norm_inv")
            s.norm_spread = sem(f"{b}_norm_spread")
            s.norm_r = sem(f"{b}_norm_r")
            s.x_new = sem(f"{b}_x_new")
            s.x_hi = sem(f"{b}_x_hi")
            s.x_lo = sem(f"{b}_x_lo")
            s.x_squared = sem(f"{b}_x_squared")
            s.x_summed = sem(f"{b}_x_summed")
            s.y_squared = sem(f"{b}_y_squared")
            s.y_summed = sem(f"{b}_y_summed")
            s.gate_in = sem(f"{b}_gate_in")
            s.silu_done = sem(f"{b}_silu_done")
            s.hidden_done = sem(f"{b}_hidden_done")
            s.hidden_hi = sem(f"{b}_hidden_hi")
            s.hidden_lo = sem(f"{b}_hidden_lo")
            s.columns_out = sem(f"{b}_columns_out")
            s.scores_done = sem(f"{b}_scores_done")
            s.scores_free = sem(f"{b}_scores_free")
            s.max_done = sem(f"{b}_max_done")
            s.exp_done = sem(f"{b}_exp_done")
            s.probs_done = sem(f"{b}_probs_done")
            s.transposed = sem(f"{b}_transposed")
            s.transposed_out = sem(f"{b}_transposed_out")
            s.pv_done = sem(f"{b}_pv_done")
            s.o_hi_out = sem(f"{b}_o_hi_out")
            return s

        def first_semaphores(b, s):
            s.o_lo_out = sem(f"{b}_o_lo_out")
            s.b_act_steps = sem(f"{b}_b_act_steps")
            s.b_sums = sem(f"{b}_b_sums")
            s.b_scaled = sem(f"{b}_b_scaled")
            s.b_hi = sem(f"{b}_b_hi")
            s.b_lo = sem(f"{b}_b_lo")
            s.dve_steps = sem(f"{b}_dve_steps")
            return s

        def second_semaphores(b, s):
            s.up_in = sem(f"{b}_up_in")
            s.last_tap = sem(f"{b}_last_tap")
            s.forget_in = sem(f"{b}_forget_in")
            s.forget_steps = sem(f"{b}_forget_steps")
            s.forget_sums = sem(f"{b}_forget_sums")
            s.forget_spread = sem(f"{b}_forget_spread")
            s.forget_out = sem(f"{b}_forget_out")
            s.inv_done = sem(f"{b}_inv_done")
            s.a_gate_in = sem(f"{b}_a_gate_in")
            s.a_gate_done = sem(f"{b}_a_gate_done")
            s.dw_taps = sem(f"{b}_dw_taps")
            s.ln_centered = sem(f"{b}_ln_centered")
            s.ln_squared = sem(f"{b}_ln_squared")
            s.ln_steps = sem(f"{b}_ln_steps")
            s.ln_scaled = sem(f"{b}_ln_scaled")
            s.ln_silu = sem(f"{b}_ln_silu")
            s.a_lo = sem(f"{b}_a_lo")
            s.pw_out = sem(f"{b}_pw_out")
            s.short_done = sem(f"{b}_short_done")
            s.head_squared = sem(f"{b}_head_squared")
            s.head_sums = sem(f"{b}_head_sums")
            s.head_steps = sem(f"{b}_head_steps")
            s.head_scaled = sem(f"{b}_head_scaled")
            s.head_hi = sem(f"{b}_head_hi")
            s.head_lo = sem(f"{b}_head_lo")
            return s

        s_ld = [sem(f"s_ld{i}") for i in range(6)]
        s_ones = sem("s_ones")
        s_const = sem("s_const")
        s_xt, s_xc, s_pt, s_pc = sem("s_xt"), sem("s_xc"), sem("s_ptr"), sem("s_pcopy")
        s_rev, s_revd, s_tbias, s_tb, s_mask = sem("s_rev"), sem("s_revd"), sem("s_tbias"), sem("s_tb"), sem("s_mask")
        s_lam = sem("s_lam")
        s_set, s_dist = sem("s_set"), sem("s_dist")
        s_ot, s_oh, s_oc, s_out = sem("s_ot"), sem("s_oh"), sem("s_oc"), sem("s_out")
        CR = 2

        b1 = Stack(
            n=1, s=first_semaphores("b1",
                                    semaphores("b1")), T=SEQ, off=META, nh=1, TW=P, NT=4, GL=2 * FFN_GRAN + MIX1_GRAN,
            evf_layer=4 * UP_ITERS, conv=False)
        b2 = Stack(
            n=2, s=second_semaphores("b2", semaphores("b2")), T=TM, off=0, nh=2, TW=88, NT=6, GL=FFN_GRAN + MIX2_GRAN,
            evf_layer=2 * UP_ITERS, conv=True)

        def halves(b):
            return [(h * b.w, b.w) for h in range(b.nh)]

        def pview(b, bank):
            return ps[:, bank:bank + b.nh, 0:b.w]

        def tview(b, ap):
            return ap.rearrange("p (h w) -> p h w", h=b.nh)

        def xs(b, t, c):
            return t[:, c, b.off:b.off + b.T] if b.n == 1 else t[:, c, 0:b.T]

        def gain(col, l, c):
            return par[:, bass.ds(l * KD + (col + c), 1)]

        def load_raw(sp, b, g, slot, src, shape):
            sp.wait_ge(b.s.weights_split, g + 1)
            k, c = shape
            dst = raw[slot][:, 0:k * c].rearrange("p (k c) -> p k c", k=k)
            sp.dma_start(dst, src.rearrange("(k p) c -> p k c", p=P)).then_inc(b.s.weights_landed[slot], 16)

        def split_hi(act, b, g, g2, slot, n=1024):
            act.wait_ge(b.s.weights_landed[slot], 16 * g2 + 16)
            act.wait_ge(b.s.granules_done, g + 1)
            act.activation(whi[slot][:, 0:n], raw[slot][:, 0:n], ACT.Copy).then_inc(b.s.weights_hi, 1)

        def split_lo(eng, b, g, slot, n=1024, handover=False):
            if handover:
                eng.wait_ge(b.s.weights_split, g + CR)
            eng.wait_ge(b.s.weights_hi, g + 1)
            eng.tensor_tensor(wlo[slot][:, 0:n], raw[slot][:, 0:n], whi[slot][:, 0:n].bitcast(F32),
                              ALU.subtract).then_inc(b.s.weights_split, 1)

        def tile_mm(pe, b, bank, slot, wcol, hi, lo, first, last, lo_ready=None):
            wh, wl = whi[slot][:, wcol:wcol + P], wlo[slot][:, wcol:wcol + P]
            if lo_ready is not None:
                for n, (t0, w) in enumerate(halves(b)):
                    pe.matmul(ps[:, bank + n, 0:w], wh, hi[:, t0:t0 + w], start=first, stop=False)
                    pe.matmul(ps[:, bank + n, 0:w], wl, hi[:, t0:t0 + w], start=False, stop=False)
                lo_ready()
                for n, (t0, w) in enumerate(halves(b)):
                    ins = pe.matmul(ps[:, bank + n, 0:w], wh, lo[:, t0:t0 + w], start=False, stop=last)
                return ins
            for n, (t0, w) in enumerate(halves(b)):
                o = ps[:, bank + n, 0:w]
                pe.matmul(o, wh, hi[:, t0:t0 + w], start=first, stop=False)
                pe.matmul(o, wh, lo[:, t0:t0 + w], start=False, stop=False)
                ins = pe.matmul(o, wl, hi[:, t0:t0 + w], start=False, stop=last)
            return ins

        def pe_hi_first(pe, b, gb, sub, tiles):
            for n, (g, bank, wcol, k, start, stop) in enumerate(tiles):
                if all(t[0] != g for t in tiles[:n]):
                    pe.wait_ge(b.s.weights_split, gb + g + 1 + CR)
                if all(t[3] != k for t in tiles[:n]):
                    pe.wait_ge(b.s.x_hi, 8 * sub + k + 1)
                for h, (t0, w) in enumerate(halves(b)):
                    for wt in (whi, wlo):
                        pe.matmul(ps[:, bank + h, 0:w], wt[g][:, wcol:wcol + P], xhi[:, k, t0:t0 + w],
                                  start=(start and wt is whi), stop=False)
            for g in range(2):
                for _, bank, wcol, k, start, stop in [t for t in tiles if t[0] == g]:
                    pe.wait_ge(b.s.x_lo, 8 * sub + k + 1)
                    for h, (t0, w) in enumerate(halves(b)):
                        ins = pe.matmul(ps[:, bank + h, 0:w], whi[g][:, wcol:wcol + P], xlo[:, k, t0:t0 + w],
                                        start=False, stop=stop)
                ins.then_inc(b.s.granules_done, 1)

        def pe_square_sum(pe, b, bank, src, first, last):
            for t in range(b.NT):
                ins = pe.matmul(ps[0:b.TW, bank, t:t + 1], src[:, t * b.TW:(t + 1) * b.TW], ones[:, 0:1],
                                start=(first and t == 0), stop=(last and t == b.NT - 1))
            if last:
                ins.then_inc(b.s.norm_sums, 1)

        def pe_spread(pe, b, n, bank):
            pe.wait_ge(b.s.norm_inv, n + 1)
            for t in range(b.NT):
                h, c0 = divmod(t * b.TW, b.w)
                ins = pe.matmul(ps[:, bank + h, c0:c0 + b.TW], rinv[0:b.TW, t:t + 1].to_broadcast([b.TW, P]),
                                ident[0:b.TW, 0:b.TW], start=True, stop=True)
            ins.then_inc(b.s.norm_spread, 1)

        def act_sqrt_table(act):
            act.activation(sqrt_warm[:, :], eps[:, :], ACT.Sqrt)

        def act_rms(act, b, n, bank):
            act.wait_ge(b.s.norm_sums, n + 1)
            act.activation(rms[0:b.TW, 0:b.NT], ps[0:b.TW, bank, 0:b.NT], ACT.Sqrt, bias=eps[0:b.TW, :],
                           scale=1.0 / D).then_inc(b.s.norm_rms, 1)

        def dve_inv(dve, b, n):
            dve.wait_ge(b.s.norm_rms, n + 1)
            dve.reciprocal(rinv[0:b.TW, 0:b.NT], rms[0:b.TW, 0:b.NT]).then_inc(b.s.norm_inv, 1)

        def act_r(act, b, sub):
            act.wait_ge(b.s.norm_spread, 2 * sub + 1)
            act.activation(tview(b, r[:, 0:b.T]), pview(b, BC_PRE), ACT.Copy).then_inc(b.s.norm_r, 1)

        SUM_PRE, BC_PRE, SUM_POST, BC_POST = 6, 6, 0, 6

        def act_operand(act, b, l, sub, col, c):
            act.wait_ge(b.s.x_new, 8 * sub + c + 1)
            act.activation(xhi[:, c, 0:b.T], xs(b, x, c), ACT.Copy, scale=gain(col, l, c)).then_inc(b.s.x_hi, 1)
            if c == 0:
                act.activation(acc[:, 0:b.T], xs(b, x, c), ACT.Square).then_inc(b.s.x_squared, 1)
            else:
                if c > 2:
                    act.wait_ge(b.s.x_summed, 7 * sub + c - 2)
                act.activation(sq[c % 2][:, 0:b.T], xs(b, x, c), ACT.Square).then_inc(b.s.x_squared, 1)

        def dve_operand_lo(dve, b, l, sub, col, c):
            dve.wait_ge(b.s.x_hi, 8 * sub + c + 1)
            dve.scalar_tensor_tensor(out=xlo[:, c, 0:b.T], in0=xs(b, x, c), scalar=gain(col, l, c),
                                     in1=xhi[:, c, 0:b.T].bitcast(F32), op0=ALU.mult,
                                     op1=ALU.subtract).then_inc(b.s.x_lo, 1)

        def pool_x(pool, b, sub):
            for c in range(1, KD):
                pool.wait_ge(b.s.x_squared, 8 * sub + c + 1)
                if c > 1:
                    pool.wait_ge(b.s.x_summed, 7 * sub + c - 1)
                pool.tensor_tensor(acc[:, 0:b.T], acc[:, 0:b.T], sq[c % 2][:, 0:b.T],
                                   ALU.add).then_inc(b.s.x_summed, 1)

        def pool_y(pool, b, sub):
            for c in range(1, KD - 2):
                pool.wait_ge(b.s.y_squared, 8 * sub + c + 1)
                if c > 1:
                    pool.wait_ge(b.s.y_summed, 5 * sub + c - 1)
                pool.tensor_tensor(acc[:, 0:b.T], acc[:, 0:b.T], sq[c % 2][:, 0:b.T],
                                   ALU.add).then_inc(b.s.y_summed, 1)

        def act_yevac(act, b, sub, m):
            for o in range(2):
                c = 2 * m + o
                if c > 2:
                    act.wait_ge(b.s.y_summed, 5 * sub + min(c - 2, 5))
                dst = acc if c == 0 else sq[c % 2]
                act.activation(tview(b, dst[:, 0:b.T]), pview(b, 4 * (m % 2) + 2 * o),
                               ACT.Square).then_inc(b.s.y_squared, 1)
            for o in range(2):
                ins = act.activation(tview(b, y[:, 2 * m + o, 0:b.T]), pview(b, 4 * (m % 2) + 2 * o), ACT.Copy)
            ins.then_inc(b.s.out_free, 1)

        def dve_residual(dve, b, l, sub, ch, factor, post, pre):
            dve.wait_ge(b.s.norm_spread, 2 * sub + 2)
            def scaled(c):
                ch(dve.scalar_tensor_tensor(out=tview(b, tt[c % 2][:, 0:b.T]), in0=tview(b, y[:, c, 0:b.T]),
                                            scalar=factor, in1=pview(b, BC_POST), op0=ALU.mult, op1=ALU.mult))

            scaled(0)
            for c in range(KD):
                ch.wait()
                dve.scalar_tensor_tensor(out=xs(b, x, c), in0=tt[c % 2][:, 0:b.T], scalar=gain(post, l, c),
                                         in1=xs(b, x, c), op0=ALU.mult, op1=ALU.add).then_inc(b.s.x_new, 1)
                if c + 1 < KD:
                    scaled(c + 1)
                if pre is not None and c > 0:
                    dve_operand_lo(dve, b, l, sub + 1, pre, c - 1)
            if pre is not None:
                dve_operand_lo(dve, b, l, sub + 1, pre, KD - 1)

        def sp_ffn(sp, b, l, f):
            with sp.Fori(0, UP_ITERS) as i:
                for q in range(4):
                    W = f.gate if q < 2 else f.up
                    src = W[bass.ds(l * D + (q % 2) * 512, 512), bass.ds(i * PAIR + f.upoff * (q // 2), PAIR)]
                    load_raw(sp, b, f.gb(l) + 4 * i + q, q % 2, src, (4, PAIR))
            for m in range(DOWN_PAIRS):
                for q, k in enumerate(DOWN_Q):
                    src = f.down[bass.ds(l * FF + q * 512, k * P), m * PAIR:(m + 1) * PAIR]
                    load_raw(sp, b, f.gb(l) + UP_GRAN + 6 * m + q, q % 2, src, (k, PAIR))

        def pe_up_granule(pe, b, l, f, i, q, between=None):
            g = f.gb(l) + 4 * i + q
            pe.wait_ge(b.s.weights_split, g + 1 + CR)
            first = q % 2 == 0
            if first:
                pe.wait_ge(b.s.hidden_free, f.ev(l) + 2 * i + q // 2 + 1)
            for o in range(2):
                for kk in range(4):
                    k = 4 * (q % 2) + kk
                    lo_ready = None
                    if isinstance(i, int) and i == 0 and q < 2 and o == 0:
                        pe.wait_ge(b.s.x_hi, 8 * f.sub(l) + k + 1)
                        lo_ready = lambda: pe.wait_ge(b.s.x_lo, 8 * f.sub(l) + k + 1)
                    ins = tile_mm(pe, b, 4 * (q // 2) + 2 * o, q % 2, kk * PAIR + o * P,
                                  xhi[:, k, :], xlo[:, k, :], first and kk == 0, not first and kk == 3, lo_ready)
                if o == 0 and between is not None:
                    between()
            ins.then_inc(b.s.granules_done, 1)

        def pe_out(pe, b, l, sub, gb, qs, hi, lo, ready, second=None, order=None):
            nq = len(qs)

            def pair_of(base, m, mi):
                pe.wait_ge(b.s.out_free, 4 * sub + base + m + 1)
                for q, kn in enumerate(qs):
                    pe.wait_ge(b.s.weights_split, gb + nq * (base + m) + q + 1 + CR)
                    ks = list(range(kn)) if order is None else order[q]
                    for kk in ks:
                        k = 4 * q + kk
                        if ready is not None and mi == 0 and m == 0:
                            ready(k)
                        for o in range(2):
                            ins = tile_mm(pe, b, 4 * m + 2 * o, q % 2, kk * PAIR + o * P, hi[:, k, :], lo[:, k, :],
                                          q == 0 and kk == ks[0], q == nq - 1 and kk == ks[-1])
                    ins.then_inc(b.s.granules_done, 1)

            for mi in range(2):
                for m in range(2):
                    if second is not None and mi == 0 and m == 1:
                        second()
                    pair_of(2 * mi, m, mi)

        def pe_post(pe, b, sub):
            pe.wait_ge(b.s.out_free, 4 * sub + 3 + CR)
            pe.wait_ge(b.s.y_summed, 5 * sub + 5)
            pe_square_sum(pe, b, SUM_POST, acc, True, False)
            pe.wait_ge(b.s.y_squared, 8 * sub + 7)
            pe_square_sum(pe, b, SUM_POST, sq[0], False, False)
            pe.wait_ge(b.s.y_squared, 8 * sub + 8)
            pe_square_sum(pe, b, SUM_POST, sq[1], False, True)
            pe.wait_ge(b.s.out_free, 4 * sub + 4 + CR)
            pe_spread(pe, b, 2 * sub + 1, BC_POST)

        def pe_pre_sum(pe, b, sub):
            pe.wait_ge(b.s.x_summed, 7 * sub + 7)
            pe_square_sum(pe, b, SUM_PRE, acc, True, True)

        def pe_ffn(pe, b, l, f):
            sub = f.sub(l)
            pe.wait_ge(b.s.out_free, 4 * sub + CR)
            if f.first:
                pe_hi_first(pe, b, f.gb(l), sub,
                            [(q, 2 * o, kk * PAIR + o * P, 4 * q + kk, q + kk == 0, q == 1 and kk == 3)
                                                  for q in range(2) for kk in range(4) for o in range(2)])
                pe_pre_sum(pe, b, sub)
            else:
                pe_up_granule(pe, b, l, f, 0, 0)
                pe_up_granule(pe, b, l, f, 0, 1, lambda: pe_pre_sum(pe, b, sub))
            pe_spread(pe, b, 2 * sub, BC_PRE)
            pe.wait_ge(b.s.norm_r, sub + 1)
            pe_up_granule(pe, b, l, f, 0, 2)
            pe_up_granule(pe, b, l, f, 0, 3)
            with pe.Fori(1, UP_ITERS) as i:
                for q in range(4):
                    pe_up_granule(pe, b, l, f, i, q)
            pe.wait_ge(b.s.hidden_free, f.ev(l) + 2 * UP_ITERS - 1 + CR)
            pe_out(pe, b, l, sub, f.gb(l) + UP_GRAN, DOWN_Q, hhi, hlo,
                   lambda k: pe.wait_ge(b.s.hidden_lo, f.hb(l) + k + 1),
                   lambda: pe.wait_ge(b.s.hidden_free, f.ev(l) + 2 * UP_ITERS + CR))
            pe_post(pe, b, sub)

        def act_ffn(act, b, l, f, nxt):
            sub, gb = f.sub(l), f.gb(l)

            def hi_split(i, q):
                split_hi(act, b, gb + 4 * i + q, f.gb2(l) + 2 * i + q // 2, q % 2)

            def first_tap(i, up):
                for o in range(2):
                    act.wait_ge(b.s.up_in, 2 * f.hb(l) + 4 * i + 2 * up + o + 1)
                    act.activation(S[2 + 2 * up + o][:, 0:b.T], S[o][:, 2:2 + b.T], ACT.Copy,
                                   scale=tap(l, 2, 2 * i + o, up)).then_inc(b.s.last_tap, 1)

            def silu(i):
                if b.conv:
                    first_tap(i, 0)
                for o in range(2):
                    act.wait_ge(b.s.gate_in, f.hb(l) + 2 * i + o + 1)
                    act.activation(S[2 + o][:, 0:b.T], S[2 + o][:, 0:b.T], ACT.Silu).then_inc(b.s.silu_done, 1)

            def hidden(i):
                if b.conv:
                    first_tap(i, 1)
                hi_split(i + 1, 2)
                for o in range(2):
                    act.wait_ge(b.s.hidden_done, f.hb(l) + 2 * i + o + 1)
                    act.activation(hhi[:, bass.ds(2 * i + o, 1), 0:b.T].rearrange("p a t -> p (a t)"),
                                   S[4 + o][:, 0:b.T], ACT.Copy).then_inc(b.s.hidden_hi, 1)

            hi_split(0, 2)
            act_rms(act, b, 2 * sub, SUM_PRE)
            act_r(act, b, sub)
            hi_split(0, 3)
            silu(0)
            hi_split(1, 0)
            hi_split(1, 1)
            hidden(0)
            with act.Fori(1, UP_ITERS) as i:
                hi_split(i, 3)
                silu(i)
                hi_split(i + 1, 0)
                hi_split(i + 1, 1)
                hidden(i)
            act_out(act, b, l, sub, gb + UP_GRAN, f.gb2(l) + UP_GRAN // 2, DOWN_Q, 3)
            act_rms(act, b, 2 * sub + 1, SUM_POST)
            if nxt is not None:
                act_next(act, b, l, sub + 1, *nxt)

        def act_out(act, b, l, sub, gb, gb2, qs, first=2):
            nq = len(qs)
            n = DOWN_PAIRS * nq
            for j in range(n):
                if j == nq:
                    act_sqrt_table(act)
                if first <= j + 2 < n:
                    split_hi(act, b, gb + j + 2, gb2 + j // 2 + 1, j % 2, qs[(j + 2) % nq] * PAIR)
                if j % nq == nq - 1:
                    act.wait_ge(b.s.granules_done, gb + j + 1 + CR)
                    act_yevac(act, b, sub, j // nq)

        def act_next(act, b, l, sub, col, gb, gb2):
            for j in range(2):
                split_hi(act, b, gb(l) + j, gb2(l), j)
            for c in range(KD):
                act_operand(act, b, l, sub, col, c)

        def dve_ffn(dve, b, l, f, ch, factor, post, nxt):
            sub, gb = f.sub(l), f.gb(l)

            def lo_split(i, q):
                split_lo(dve, b, gb + 4 * i + q, q % 2)

            def conv(i, up):
                for o in range(2):
                    dve.tensor_tensor(tview(b, S[o][:, 2:2 + b.T]), pview(b, 4 * up + 2 * o), tview(b, r[:, 0:b.T]),
                                      ALU.mult).then_inc(b.s.up_in, 1)
                dve.wait_ge(b.s.up_in, 2 * f.hb(l) + 4 * i + 2 * up + 2)
                dve.sem_inc(b.s.hidden_free, 1)
                for k in (1, 0):
                    for o in range(2):
                        c_ = S[2 + 2 * up + o][:, 0:b.T]
                        if k:
                            dve.wait_ge(b.s.last_tap, 2 * f.hb(l) + 4 * i + 2 * up + o + 1)
                        ins = dve.scalar_tensor_tensor(out=c_, in0=S[o][:, k:k + b.T],
                                                       scalar=tap(l, k, 2 * i + o, up),
                                                       in1=c_, op0=ALU.mult, op1=ALU.add)
                        if k == 0 and not up:
                            ins.then_inc(b.s.gate_in, 1)
                        else:
                            ch(ins)
                    if k or up:
                        ch.wait()

            def gate(i):
                dve.wait_ge(b.s.granules_done, gb + 4 * i + 2 + CR)
                if b.conv:
                    return conv(i, 0)
                for o in range(2):
                    ins = dve.tensor_tensor(tview(b, S[2 + o][:, 0:b.T]), pview(b, 2 * o), tview(b, r[:, 0:b.T]),
                                            ALU.mult).then_inc(b.s.gate_in, 1)
                dve.wait_ge(b.s.gate_in, f.hb(l) + 2 * i + 2)
                dve.sem_inc(b.s.hidden_free, 1)

            def up(i):
                dve.wait_ge(b.s.granules_done, gb + 4 * i + 4 + CR)
                if b.conv:
                    conv(i, 1)
                else:
                    for o in range(2):
                        ch(dve.tensor_tensor(tview(b, S[4 + o][:, 0:b.T]), pview(b, 4 + 2 * o),
                                             tview(b, r[:, 0:b.T]), ALU.mult))
                    ch.wait()
                    dve.sem_inc(b.s.hidden_free, 1)
                lo_split(i + 1, 2)
                for o in range(2):
                    dve.wait_ge(b.s.silu_done, f.hb(l) + 2 * i + o + 1)
                    dve.tensor_tensor(S[4 + o][:, 0:b.T], S[4 + o][:, 0:b.T], S[2 + o][:, 0:b.T],
                                      ALU.mult).then_inc(b.s.hidden_done, 1)
                for o in range(2):
                    dve.wait_ge(b.s.hidden_hi, f.hb(l) + 2 * i + o + 1)
                    h = bass.ds(2 * i + o, 1)
                    dve.tensor_tensor(hlo[:, h, 0:b.T].rearrange("p a t -> p (a t)"), S[4 + o][:, 0:b.T],
                                      hhi[:, h, 0:b.T].rearrange("p a t -> p (a t)").bitcast(F32),
                                      ALU.subtract).then_inc(b.s.hidden_lo, 1)

            split_lo(dve, b, gb + 2, 0, handover=True)
            dve_inv(dve, b, 2 * sub)
            lo_split(0, 3)
            dve.wait_ge(b.s.norm_r, sub + 1)
            if b.conv:
                for o in range(2):
                    ch(dve.memset(S[o][:, 0:2], 0.0))
            gate(0)
            lo_split(1, 0)
            lo_split(1, 1)
            up(0)
            per = 6 if b.conv else 2
            with dve.Fori(1, UP_ITERS) as i:
                base, n0 = ch.base, ch.n
                ch.base = base + (i - 1) * per
                lo_split(i, 3)
                gate(i)
                lo_split(i + 1, 0)
                lo_split(i + 1, 1)
                up(i)
                assert ch.n == n0 + per, ch.n - n0
            ch.base, ch.n = base, n0 + per * (UP_ITERS - 1)
            dve_out(dve, b, l, sub, gb + UP_GRAN, DOWN_Q, ch, factor, post, nxt, 3)

        def dve_out(dve, b, l, sub, gb, qs, ch, factor, post, nxt, first=2):
            nq = len(qs)
            for j in range(first - 2, DOWN_PAIRS * nq - 2):
                split_lo(dve, b, gb + j + 2, j % 2, qs[(j + 2) % nq] * PAIR, handover=(qs is OUT_Q and j == 0))
            dve_inv(dve, b, 2 * sub + 1)
            dve_residual(dve, b, l, sub, ch, factor, post, nxt)

        def pool_first(pool, b, l, gb):
            for j in range(2):
                split_lo(pool, b, gb(l) + j, j, handover=True)

        def dve_first(dve, b, l, sub, col):
            for c in range(KD):
                dve_operand_lo(dve, b, l, sub, col, c)

        def tap(l, k, chunk, up):
            return par[:, bass.ds(l * 132 + chunk + (PAR_FCW + 44 * k + 22 * up), 1)]

        def ffn1(which):
            g0 = 0 if which == 0 else FFN_GRAN + MIX1_GRAN
            return Ffn(
                first=(which == 0), sub=lambda l: l * 3 + 2 * which, gb=lambda l: l * b1.GL + g0,
                gb2=lambda l: l * (b1.GL // 2) + g0 // 2,
                ev=lambda l: l * b1.evf_layer + 2 * UP_ITERS * which, hb=lambda l: l * 2 * KF + KF * which,
                gate=I[f"ffn{which + 1}_w_gate"].rearrange("l d f -> (l d) f"),
                up=I[f"ffn{which + 1}_w_up"].rearrange("l d f -> (l d) f"), upoff=0,
                down=I[f"ffn{which + 1}_w_down"].rearrange("l f d -> (l f) d"))

        f1, f2 = ffn1(0), ffn1(1)
        mgb = lambda l: l * b1.GL + FFN_GRAN
        mgb2 = lambda l: l * (b1.GL // 2) + FFN_GRAN // 2
        win1 = I["w_in"].rearrange("l d f -> (l d) f")
        wout1 = I["w_out"].rearrange("l d f -> (l d) f")

        def sp_mix1(sp, l):
            b = b1
            for p in range(8):
                for j in range(3):
                    g = 3 * p + j
                    src = win1[bass.ds(l * D, D), QKV1[p][j]:QKV1[p][j] + P]
                    load_raw(sp, b, mgb(l) + g, g % 2, src, (8, P))
                if p == 0:
                    sp.wait_ge(b.s.x_new, 8 * (l * 3 + 1) + 8)
                    sp.wait_ge(s_tbias, 16)
                    sp.dma_start(tb,
                                 tbias_dram[bass.ds(l * 6, 6), :, :].rearrange("h p c -> p h c")).then_inc(s_tb, 16)
            sp_wout(sp, b, l, mgb(l) + 24, wout1)

        def sp_wout(sp, b, l, gb, W):
            for m in range(DOWN_PAIRS):
                for q in range(2):
                    src = W[bass.ds(l * D + q * 512, 512), m * PAIR:(m + 1) * PAIR]
                    load_raw(sp, b, gb + 2 * m + q, q, src, (4, PAIR))

        def first_two(gtile):
            for t in range(8 + 3):
                if t < 8:
                    gtile(0, t)
                if t >= 3:
                    gtile(1, t - 3)

        def gbank1(g):
            return 2 if g == 2 else g % 2

        def sbank(u):
            return 4 + 2 * (u % 2)

        def unit1(u):
            p, h, j = u // 8, (u // 4) % 2, u % 4
            return p, h, j, KINDS[p], P * (j + 1)

        def pe_mix1(pe, l):
            b, s = b1, b1.s
            sub = l * 3 + 1
            U = l * UNITS1

            def gtile(g, t):
                if t == 0:
                    pe.wait_ge(s.weights_split, mgb(l) + g + 1 + CR)
                    if g != 2:
                        pe.wait_ge(s.columns_out, l * 24 + g + 1)
                lo_ready = None
                if g == 0:
                    pe.wait_ge(s.x_hi, 8 * sub + t + 1)
                    lo_ready = lambda: pe.wait_ge(s.x_lo, 8 * sub + t + 1)
                ins = tile_mm(pe, b, gbank1(g), g % 2, t * P, xhi[:, t, :], xlo[:, t, :], t == 0, t == 7, lo_ready)
                if t == 7:
                    ins.then_inc(s.granules_done, 1)

            def scores(u):
                p, h, j, kind, n = unit1(u)
                pe.wait_ge(s.columns_out, l * 24 + 3 * p + 2 + CR)
                pe.wait_ge(s.scores_free, U + u + 1)
                maps = 2 if kind == "B" else 1
                rows = 64 // maps
                for m in range(maps):
                    a = 64 * h + rows * m
                    ins = pe.matmul(ps[:, sbank(u) + m, 0:n], m1.q[p % 2][a:a + rows, P * j:P * j + P],
                                    m1.k[p % 2][a:a + rows, 0:n], start=True, stop=True)
                ins.then_inc(s.scores_done, 1)

            def vtrans(p):
                e = TEV1["v", p]
                pe.wait_ge(s.columns_out, l * 24 + 3 * p + 3 + CR)
                pe.wait_ge(s.transposed_out, l * len(TEV1) + e + 1)
                for t in range(4):
                    ins = pe.transpose(ps[:, 2, P * t:P * t + P], m1.vt[p % 2][:, P * t:P * t + P], ident[:, :])
                ins.then_inc(s.transposed, 1)

            def ptrans(u):
                p, h, j, kind, n = unit1(u)
                pe.wait_ge(s.probs_done, U + u + 1)
                pe.wait_ge(s.transposed_out, l * len(TEV1) + TEV1["p", u] + 1)
                for t in range(j + 1):
                    ins = pe.transpose(ps[:, 2, P * t:P * t + P], m1.w[u % 4][:, 0, P * t:P * t + P], ident[:, :])
                ins.then_inc(s.transposed, 1)

            def pv(u):
                p, h, j, kind, n = unit1(u)
                pe.wait_ge(s.transposed_out, l * len(TEV1) + TEV1["p", u] + 2)
                if u % 8 == 0:
                    pe.wait_ge(s.o_hi_out, l * 8 + p + 1)
                    pe.wait_ge(s.o_lo_out, l * 8 + p + 1)
                for t in range(j + 1):
                    ins = pe.matmul(ps[64 * h:64 * h + 64, 3, P * j:P * j + P], m1.v[p % 2][:, t, 64 * h:64 * h + 64],
                                    m1.pt[u % 2][:, t, :], start=(t == 0), stop=(t == j))
                ins.then_inc(s.pv_done, 1)

            pe.wait_ge(s.out_free, 4 * sub + CR)
            first_two(gtile)
            pe_pre_sum(pe, b, sub)
            for t in range(8):
                gtile(2, t)
                if t == 2:
                    pe_spread(pe, b, 2 * sub, BC_PRE)
            pe.wait_ge(s.norm_r, sub + 1)
            for n_step, st in enumerate(STEPS1):
                for u in st.tr:
                    ptrans(u)
                if st.sc is not None:
                    scores(st.sc)
                for tile in st.tiles[:2]:
                    gtile(*tile)
                if st.vt is not None:
                    vtrans(st.vt)
                for tile in st.tiles[2:]:
                    gtile(*tile)
                for u in st.tr:
                    pv(u)
                if n_step == B_NORM:
                    pe.wait_ge(s.b_act_steps, l * 3 + 1)
                    for c in range(2):
                        ins = pe.matmul(ps[:, 5 + 2 * c, 0:SEQ], bd[:, :], m1.sqb[:, c, :], start=True, stop=True)
                    ins.then_inc(s.b_sums, 1)
            pe.wait_ge(s.o_lo_out, l * 8 + 9)
            pe.wait_ge(s.o_hi_out, l * 8 + 9)
            pe.wait_ge(s.b_lo, l + 1)
            pe_out(pe, b, l, sub, mgb(l) + 24, OUT_Q, m1.ohi, m1.olo, None)
            pe_post(pe, b, sub)

        B_NORM = 44

        def act_mix1(act, l, nxt):
            b, s = b1, b1.s
            sub = l * 3 + 1
            U = l * UNITS1

            def hi_split(g):
                split_hi(act, b, mgb(l) + g, mgb2(l) + g // 2, g % 2)

            hi_split(2)
            act_rms(act, b, 2 * sub, SUM_PRE)
            act_r(act, b, sub)
            hi_split(3)
            hi_split(4)
            def outputs(p_):
                act.wait_ge(s.pv_done, U + 8 * p_ + 8)
                if KINDS[p_] == "B":
                    act.activation(m1.ob[:, p_ - 3, :], ps[:, 3, :], ACT.Copy).then_inc(s.o_hi_out, 1)
                    if p_ == 4:
                        act.wait_ge(s.o_hi_out, l * 8 + p_ + 2)
                        act.activation(m1.sqb[:, :, :], m1.ob[:, :, :], ACT.Square).then_inc(s.b_act_steps, 1)
                else:
                    act.activation(m1.ohi[:, p_, :], ps[:, 3, :], ACT.Copy).then_inc(s.o_hi_out, 1)

            for n_step, st in enumerate(STEPS1):
                for v in st.tr:
                    act.wait_ge(s.transposed, l * len(TEV1) + TEV1["p", v] + 1)
                    if v >= 2:
                        act.wait_ge(s.pv_done, U + v - 1)
                    nn = unit1(v)[4]
                    act.activation(m1.pt[v % 2][:, :, :].rearrange("p a b -> p (a b)")[:, 0:nn], ps[:, 2, 0:nn],
                                   ACT.Copy).then_inc(s.transposed_out, 1)
                if n_step > 0:
                    for p_ in STEPS1[n_step - 1].pairs:
                        outputs(p_)
                u = n_step - 1
                if 0 <= u < UNITS1 and KINDS[u // 8] in "AB":
                    p, h, j, kind, n = unit1(u)
                    act.wait_ge(s.max_done, l * 40 + u + 1)
                    for m in range(2 if kind == "B" else 1):
                        w = m1.w[u % 4][:, m, 0:n]
                        ins = act.activation(w, w, ACT.Exp, bias=m1.nmax[u % 4][:, m:m + 1],
                                             scale=B_SCALE if kind == "B" else 1.0,
                                             accum_out=m1.sums[u % 4][:, m:m + 1])
                    ins.then_inc(s.exp_done, 1)
                u = st.sc
                if u is not None and KINDS[u // 8] == "C":
                    w3, n = m1.w[u % 4], unit1(u)[4]
                    act.wait_ge(s.scores_done, U + u + 1)
                    act.wait_ge(s.transposed, l * len(TEV1) + TEV1["p", u - 4] + 1)
                    S_ = ps[:, sbank(u), 0:n]
                    act.activation(w3[:, 0, 0:n], S_, ACT.Sigmoid)
                    act.activation(w3[:, 1, 0:n], S_, ACT.Sigmoid, scale=-1.0).then_inc(s.exp_done, 1)
                    act.wait_ge(s.exp_done, U + u + 1)
                    act.sem_inc(s.scores_free, 1)
                if st.vt is not None:
                    act.wait_ge(s.transposed, l * len(TEV1) + TEV1["v", st.vt] + 1)
                    act.activation(m1.v[st.vt % 2][:, :, :].rearrange("p a b -> p (a b)"), ps[:, 2, :],
                                   ACT.Copy).then_inc(s.transposed_out, 1)
                for g in st.done:
                    hi_split(g + 2)
                if n_step == B_NORM:
                    act.wait_ge(s.b_sums, l + 1)
                    for c in range(2):
                        ins = act.activation(m1.rb[:, c, :], ps[:, 5 + 2 * c, 0:SEQ], ACT.Ln, bias=eps[:, :],
                                             scale=1.0 / 64)
                    ins.then_inc(s.b_act_steps, 1)
                    act.wait_ge(s.b_act_steps, l * 3 + 2)
                    act.activation(m1.rb[:, :, :], m1.rb[:, :, :], ACT.Exp, scale=-0.5).then_inc(s.b_act_steps, 1)
                if n_step == B_NORM + 2:
                    act.wait_ge(s.b_scaled, l + 1)
                    for c in range(2):
                        ins = act.activation(m1.ohi[:, 3 + c, :], m1.ob[:, c, :], ACT.Copy,
                                             scale=par[:, bass.ds(l + PAR_SUBLN, 1)])
                    ins.then_inc(s.b_hi, 1)
            outputs(7)
            act_out(act, b, l, sub, mgb(l) + 24, mgb2(l) + 12, OUT_Q)
            act_rms(act, b, 2 * sub + 1, SUM_POST)
            act_next(act, b, l, sub + 1, *nxt)

        def dve_mix1(dve, l, ch, nxt):
            b, s = b1, b1.s
            sub = l * 3 + 1
            U = l * UNITS1

            def evac(g):
                p, j = divmod(g, 3)
                dve.wait_ge(s.granules_done, mgb(l) + g + 1 + CR)
                dst = (m1.q, m1.k, m1.vt)[j][p % 2]
                factor = 0.125 if j == 0 and KINDS[p] != "B" else 1.0
                dve.scalar_tensor_tensor(out=dst[:, :], in0=ps[:, gbank1(g), :], scalar=factor, in1=r[:, 0:SEQ],
                                         op0=ALU.mult, op1=ALU.mult).then_inc(s.columns_out, 1)

            split_lo(dve, b, mgb(l) + 2, 0, handover=True)
            dve_inv(dve, b, 2 * sub)
            dve.wait_ge(s.norm_r, sub + 1)
            evac(0)
            evac(1)
            evac(2)
            dve.wait_ge(s_tb, 16 * l + 16)
            ch(dve.memset(tb[0:64, :, SEQ - 64:SEQ], NEG))
            ch.wait()
            ch(dve.memset(m1.scan[:, SEQ:SEQ + 1], 1.0))

            def probabilities(u):
                p, h, j, kind, n = unit1(u)
                w3 = m1.w[u % 4]
                w = w3[:, 0, 0:n]
                dve.wait_ge(s.exp_done, U + u + 1)
                if kind == "A":
                    ch(dve.reciprocal(m1.inv[u % 4][:, 0:1], m1.sums[u % 4][:, 0:1]))
                    ch.wait()
                    dve.tensor_scalar(w, w, m1.inv[u % 4][:, 0:1], None, ALU.mult).then_inc(s.probs_done, 1)
                elif kind == "B":
                    ch(dve.reciprocal(m1.inv[u % 4][:, 0:2], m1.sums[u % 4][:, 0:2]))
                    ch.wait()
                    ch(dve.tensor_tensor(m1.c1[u % 4][:, :], m1.inv[u % 4][:, 1:2], nlam[:, bass.ds(l, 1)], ALU.mult))
                    ch.wait()
                    ch(dve.tensor_scalar(w3[:, 1, 0:n], w3[:, 1, 0:n], m1.c1[u % 4][:, 0:1], None, ALU.mult))
                    ch.wait()
                    dve.scalar_tensor_tensor(out=w, in0=w, scalar=m1.inv[u % 4][:, 0:1], in1=w3[:, 1, 0:n],
                                             op0=ALU.mult, op1=ALU.add).then_inc(s.probs_done, 1)
                else:
                    d = w3[:, 1, n - P:n]
                    ch(dve.tensor_tensor(d, d, later[:, :], ALU.max))
                    ch.wait()
                    ch(dve.tensor_tensor_scan(m1.scan[:, SEQ - n:SEQ][:, ::-1], w3[:, 1, 0:n][:, ::-1], ones[:, 0:n],
                                              1.0, ALU.mult, ALU.mult))
                    ch.wait()
                    ch(dve.tensor_tensor(w, w, m1.scan[:, SEQ - n + 1:SEQ + 1], ALU.mult))
                    ch.wait()
                    d = w3[:, 0, n - P:n]
                    dve.tensor_tensor(d, d, strict[:, :], ALU.mult).then_inc(s.probs_done, 1)

            def logits(u):
                p, h, j, kind, n = unit1(u)
                w3 = m1.w[u % 4]
                w = w3[:, 0, 0:n]
                dve.wait_ge(s.scores_done, U + u + 1)
                if u >= 4:
                    dve.wait_ge(s.transposed, l * len(TEV1) + TEV1["p", u - 4] + 1)
                if kind == "A":
                    head = 2 * p + h
                    ch(dve.tensor_tensor(w, ps[:, sbank(u), 0:n], tb[:, head, SEQ - n:SEQ], ALU.add))
                    ch.wait()
                    dve.sem_inc(s.scores_free, 1)
                    dve.tensor_reduce(m1.nmax[u % 4][:, 0:1], w, AX.X, ALU.max, negate=True).then_inc(s.max_done, 1)
                else:
                    head = 2 * (p - 3) + h
                    for m in range(2):
                        ch(dve.scalar_tensor_tensor(
                            out=w3[:, m, 0:n], in0=dist[:, SEQ - n:SEQ], scalar=-SLOPE[head] / B_SCALE,
                            in1=ps[:, sbank(u) + m, 0:n], op0=ALU.mult, op1=ALU.add))
                    ch.wait()
                    dve.sem_inc(s.scores_free, 1)
                    ch(dve.tensor_reduce(m1.nmax[u % 4][:, 0:2], w3[:, :, 0:n], AX.X, ALU.max, negate=True))
                    ch.wait()
                    dve.tensor_scalar(m1.nmax[u % 4][:, 0:2], m1.nmax[u % 4][:, 0:2], B_SCALE, None,
                                      ALU.mult).then_inc(s.max_done, 1)

            def outputs(p_):
                dve.wait_ge(s.o_hi_out, l * 8 + p_ + 2)
                if KINDS[p_] == "B":
                    dve.sem_inc(s.o_lo_out, 1)
                else:
                    dve.tensor_tensor(m1.olo[:, p_, :], ps[:, 3, :], m1.ohi[:, p_, :].bitcast(F32),
                                      ALU.subtract).then_inc(s.o_lo_out, 1)

            for n_step, st in enumerate(STEPS1):
                if 2 <= n_step <= UNITS1 + 1:
                    probabilities(n_step - 2)
                if st.sc is not None and KINDS[st.sc // 8] != "C":
                    logits(st.sc)
                if n_step > 0:
                    for p_ in STEPS1[n_step - 1].pairs:
                        outputs(p_)
                for g in st.done:
                    evac(g)
                if n_step == B_NORM + 1:
                    dve.wait_ge(s.b_act_steps, l * 3 + 3)
                    dve.tensor_tensor(m1.ob[:, :, :], m1.ob[:, :, :], m1.rb[:, :, :],
                                      ALU.mult).then_inc(s.b_scaled, 1)
                if n_step == B_NORM + 3:
                    dve.wait_ge(s.b_scaled, l + 1)
                    dve.wait_ge(s.b_hi, l + 1)
                    dve.scalar_tensor_tensor(out=m1.olo[:, 3:5, :], in0=m1.ob[:, :, :],
                                             scalar=par[:, bass.ds(l + PAR_SUBLN, 1)],
                                             in1=m1.ohi[:, 3:5, :].bitcast(F32), op0=ALU.mult,
                                             op1=ALU.subtract).then_inc(s.b_lo, 1)
            outputs(7)
            dve_out(dve, b, l, sub, mgb(l) + 24, OUT_Q, ch, 1.0, PAR_MIXPOST, nxt)


        def pool_mix1(pool, l):
            for g in range(3, 26):
                split_lo(pool, b1, mgb(l) + g, g % 2, handover=(g == 3))

        fg = Ffn(
            first=False, sub=lambda l: l * 2 + 1, gb=lambda l: l * b2.GL + MIX2_GRAN,
            gb2=lambda l: l * (b2.GL // 2) + MIX2_GRAN // 2,
            ev=lambda l: l * b2.evf_layer, hb=lambda l: l * KF,
            gate=I["ffn_w_up_2"].rearrange("l d f -> (l d) f"), up=I["ffn_w_up_2"].rearrange("l d f -> (l d) f"),
            upoff=FF, down=I["ffn_w_down_2"].rearrange("l f d -> (l f) d"))
        g2b = lambda l: l * b2.GL
        g2b2 = lambda l: l * (b2.GL // 2)
        win2 = I["w_in_2"].rearrange("l d f -> (l d) f")
        wout2 = I["w_out_2"].rearrange("l d f -> (l d) f")
        pw2 = I["a_pw_w_2"].rearrange("l d f -> (l d) f")
        NCOL = len(COLS2)

        def sp_mix2(sp, l):
            for g, c0 in enumerate(COLS2):
                row = l * D if c0 else l * KD * P
                load_raw(sp, b2, g2b(l) + g, g % 2, win2[bass.ds(row, D), c0:c0 + P], (8, P))
            load_raw(sp, b2, g2b(l) + NCOL, NCOL % 2, pw2[bass.ds(l * 2 * P, 2 * P), :], (2, PAIR))
            sp_wout(sp, b2, l, g2b(l) + NCOL + 1, wout2)

        def n_of(g):
            return 512 if g == NCOL else 1024

        def gbank(g):
            return 4 if g == 2 else 2 if g < 8 and g % 2 == 0 else 0

        def unit2(u):
            p, qb, h = u // (2 * QB), (u // 2) % QB, u % 2
            return p, qb, h, (0 if qb == 0 else META + P * (qb - 1)), (META if qb == 0 else P), META + P * qb

        def s2(u, n):
            bank = 4 + 2 * (u % 2)
            return ps[:, bank:bank + 2, :].rearrange("p a b -> p (a b)")[:, SEQ - META:SEQ - META + n]

        def inv_tile(c):
            return S[2 + (INVERSE_STEP.index(c) if c in INVERSE_STEP else {7: 0, 3: 1, 4: 2, 5: 3}[c])]

        def pe_mix2(pe, l):
            b, s = b2, b2.s
            sub = l * 2
            U = l * UNITS2
            TE = l * len(TEV2)

            def gtile(g, t):
                if t == 0:
                    pe.wait_ge(s.weights_split, g2b(l) + g + 1 + CR)
                    if g >= 3:
                        pe.wait_ge(s.columns_out, l * NCOL + g + CR - (1 if g < 8 else 0))
                ins = tile_mm(pe, b, gbank(g), g % 2, t * P, xhi[:, t, :], xlo[:, t, :], t == 0, t == 7)
                if t == 7:
                    ins.then_inc(s.granules_done, 1)

            def scores(u):
                p, qb, h, t0, nq, n = unit2(u)
                pe.wait_ge(s.columns_out, l * NCOL + QKV2[p] + 2 + CR)
                pe.wait_ge(s.scores_free, U + u + 1)
                if u == 2:
                    pe.wait_ge(s.transposed_out, TE + TEV2["v", 0] + 2)
                bank = 4 + 2 * (u % 2)
                a = 64 * h
                lhs = m2.q[p % 2][a:a + 64, t0:t0 + P]
                ins = pe.matmul(ps[:, bank, SEQ - META:SEQ], lhs, m2.k[p % 2][a:a + 64, 0:META], start=True,
                                stop=True)
                if qb:
                    ins = pe.matmul(ps[0:nq, bank + 1, 0:P * qb], lhs, m2.k[p % 2][a:a + 64, META:n],
                                    start=True, stop=True)
                ins.then_inc(s.scores_done, 1)

            def vtrans(p):
                pe.wait_ge(s.columns_out, l * NCOL + QKV2[p] + 3 + CR)
                pe.wait_ge(s.transposed_out, TE + TEV2["v", p] + 1)
                pe.wait_ge(s.scores_free, U + 2 * QB * p + 1 + CR)
                pe.transpose(ps[0:META, 4, 0:P], m2.vt[p % 2][:, 0:META], ident[:, :])
                for t in range(4):
                    t0 = META + P * t
                    ins = pe.transpose(ps[:, 2, P * t:P * t + P], m2.vt[p % 2][:, t0:t0 + P], ident[:, :])
                ins.then_inc(s.transposed, 1)

            def ptrans(u):
                p, qb, h, t0, nq, n = unit2(u)
                pe.wait_ge(s.probs_done, U + u + 1)
                pe.wait_ge(s.transposed_out, TE + TEV2["p", u] + 1)
                pe.wait_ge(s.scores_free, U + min(u + LAG, UNITS2) + CR)
                ins = pe.transpose(ps[0:META, 6 - 2 * ((u + LAG) % 2), 0:P], m2.w[u % 4][:, 0:META], ident[:, :])
                for t in range(qb):
                    ins = pe.transpose(ps[:, 2, P * t:P * t + P], m2.w[u % 4][:, META + P * t:META + P * t + P],
                                       ident[:, :])
                ins.then_inc(s.transposed, 1)

            def pv(u):
                p, qb, h, t0, nq, n = unit2(u)
                pe.wait_ge(s.transposed_out, TE + TEV2["p", u] + 2)
                if h == 0 and qb < 2:
                    pe.wait_ge(s.o_hi_out, l * 8 + 2 * p + qb + 1)
                c0 = P * max(qb - 1, 0)
                o = ps[64 * h:64 * h + 64, 3, c0:c0 + nq]
                ins = pe.matmul(o, m2.v[p % 2][0:META, 0, 64 * h:64 * h + 64], m2.pt[u % 2][0:META, 0, 0:nq],
                                start=True, stop=(qb == 0))
                for t in range(qb):
                    ins = pe.matmul(o, m2.v[p % 2][:, 1 + t, 64 * h:64 * h + 64], m2.pt[u % 2][:, 1 + t, :],
                                    start=False, stop=(t == qb - 1))
                ins.then_inc(s.pv_done, 1)

            def forget(h):
                pe.wait_ge(s.forget_sums, l + 1)
                if h >= 2:
                    pe.wait_ge(s.forget_out, l * 8 + h - 1)
                for i, (t0, w) in enumerate(halves(b)):
                    ins = pe.matmul(ps[:, 4 + 2 * (h % 2) + i, 0:w], ident[0:8, h:h + 1].to_broadcast([8, P]),
                                    m2.nf[:, t0:t0 + w], start=True, stop=True)
                ins.then_inc(s.forget_spread, 1)

            pe.wait_ge(s.out_free, 4 * sub + CR)
            pe_hi_first(pe, b, g2b(l), sub, [(g, gbank(g), t * P, t, t == 0, t == 7)
                                             for t in range(8) for g in range(2)])
            pe_pre_sum(pe, b, sub)
            for g in range(2, 8):
                for t in range(8):
                    gtile(g, t)
                    if g == 2 and t == 2:
                        pe_spread(pe, b, 2 * sub, BC_PRE)
                if g == 3:
                    pe.wait_ge(s.norm_r, sub + 1)
                if g >= 4:
                    forget(2 * g - 8)
                    forget(2 * g - 7)
            pe.wait_ge(s.forget_out, l * 8 + 8)
            def sums(k, n_step):
                if k == "mean":
                    pe.wait_ge(s.dw_taps, l * len(DW_OPS) + len(DW_OPS))
                    mat, srcs = ones, [aconv[:, 0, :], aconv[:, 1, :]]
                elif k == "variance":
                    pe.wait_ge(s.ln_squared, l + 1)
                    mat, srcs = ones, [m2.lsq[:, 0, :], m2.lsq[:, 1, :]]
                else:
                    i = SQUARED.index(k)
                    pe.wait_ge(s.head_squared, l * 8 + i + 1)
                    mat, srcs = bd, [S[i % 2]]
                pe.wait_ge(s.transposed_out, TE + TEV2["x", k] + 1)
                for o, t0, w in ((ps[:, 6 - 2 * (n_step % 2), 0:META], 0, META), (ps[:, 2, :], META, SEQ)):
                    for j, src in enumerate(srcs):
                        ins = pe.matmul(o, mat[:, 0:P], src[:, t0:t0 + w], start=(j == 0), stop=(j == len(srcs) - 1))
                ins.then_inc(s.transposed, 1)

            for n_step, st in enumerate(STEPS2):
                for u in st.tr:
                    ptrans(u)
                if st.sc is not None:
                    scores(st.sc)
                for tile in st.tiles[:2]:
                    gtile(*tile)
                if st.vt is not None:
                    vtrans(st.vt)
                if st.extra is not None:
                    sums(st.extra, n_step)
                for tile in st.tiles[2:]:
                    gtile(*tile)
                for u in st.tr:
                    pv(u)
            pe.wait_ge(s.weights_split, g2b(l) + NCOL + 1 + CR)
            pe.wait_ge(s.a_lo, l + 1)
            pe.wait_ge(s.columns_out, l * NCOL + NCOL + CR)
            for o in range(2):
                if o == 1:
                    pe.wait_ge(s.o_hi_out, l * 8 + 9)
                for k in range(2):
                    ins = tile_mm(pe, b, 2 * o, NCOL % 2, k * PAIR + o * P, m2.ahi[:, k, :], m2.alo[:, k, :],
                                  k == 0, k == 1)
            ins.then_inc(s.granules_done, 1)
            for i in range(5, 8):
                pe.wait_ge(s.head_squared, l * 8 + i + 1)
                if i == 7:
                    pe.wait_ge(s.head_steps, l * 16 + 8 + 1)
                for j, (t0, w) in enumerate(halves(b)):
                    ins = pe.matmul(ps[:, (4, 6, 4)[i - 5] + j, 0:w], bd[:, :], S[i % 2][:, t0:t0 + w],
                                    start=True, stop=True)
                ins.then_inc(s.head_sums, 1)
            pe.wait_ge(s.pw_out, l + 1)
            pe.wait_ge(s.head_steps, l * 16 + 8 + 4)
            pe_out(pe, b, l, sub, g2b(l) + NCOL + 1, OUT_Q, m2.ohi, m2.olo,
                   lambda k: pe.wait_ge(s.head_lo, l * 8 + HEADS_ORDER.index(k) + 1),
                   order=([0, 1, 2, 3], [2, 3, 0, 1]))
            pe_post(pe, b, sub)

        def act_mix2(act, l, nxt):
            b, s = b2, b2.s
            sub = l * 2
            U = l * UNITS2
            TE = l * len(TEV2)

            def hi_split(g):
                split_hi(act, b, g2b(l) + g, g2b2(l) + g // 2, g % 2, n_of(g))

            def forget(h):
                act.wait_ge(s.forget_spread, l * 8 + h + 1)
                act.activation(tview(b, fb[:, h, :]), pview(b, 4 + 2 * (h % 2)), ACT.Copy).then_inc(s.forget_out, 1)

            hi_split(2)
            act_rms(act, b, 2 * sub, SUM_PRE)
            act_r(act, b, sub)
            hi_split(3)
            act.wait_ge(s.forget_in, l + 1)
            act.activation(m2.e[:, :], m2.u[:, :], ACT.Abs).then_inc(s.forget_steps, 1)
            act.wait_ge(s.forget_steps, l * 3 + 1)
            act.activation(m2.e[:, :], m2.e[:, :], ACT.Exp, scale=-1.0).then_inc(s.forget_steps, 1)
            act.wait_ge(s.forget_steps, l * 3 + 2)
            act.activation(m2.e[:, :], m2.e[:, :], ACT.Ln, bias=1.0).then_inc(s.forget_steps, 1)
            for g in range(2, 8):
                hi_split(g + 2)
                if g == 4:
                    act.wait_ge(s.a_gate_in, l + 1)
                    act.activation(aconv[:, :, :], aconv[:, :, :], ACT.Sigmoid).then_inc(s.a_gate_done, 1)
                if g >= 4:
                    forget(2 * g - 8)
                    forget(2 * g - 7)
            def square(i):
                c = SQUARED[i]
                if c < 4:
                    act.wait_ge(s.o_hi_out, l * 8 + 2 * c + 3)
                elif c >= 6:
                    act.wait_ge(s.short_done, l * 2 + c - 5)
                else:
                    act.wait_ge(s.pw_out, l + 1)
                if i == 7:
                    act.wait_ge(s.head_sums, l * 3 + 1)
                act.activation(S[i % 2][:, 0:TM], y[:, c, :], ACT.Square).then_inc(s.head_squared, 1)

            def exps(chunks, base):
                act.wait_ge(s.head_steps, l * 16 + base + 4)
                for c in chunks:
                    t = inv_tile(c)[:, 0:TM]
                    act.activation(t, t, ACT.Exp, scale=-0.5).then_inc(s.head_steps, 1)

            def hi(i):
                c = HEADS_ORDER[i]
                act.wait_ge(s.head_scaled, l * 8 + (INVERSE_STEP + INVERSE_LATE).index(c) + 1)
                act.activation(m2.ohi[:, c, :], y[:, c, :], ACT.Copy,
                               scale=gain(PAR_HEADG, l, c)).then_inc(s.head_hi, 1)

            def outputs(v):
                p, qb, h, t0, nq, n = unit2(v)
                if h == 1 and qb in (0, QB - 1):
                    act.wait_ge(s.pv_done, U + v + 1)
                    dst, src = (y[:, p, 0:META], ps[:, 3, 0:META]) if qb == 0 else (y[:, p, META:TM], ps[:, 3, :])
                    act.activation(dst, src, ACT.Copy).then_inc(s.o_hi_out, 1)

            for n_step, st in enumerate(STEPS2):
                for v in st.tr:
                    p, qb, h, t0, nq, n = unit2(v)
                    act.wait_ge(s.transposed, TE + TEV2["p", v] + 1)
                    if v >= 2:
                        act.wait_ge(s.pv_done, U + v - 1)
                    ins = act.activation(m2.pt[v % 2][0:META, 0, :], ps[0:META, 6 - 2 * (n_step % 2), 0:P], ACT.Copy)
                    if qb:
                        ins = act.activation(m2.pt[v % 2][:, 1:1 + qb, :].rearrange("p a b -> p (a b)"),
                                             ps[:, 2, 0:P * qb], ACT.Copy)
                    ins.then_inc(s.transposed_out, 1)
                if n_step > LAG:
                    outputs(n_step - LAG - 1)
                u = n_step - 1
                if 0 <= u < UNITS2:
                    act.wait_ge(s.max_done, U + u + 1)
                    w = m2.w[u % 4][:, 0:unit2(u)[5]]
                    act.activation(w, w, ACT.Exp, bias=m2.nmax[u % 4][:, :], scale=1.0,
                                   accum_out=m2.sums[u % 4][:, :]).then_inc(s.exp_done, 1)
                u = n_step - 2
                if 0 <= u < UNITS2:
                    w = m2.w[u % 4][:, 0:unit2(u)[5]]
                    act.wait_ge(s.inv_done, U + u + 1)
                    act.activation(w, w, ACT.Copy, scale=m2.inv[u % 4][:, :]).then_inc(s.probs_done, 1)
                if st.vt is not None:
                    act.wait_ge(s.transposed, TE + TEV2["v", st.vt] + 1)
                    act.activation(m2.v[st.vt % 2][0:META, 0, :], ps[0:META, 4, 0:P], ACT.Copy)
                    act.activation(m2.v[st.vt % 2][:, 1:QB, :].rearrange("p a b -> p (a b)"), ps[:, 2, :],
                                   ACT.Copy).then_inc(s.transposed_out, 1)
                if st.extra is not None:
                    x_ = st.extra
                    dst = m2.lrs if x_ in ("mean", "variance") else inv_tile(x_)
                    if x_ == 7:
                        act.wait_ge(s.head_scaled, l * 8 + 1)
                    act.wait_ge(s.transposed, TE + TEV2["x", x_] + 1)
                    act.activation(dst[:, 0:META], ps[:, 6 - 2 * (n_step % 2), 0:META], ACT.Copy)
                    act.activation(dst[:, META:TM], ps[:, 2, :], ACT.Copy).then_inc(s.transposed_out, 1)
                for g in st.done:
                    hi_split(g + 2)
                if n_step in SQUARE_STEP:
                    square(SQUARE_STEP[n_step])
                if n_step == 24:
                    act.wait_ge(s.ln_centered, l + 1)
                    act.activation(m2.lsq[:, :, :], aconv[:, :, :], ACT.Square).then_inc(s.ln_squared, 1)
                if n_step == 25:
                    t = m2.lrs[:, :]
                    act.wait_ge(s.transposed_out, TE + TEV2["x", "variance"] + 2)
                    act.activation(t, t, ACT.Ln, bias=lneps[:, :], scale=1.0 / 256).then_inc(s.ln_steps, 1)
                    act.wait_ge(s.ln_steps, l * 2 + 1)
                    act.activation(t, t, ACT.Exp, scale=-0.5).then_inc(s.ln_steps, 1)
                if n_step == 27:
                    act.wait_ge(s.ln_scaled, l + 1)
                    for c in range(2):
                        ins = act.activation(aconv[:, c, :], aconv[:, c, :], ACT.Silu,
                                             bias=par[:, bass.ds(l * 2 + (PAR_LNB + c), 1)],
                                             scale=par[:, bass.ds(l * 2 + (PAR_LNG + c), 1)])
                    ins.then_inc(s.ln_silu, 1)
                    act.wait_ge(s.ln_silu, 2 * l + 1)
                    act.activation(m2.ahi[:, :, :], aconv[:, :, :], ACT.Copy).then_inc(s.ln_silu, 1)
                if n_step == 35:
                    act.wait_ge(s.transposed_out, TE + TEV2["x", 2] + 2)
                    for c in INVERSE_STEP:
                        t = inv_tile(c)[:, 0:TM]
                        act.activation(t, t, ACT.Ln, bias=eps[:, :], scale=1.0 / 64).then_inc(s.head_steps, 1)
                if n_step == 36:
                    exps(INVERSE_STEP[0:2], 0)
                if n_step == 37:
                    exps(INVERSE_STEP[2:4], 0)
                if n_step in (39, 40, 41):
                    hi(n_step - 39)
            outputs(UNITS2 - 1)
            square(5)
            act.wait_ge(s.granules_done, g2b(l) + NCOL + 1 + CR)
            for o in range(2):
                ins = act.activation(tview(b, y[:, 4 + o, :]), pview(b, 2 * o), ACT.Copy)
            ins.then_inc(s.pw_out, 1)
            square(6)
            square(7)
            hi_split(NCOL + 2)
            act.wait_ge(s.head_sums, l * 3 + 1)
            for c, bank in ((3, 4), (7, None), (4, 6), (5, 4)):
                dst = inv_tile(c)[:, 0:TM]
                if c == 7:
                    act.wait_ge(s.transposed_out, TE + TEV2["x", 7] + 2)
                    ins = act.activation(dst, dst, ACT.Ln, bias=eps[:, :], scale=1.0 / 64)
                else:
                    act.wait_ge(s.head_sums, l * 3 + (3, 4, 5).index(c) + 1)
                    ins = act.activation(tview(b, dst), pview(b, bank), ACT.Ln, bias=eps[:, :], scale=1.0 / 64)
                ins.then_inc(s.head_steps, 1)
            exps(INVERSE_LATE, 8)
            for i in range(3, 8):
                hi(i)
            act_out(act, b, l, sub, g2b(l) + NCOL + 1, g2b2(l) + (NCOL + 1) // 2, OUT_Q)
            act_rms(act, b, 2 * sub + 1, SUM_POST)
            act_next(act, b, l, sub + 1, *nxt)

        def dve_mix2(dve, l, ch, nxt):
            b, s = b2, b2.s
            sub = l * 2
            U = l * UNITS2
            TE = l * len(TEV2)

            def scaled(dst, g, rows=P, factor=None):
                src = ps[0:rows, gbank(g):gbank(g) + 2, 0:b.w]
                rr = tview(b, r[0:rows, 0:TM])
                if factor is None:
                    return dve.tensor_tensor(tview(b, dst), src, rr, ALU.mult)
                return dve.scalar_tensor_tensor(out=tview(b, dst), in0=src, scalar=factor, in1=rr,
                                                op0=ALU.mult, op1=ALU.mult)

            def evac(g):
                dve.wait_ge(s.granules_done, g2b(l) + g + 1 + CR)
                if g == 0:
                    dst = m2.u[:, :]
                elif g < 5:
                    c = (g - 1) // 2
                    dst = aconv[:, c, :] if g % 2 == 0 else apad[:, c, TAPS - 1:]
                elif g in SC_B2 + SC_C2 + SC_X2:
                    dst = scb[:, :] if g in SC_B2 else scc[:, :] if g in SC_C2 else scx[:, 2:]
                else:
                    p = max(i for i in range(4) if g >= QKV2[i])
                    dst = (m2.q, m2.k, m2.vt)[g - QKV2[p]][p % 2][:, :]
                scaled(dst, g, 8 if g == 0 else P, 0.125 if g in QKV2 else None).then_inc(s.columns_out, 1)

            def short_conv(c, part):
                if part == 0:
                    dve.wait_ge(s.columns_out, l * NCOL + SC_X2[c] + 1 + CR)
                    ch(dve.tensor_tensor(scx[:, 2:], scx[:, 2:], scc[:, :], ALU.mult))
                for k in ((2,), (1,), (0,))[part]:
                    w = par[:, bass.ds(l * 6 + (PAR_SCW + 2 * k + c), 1)]
                    ch.wait()
                    if k == 2:
                        ch(dve.tensor_scalar(scc[:, :], scx[:, 2:2 + TM], w, None, ALU.mult))
                    else:
                        ch(dve.scalar_tensor_tensor(out=scc[:, :], in0=scx[:, k:k + TM], scalar=w, in1=scc[:, :],
                                                    op0=ALU.mult, op1=ALU.add))
                if part == 2:
                    ch.wait()
                    dve.tensor_tensor(y[:, 6 + c, :], scb[:, :], scc[:, :], ALU.mult).then_inc(s.short_done, 1)

            dw_at = [0]

            def depthwise(n):
                for t, c in DW_OPS[dw_at[0]:dw_at[0] + n]:
                    w = par[:, bass.ds(l * 2 * TAPS + (PAR_DW + 2 * t + c), 1)]
                    src, dst = apad[:, c, t:t + TM], aconv[:, c, :]
                    if t == 0:
                        dve.tensor_scalar(dst, src, w, par[:, bass.ds(l * 2 + (PAR_DWB + c), 1)], ALU.mult,
                                          ALU.add).then_inc(s.dw_taps, 1)
                    else:
                        dve.wait_ge(s.dw_taps, l * len(DW_OPS) + 2 * (t - 1) + c + 1)
                        dve.scalar_tensor_tensor(out=dst, in0=src, scalar=w, in1=dst, op0=ALU.mult,
                                                 op1=ALU.add).then_inc(s.dw_taps, 1)
                dw_at[0] += n

            split_lo(dve, b, g2b(l) + 2, 0, handover=True)
            dve_inv(dve, b, 2 * sub)
            ch(dve.memset(apad[:, :, 0:TAPS - 1], 0.0))
            ch(dve.memset(scx[:, 0:2], 0.0))
            dve.wait_ge(s.norm_r, sub + 1)
            evac(0)
            dve.wait_ge(s.columns_out, l * NCOL + 1 + CR)
            dve.tensor_scalar(m2.u[:, :], m2.u[:, :], bf[:, bass.ds(l, 1)], None, ALU.add).then_inc(s.forget_in, 1)
            evac(1)
            dve.wait_ge(s.forget_steps, l * 3 + 3)
            ch(dve.scalar_tensor_tensor(out=m2.lf[:, :], in0=m2.u[:, :], scalar=0.0, in1=m2.e[:, :], op0=ALU.min,
                                        op1=ALU.subtract))
            ch.wait()
            for a, n in ((0, SEQ), (SEQ, META)):
                ch(dve.tensor_tensor_scan(m2.nf[:, a:a + n], ones[0:8, 0:n], m2.lf[:, a:a + n],
                                          0.0 if a == 0 else m2.nf[:, a - 1:a], ALU.mult, ALU.subtract))
                ch.wait()
            dve.sem_inc(s.forget_sums, 1)
            for g in range(2, 8):
                evac(g)
                if g == 4:
                    dve.wait_ge(s.columns_out, l * NCOL + 5 + CR)
                    dve.sem_inc(s.a_gate_in, 1)
                if g == 5:
                    dve.wait_ge(s.a_gate_done, l + 1)
                    ch(dve.tensor_tensor(apad[:, :, TAPS - 1:], apad[:, :, TAPS - 1:], aconv[:, :, :], ALU.mult))
                    ch.wait()
            dve.wait_ge(s.forget_out, l * 8 + 8)

            def mul(c):
                if c in INVERSE_STEP:
                    dve.wait_ge(s.head_steps, l * 16 + 4 + INVERSE_STEP.index(c) + 1)
                else:
                    dve.wait_ge(s.head_steps, l * 16 + 12 + INVERSE_LATE.index(c) + 1)
                dve.tensor_tensor(y[:, c, :], y[:, c, :], inv_tile(c)[:, 0:TM], ALU.mult).then_inc(s.head_scaled, 1)

            def lo(i):
                c = HEADS_ORDER[i]
                dve.wait_ge(s.head_hi, l * 8 + i + 1)
                dve.scalar_tensor_tensor(out=m2.olo[:, c, :], in0=y[:, c, :], scalar=gain(PAR_HEADG, l, c),
                                         in1=m2.ohi[:, c, :].bitcast(F32), op0=ALU.mult,
                                         op1=ALU.subtract).then_inc(s.head_lo, 1)

            for n_step, st in enumerate(STEPS2):
                if 2 <= n_step <= UNITS2 + 1:
                    u = n_step - 2
                    dve.wait_ge(s.exp_done, U + u + 1)
                    dve.reciprocal(m2.inv[u % 4][:, :], m2.sums[u % 4][:, :]).then_inc(s.inv_done, 1)
                u = st.sc
                if u is not None:
                    p, qb, h, t0, nq, n = unit2(u)
                    w = m2.w[u % 4]
                    dve.wait_ge(s.scores_done, U + u + 1)
                    if u >= 4:
                        dve.wait_ge(s.transposed, TE + TEV2["p", u - 4] + 1)
                    ch(dve.tensor_tensor(w[:, 0:n], s2(u, n)[:, :], fb[:, 2 * p + h, 0:n], ALU.add))
                    ch.wait()
                    dve.sem_inc(s.scores_free, 1)
                    ch(dve.tensor_tensor(w[:, n - nq:n], w[:, n - nq:n], negc[:, 0:nq], ALU.add))
                    ch.wait()
                    dve.tensor_reduce(m2.nmax[u % 4][:, :], w[:, 0:n], AX.X, ALU.max,
                                      negate=True).then_inc(s.max_done, 1)
                for g in st.done:
                    evac(g)
                if n_step in SHORT_STEP:
                    short_conv(*SHORT_STEP[n_step])
                depthwise(DW_PER_STEP)
                if n_step == 23:
                    dve.wait_ge(s.transposed_out, TE + TEV2["x", "mean"] + 2)
                    for c in range(2):
                        ch(dve.scalar_tensor_tensor(out=aconv[:, c, :], in0=m2.lrs[:, :], scalar=-1.0 / 256,
                                                    in1=aconv[:, c, :], op0=ALU.mult, op1=ALU.add))
                    ch.wait()
                    dve.sem_inc(s.ln_centered, 1)
                if n_step == 26:
                    dve.wait_ge(s.ln_steps, l * 2 + 2)
                    dve.tensor_tensor(aconv[:, :, :], aconv[:, :, :],
                                      m2.lrs[:, :].unsqueeze(1).to_broadcast([P, 2, TM]),
                                      ALU.mult).then_inc(s.ln_scaled, 1)
                if n_step == 28:
                    dve.wait_ge(s.ln_silu, 2 * l + 2)
                    dve.tensor_tensor(m2.alo[:, :, :], aconv[:, :, :], m2.ahi[:, :, :].bitcast(F32),
                                      ALU.subtract).then_inc(s.a_lo, 1)
                for c in {37: (0,), 39: (1,), 40: (6, 2)}.get(n_step, ()):
                    mul(c)
                if n_step == 42:
                    for i in range(3):
                        lo(i)
            assert dw_at[0] >= len(DW_OPS)
            split_lo(dve, b, g2b(l) + NCOL + 2, (NCOL + 2) % 2, handover=True)
            for c in INVERSE_LATE:
                mul(c)
            for i in range(3, 8):
                lo(i)
            dve_out(dve, b, l, sub, g2b(l) + NCOL + 1, OUT_Q, ch, 1.0, PAR_MIXPOST2, nxt)

        def pool_mix2(pool, l):
            for g in range(3, NCOL + 2):
                split_lo(pool, b2, g2b(l) + g, g % 2, n_of(g), handover=(g == 3))

        def rows(name):
            t = I[name]
            return t.rearrange("l (c p) -> (l c) p", p=P)

        P1 = ["ffn1_pre_g", "ffn1_post_g", "mix_pre_g", "mix_post_g", "ffn2_pre_g", "ffn2_post_g"]
        P2 = ["mix_pre_g_2", "mix_post_g_2", "ffn_pre_g_2", "ffn_post_g_2", "head_g_2"]
        P2B = ["a_dw_b_2", "a_ln_g_2", "a_ln_b_2"]
        PSIZE = [96, 106, 124, 88, 88, 88]
        PCOL = [0, 96, 202, 326, 414, 502]
        NLD_PAR = 5 + 3 + 2 + 1 + 1 + 3 + 1

        def sp_setup(sp):
            for i, n_ in enumerate(P1):
                sp.dma_start(prow[0][16 * i:16 * i + 16, :], rows(n_)).then_inc(s_ld[0], 16)
            sp.dma_start(xin, I["x"].rearrange("b (a p) d -> p (b a) d", p=P)).then_inc(s_ld[1], 16)

        def act_loads(act):
            for i, n_ in enumerate(P2):
                act.dma_start(prow[1][16 * i:16 * i + 16, :], rows(n_)).then_inc(s_ld[2], 16)
            for i, n_ in enumerate(P2B):
                act.dma_start(prow[1][80 + 4 * i:84 + 4 * i, :], rows(n_)).then_inc(s_ld[2], 16)
            for i in range(2):
                act.dma_start(prow[1][92:94, 64 * i:64 * i + 64], I["diff_subln_g"]).then_inc(s_ld[2], 16)
            act.dma_start(prow[1][94:106, :],
                          I["sc_conv_w_2"].rearrange("l k (c p) -> (l k c) p", p=P)).then_inc(s_ld[2], 16)
            act.dma_start(prow[2][0:124, :],
                          I["a_dw_w_2"].rearrange("l k (c p) -> (l k c) p", p=P)).then_inc(s_ld[2], 16)
            conv_rows = I["ffn_conv_w_2"].rearrange("l k (c p) -> (l k c) p", p=P)
            for i in range(3):
                act.dma_start(prow[3 + i][0:88, :], conv_rows[88 * i:88 * i + 88, :]).then_inc(s_ld[2], 16)
            act.dma_start(metain[:, :], I["meta_tokens_2"]).then_inc(s_ld[2], 16)

        def pool_loads(pool):
            pool.dma_start(relin[:, :], I["rel_bias"].rearrange("l h r -> (l h) r")).then_inc(s_ld[3], 16)
            for i, n_ in enumerate(["diff_lambda_q1", "diff_lambda_k1", "diff_lambda_q2", "diff_lambda_k2"]):
                pool.dma_start(lam_in[:, i, :, :].rearrange("p l d -> p (l d)"),
                               I[n_].rearrange("l d -> (l d)").partition_broadcast(P)).then_inc(s_ld[4], 16)
            with nc.allow_non_contiguous_dma(reason="sixteen forget biases"):
                pool.dma_start(bf[:, :], I["b_forget_2"].rearrange("l h -> h l")).then_inc(s_ld[5], 16)

        def pool_setup(pool):
            pool.memset(ident[:, :], 0.0).then_inc(s_mask, 1)
            pool.wait_ge(s_mask, 1)
            pool.affine_select(out=ident[:, :], in_=ident[:, :], compare_op=ALU.not_equal, fill=1.0, base=0,
                               pattern=[[-1, P]], channel_multiplier=1).then_inc(s_const, 1)
            pool_loads(pool)

            pool.iota(dist[:, :], pattern=[[-1, SEQ]], base=SEQ - P, channel_multiplier=1,
                      allow_small_or_imprecise_dtypes=True).then_inc(s_set, 1)
            pool.memset(strict[:, :], 1.0).then_inc(s_set, 1)
            pool.memset(later[:, :], 0.0).then_inc(s_set, 1)
            pool.memset(bd[:, :], 0.0).then_inc(s_set, 1)
            pool.wait_ge(s_set, 4)
            pool.affine_select(out=strict[:, :], in_=strict[:, :], compare_op=ALU.is_gt, fill=0.0, base=0,
                               pattern=[[-1, P]], channel_multiplier=1).then_inc(s_set, 1)
            pool.affine_select(out=later[:, :], in_=later[:, :], compare_op=ALU.is_gt, fill=1.0, base=0,
                               pattern=[[-1, P]], channel_multiplier=1).then_inc(s_set, 1)
            for h in range(2):
                pool.wait_ge(s_set, 6 + h)
                pool.memset(bd[64 * h:64 * h + 64, 64 * h:64 * h + 64], 1.0).then_inc(s_set, 1)
            pool.wait_ge(s_dist, 1)
            pool.memset(dist[0:64, SEQ - 64:SEQ], -NEG).then_inc(s_set, 1)
            pool.memset(negc[:, :], 0.0).then_inc(s_set, 1)
            pool.wait_ge(s_set, 10)
            pool.affine_select(out=negc[:, :], in_=negc[:, :], compare_op=ALU.is_ge, fill=NEG, base=0,
                               pattern=[[-1, P]], channel_multiplier=1).then_inc(s_set, 1)

        def dve_setup(dve, ch):
            dve.memset(ones[:, :], 1.0).then_inc(s_ones, 1)
            dve.memset(eps[:, :], EPS).then_inc(s_ones, 1)
            dve.memset(lneps[:, :], LN_EPS).then_inc(s_ones, 1)
            dve.sem_inc(b1.s.weights_split, CR)
            for b in (b1, b2):
                dve.sem_inc(b.s.hidden_free, CR)
                dve.sem_inc(b.s.columns_out, CR)
                dve.sem_inc(b.s.scores_free, CR)
            dve.sem_inc(b1.s.o_lo_out, 1)
            dve.wait_ge(s_ones, 3)
            dve.wait_ge(s_ld[3], 16)
            dve.tensor_copy(rev[:, 640 - 257:640], relin[:, ::-1]).then_inc(s_rev, 1)
            dve.tensor_scalar(rev[:, 0:640 - 257], ones[0:12, 0:640 - 257], relin[:, 256:257], None,
                              ALU.mult).then_inc(s_rev, 1)
            def parameters(i):
                dve.wait_ge(s_pt, i + 1)
                dve.tensor_copy(par[:, PCOL[i]:PCOL[i] + PSIZE[i]], ps[:, 2 + i, 0:PSIZE[i]]).then_inc(s_pc, 1)

            parameters(0)
            dve.wait_ge(s_ld[4], 64)
            for i in range(2):
                ch(dve.tensor_tensor(lam_pr[:, i, :, :], lam_in[:, 2 * i, :, :], lam_in[:, 2 * i + 1, :, :], ALU.mult))
            ch.wait()
            dve.tensor_reduce(lam_s[:, :, :], lam_pr[:, :, :, :], AX.X, ALU.add).then_inc(s_lam, 1)
            dve.wait_ge(s_lam, 2)
            ch(dve.tensor_tensor(nlam[:, :], lam_e[:, 1, :], lam_e[:, 0, :], ALU.subtract))
            ch.wait()
            for l in range(LAYERS):
                li = 0.8 - 0.6 * math.exp(-0.3 * l)
                ch(dve.tensor_scalar(nlam[:, l:l + 1], nlam[:, l:l + 1], -li, None, ALU.add))
            ch.wait()
            for c in range(KD):
                dve.wait_ge(s_xt, c + 1)
                dve.tensor_copy(x[:, c, META:TM], ps[:, c, :]).then_inc(b1.s.x_new, 1)
            dve.wait_ge(s_xt, KD + 1)
            ch(dve.tensor_copy(x[:, :, 0:META], ps[:, 1, 0:KD * META].rearrange("p (k t) -> p k t", k=KD)))
            ch.wait()
            dve.sem_inc(s_xc, 1)
            for i in range(1, 6):
                parameters(i)
            dve.wait_ge(s_pc, 6)
            for l in range(LAYERS):
                li = 0.8 - 0.6 * math.exp(-0.3 * l)
                c = PAR_SUBLN + l
                ch(dve.tensor_scalar(par[:, c:c + 1], par[:, c:c + 1], 1.0 - li, None, ALU.mult))
            dve.wait_ge(s_set, 11)
            dve.wait_ge(s_ld[5], 16)

        def act_setup(act):
            act_loads(act)
            for b in (b1, b2):
                act.sem_inc(b.s.out_free, CR)
                act.sem_inc(b.s.o_hi_out, 1)
                act.sem_inc(b.s.transposed_out, 1)
            act.wait_ge(s_rev, 2)
            act.dma_start(rev_dram, rev[:, :]).then_inc(s_revd, 16)
            act.wait_ge(s_revd, 16)
            b0 = rev_dram[0:1, P - 1:P]
            src = bass.AP(tensor=b0.tensor, offset=b0.offset, ap=[[640, 12], [-1, P], [1, SEQ]])
            act.dma_start(tbias_dram, src).then_inc(s_tbias, 16)
            act.wait_ge(s_set, 8)
            act.activation(dist[:, :], dist[:, :], ACT.Abs).then_inc(s_dist, 1)
            act.wait_ge(s_lam, 1)
            act.activation(lam_e[:, :, :], lam_s[:, :, :], ACT.Exp).then_inc(s_lam, 1)
            act.wait_ge(s_pc, 1)
            act.wait_ge(s_ones, 3)

        def pe_setup(pe):
            pe.sem_inc(b1.s.granules_done, CR)
            pe.wait_ge(s_const, 1)
            def parameters(i):
                n_ = PSIZE[i]
                pe.transpose(ps[:, 2 + i, 0:n_], prow[i][0:n_, :], ident[0:n_, 0:n_]).then_inc(s_pt, 1)

            pe.wait_ge(s_ld[0], 16 * 6)
            parameters(0)
            pe.wait_ge(s_ld[1], 16)
            for c in range(KD):
                if c == 2:
                    pe.wait_ge(s_pc, 1)
                for a in range(4):
                    ins = pe.transpose(ps[:, c, P * a:P * a + P], xin[:, a, P * c:P * c + P], ident[:, :])
                ins.then_inc(s_xt, 1)
            pe.wait_ge(s_ld[2], 16 * NLD_PAR)
            pe.wait_ge(b1.s.x_new, 8)
            for c in range(KD):
                ins = pe.transpose(ps[:, 1, META * c:META * c + META], metain[:, P * c:P * c + P],
                                   ident[0:META, 0:META])
            ins.then_inc(s_xt, 1)
            for i in range(1, 6):
                parameters(i)
            pe.wait_ge(s_ones, 3)
            pe.wait_ge(s_xc, 1)
            pe.wait_ge(s_set, 11)
            pe.wait_ge(s_ld[5], 16)

        block = ctx.enter_context(nc.Block())

        nx_m1 = (PAR_MIXPRE, mgb, mgb2)
        nx_f2 = (PAR_FF2PRE, f2.gb, f2.gb2)

        @block.sync
        def _(sp):
            sp_setup(sp)
            with sp.Fori(0, LAYERS) as l:
                sp_ffn(sp, b1, l, f1)
                sp_mix1(sp, l)
                sp_ffn(sp, b1, l, f2)
            with sp.Fori(0, LAYERS) as l:
                sp_mix2(sp, l)
                sp_ffn(sp, b2, l, fg)
            sp.wait_ge(s_oh, 1)
            for a in range(4):
                sp.wait_ge(s_oc, a + 1)
                sp.dma_start(out[0, P * a:P * a + P, :], xin[:, a, :]).then_inc(s_out, 16)
            sp.wait_ge(s_out, 64)

        @block.gpsimd
        def _(pool):
            pool_setup(pool)
            with pool.Fori(0, LAYERS) as l:
                pool_first(pool, b1, l, f1.gb)
                pool_x(pool, b1, l * 3)
                pool_y(pool, b1, l * 3)
                pool_first(pool, b1, l, mgb)
                pool_x(pool, b1, l * 3 + 1)
                pool_mix1(pool, l)
                pool_y(pool, b1, l * 3 + 1)
                pool_first(pool, b1, l, f2.gb)
                pool_x(pool, b1, l * 3 + 2)
                pool_y(pool, b1, l * 3 + 2)
            pool.wait_ge(b1.s.weights_split, LAYERS * b1.GL + CR)
            pool.sem_inc(b2.s.weights_split, CR)
            with pool.Fori(0, LAYERS) as l:
                pool_first(pool, b2, l, g2b)
                pool_x(pool, b2, l * 2)
                pool_mix2(pool, l)
                pool_y(pool, b2, l * 2)
                pool_first(pool, b2, l, fg.gb)
                pool_x(pool, b2, l * 2 + 1)
                pool_y(pool, b2, l * 2 + 1)

        @block.scalar
        def _(act):
            act_setup(act)
            with act.Fori(0, LAYERS) as l:
                act_next(act, b1, l, l * 3, PAR_FF1PRE, f1.gb, f1.gb2)
                act_ffn(act, b1, l, f1, nx_m1)
                act_mix1(act, l, nx_f2)
                act_ffn(act, b1, l, f2, None)
            with act.Fori(0, LAYERS) as l:
                act_next(act, b2, l, l * 2, PAR_MIXPRE2, g2b, g2b2)
                act_mix2(act, l, (PAR_FFPRE2, fg.gb, fg.gb2))
                act_ffn(act, b2, l, fg, None)
            act.wait_ge(s_ot, 1)
            act.wait_ge(b2.s.x_new, 8 * 2 * LAYERS + 8)
            for a in range(4):
                ins = act.activation(xin[:, a, 0:512], ps[:, a, :], ACT.Copy)
            ins.then_inc(s_oh, 1)

        @block.vector
        def _(dve):
            ch = Chain(dve, b1.s.dve_steps, 0)
            dve_setup(dve, ch)
            base = ch.n
            with dve.Fori(0, LAYERS) as l:
                ch.base, n0 = l * CHAIN1, ch.n
                dve_first(dve, b1, l, l * 3, PAR_FF1PRE)
                dve_ffn(dve, b1, l, f1, ch, 0.5, PAR_FF1POST, PAR_MIXPRE)
                dve_mix1(dve, l, ch, PAR_FF2PRE)
                dve_ffn(dve, b1, l, f2, ch, 0.5, PAR_FF2POST, None)
                if ch.n - n0 != CHAIN1:
                    raise ValueError(f"CHAIN1 is {ch.n - n0}")
            chain1_end = base + LAYERS * CHAIN1
            ch.base, ch.n = 0, chain1_end
            with dve.Fori(0, LAYERS) as l:
                ch.base, n0 = l * CHAIN2, ch.n
                dve_first(dve, b2, l, l * 2, PAR_MIXPRE2)
                dve_mix2(dve, l, ch, PAR_FFPRE2)
                dve_ffn(dve, b2, l, fg, ch, 1.0, PAR_FFPOST2, None)
                if ch.n - n0 != CHAIN2:
                    raise ValueError(f"CHAIN2 is {ch.n - n0}")
            ch.base, ch.n = 0, chain1_end + LAYERS * CHAIN2
            dve.wait_ge(s_ot, 2)
            for a in range(4):
                dve.tensor_copy(xin[:, a, 512:1024], ps[:, 4 + a, :]).then_inc(s_oc, 1)

        @block.tensor
        def _(pe):
            pe_setup(pe)
            with pe.Fori(0, LAYERS) as l:
                pe_ffn(pe, b1, l, f1)
                pe_mix1(pe, l)
                pe_ffn(pe, b1, l, f2)
            pe.wait_ge(b1.s.granules_done, LAYERS * b1.GL + CR)
            pe.sem_inc(b2.s.granules_done, CR)
            for c in range(KD):
                pe.wait_ge(b1.s.x_new, 8 * 3 * LAYERS + c + 1)
                pe.sem_inc(b2.s.x_new, 1)
            with pe.Fori(0, LAYERS) as l:
                pe_mix2(pe, l)
                pe_ffn(pe, b2, l, fg)
            for h in range(2):
                for c in range(4):
                    pe.wait_ge(b2.s.x_new, 8 * 2 * LAYERS + 8 if h else 8 * 2 * LAYERS + c + 1)
                    for a in range(4):
                        t0 = META + P * a
                        ins = pe.transpose(ps[:, 4 * h + a, P * c:P * c + P], x[:, 4 * h + c, t0:t0 + P], ident[:, :])
                ins.then_inc(s_ot, 1)



CHAIN1 = 286
CHAIN2 = 180

_INS = ["x", "ffn1_pre_g", "ffn1_w_gate", "ffn1_w_up", "ffn1_w_down", "ffn1_post_g", "mix_pre_g", "w_in", "rel_bias",
        "diff_lambda_q1", "diff_lambda_k1", "diff_lambda_q2", "diff_lambda_k2", "diff_subln_g", "w_out",
        "mix_post_g", "ffn2_pre_g", "ffn2_w_gate", "ffn2_w_up", "ffn2_w_down", "ffn2_post_g", "meta_tokens_2",
        "mix_pre_g_2", "mix_post_g_2", "w_in_2", "b_forget_2", "a_dw_w_2", "a_dw_b_2", "a_ln_g_2", "a_ln_b_2",
        "a_pw_w_2", "sc_conv_w_2", "head_g_2", "w_out_2", "ffn_pre_g_2", "ffn_post_g_2", "ffn_w_up_2",
        "ffn_conv_w_2", "ffn_w_down_2"]


def kernel(**inputs):
    import numpy as np
    import concourse.bacc as bacc
    from concourse.bass_utils import run_bass_kernel_spmd

    nc = bacc.Bacc("TRN2", target_bir_lowering=False, num_devices=1)
    arrays, tensors = {}, {}
    for name in _INS:
        a = np.ascontiguousarray(inputs[name])
        arrays[f"in_{name}_dram"] = a
        tensors[name] = nc.dram_tensor(f"in_{name}_dram", a.shape, mybir.dt.from_np(a.dtype),
                                       kind="ExternalInput").ap()
    out = nc.dram_tensor("out_0_dram", (1, SEQ, D), F32, kind="ExternalOutput").ap()
    program(nc, tensors, out)
    r = run_bass_kernel_spmd(nc, [arrays], core_ids=[0])
    return r.results[0]["out_0_dram"]
```
